# Optimizing a Trainium2 kernel written in Bass

```python
import numpy as np
import jax
import jax.numpy as jnp
from jax import lax

D_MODEL = 1024
BATCH = 1
SEQ = 1024
DEPTH = 1

D_FF = 4 * D_MODEL
EPS = 1e-6
Q_BLOCK = 128
N_BRANCH = 3
MASK_NEG = -1e30

GDN_HEADS = 4
GDN_DK = 128
GDN_DV = 128
GDN_CONV = 4
GDN_CHUNK = 64
GDN_QK_W = GDN_HEADS * GDN_DK
GDN_V_W = GDN_HEADS * GDN_DV

NSA_HEADS = 8
NSA_KV_HEADS = 2
NSA_DH = 64
NSA_GROUP = NSA_HEADS // NSA_KV_HEADS
NSA_W = NSA_HEADS * NSA_DH
NSA_KV_W = NSA_KV_HEADS * NSA_DH
CMP_LEN = 32
CMP_STRIDE = 16
SEL_LEN = 64
SEL_TOPK = 8
WINDOW = 512
FORCE_BONUS = 1e3

SB_HEADS = 8
SB_DH = 64
SB_W = SB_HEADS * SB_DH

IN_SPLITS = (GDN_QK_W, GDN_QK_W, GDN_V_W, GDN_V_W, GDN_HEADS, GDN_HEADS,
             NSA_W, 6 * NSA_KV_W, 3 * NSA_HEADS,
             SB_W, SB_W, SB_W,
             N_BRANCH * D_MODEL)
N_IN = sum(IN_SPLITS)

kernel_name = 'hybrid_gdn_nsa_stickbreak_block'

def rms_norm(x, g):
    xf = x.astype(jnp.float32)
    y = xf * lax.rsqrt(jnp.mean(xf * xf, axis=-1, keepdims=True) + EPS)
    return (y * g.astype(jnp.float32)).astype(x.dtype)

def l2_norm(x):
    xf = x.astype(jnp.float32)
    return xf * lax.rsqrt(jnp.sum(xf * xf, axis=-1, keepdims=True) + EPS)

def causal_depthwise_conv(x, w):
    c = x.shape[-1]
    k = w.shape[0]
    return lax.conv_general_dilated(x, w[:, None, :].astype(x.dtype), window_strides=(1,),
                                    padding=[(k - 1, 0)], dimension_numbers=('NWC', 'WIO', 'NWC'),
                                    feature_group_count=c)

def chunk_gated_delta_rule(q, k, v, g, beta):
    b, h, s, dk = q.shape
    dv = v.shape[-1]
    c = GDN_CHUNK
    n = s // c
    q = q.reshape(b, h, n, c, dk)
    k = k.reshape(b, h, n, c, dk)
    v = v.reshape(b, h, n, c, dv)
    g = jnp.cumsum(g.reshape(b, h, n, c), axis=-1)
    beta = beta.reshape(b, h, n, c)
    incl = jnp.tril(jnp.ones((c, c), dtype=bool))
    strict = jnp.tril(jnp.ones((c, c), dtype=bool), -1)
    diff = g[..., :, None] - g[..., None, :]
    decay = jnp.where(incl, jnp.exp(jnp.where(incl, diff, 0.0)), 0.0)
    k_beta = k * beta[..., None]
    a_strict = jnp.where(strict, jnp.einsum('bhnid,bhnjd->bhnij', k_beta, k) * decay, 0.0)
    eye = jnp.eye(c, dtype=q.dtype)
    t_inv = lax.linalg.triangular_solve(a_strict + eye, jnp.broadcast_to(eye, a_strict.shape),
                                        left_side=True, lower=True)
    u = jnp.einsum('bhnij,bhnjd->bhnid', t_inv, v * beta[..., None])
    w = jnp.einsum('bhnij,bhnjd->bhnid', t_inv, k_beta * jnp.exp(g)[..., None])
    attn = jnp.einsum('bhnid,bhnjd->bhnij', q, k) * decay
    g_last = g[..., -1]
    k_dec = k * jnp.exp(g_last[..., None] - g)[..., None]

    def step(state, xs):
        q_c, kd_c, u_c, w_c, g_c, attn_c, gl_c = xs
        v_new = u_c - jnp.einsum('bhck,bhkv->bhcv', w_c, state)
        o = (jnp.einsum('bhck,bhkv->bhcv', q_c * jnp.exp(g_c)[..., None], state)
             + jnp.einsum('bhij,bhjv->bhiv', attn_c, v_new))
        state = state * jnp.exp(gl_c)[..., None, None] + jnp.einsum('bhck,bhcv->bhkv', kd_c, v_new)
        return state, o

    xs = tuple(jnp.moveaxis(t, 2, 0) for t in (q, k_dec, u, w, g, attn, g_last))
    state0 = jnp.zeros((b, h, dk, dv), q.dtype)
    _, o = lax.scan(step, state0, xs)
    return jnp.moveaxis(o, 0, 2).reshape(b, h, s, dv)

def gated_deltanet(q, k, v, z, a, bt, conv_w, a_log, dt_bias, norm_g):
    b, s, _ = q.shape
    dt = q.dtype
    f32 = jnp.float32
    qkv = jax.nn.silu(causal_depthwise_conv(jnp.concatenate([q, k, v], axis=-1), conv_w))
    q, k, v = jnp.split(qkv, [GDN_QK_W, 2 * GDN_QK_W], axis=-1)

    def heads(t, d):
        return t.reshape(b, s, GDN_HEADS, d).transpose(0, 2, 1, 3)

    qh = l2_norm(heads(q, GDN_DK)) * (GDN_DK ** -0.5)
    kh = l2_norm(heads(k, GDN_DK))
    vh = heads(v, GDN_DV).astype(f32)
    beta = jax.nn.sigmoid(bt.astype(f32)).transpose(0, 2, 1)
    g = -(jnp.exp(a_log.astype(f32))[:, None]
          * jax.nn.softplus(a.astype(f32) + dt_bias.astype(f32)).transpose(0, 2, 1))
    o = chunk_gated_delta_rule(qh, kh, vh, g, beta).transpose(0, 2, 1, 3)
    o = rms_norm(o, norm_g) * jax.nn.silu(z.astype(f32).reshape(b, s, GDN_HEADS, GDN_DV))
    return o.reshape(b, s, GDN_V_W).astype(dt)

def native_sparse_attention(q, kv, gate_logits, cmp_wk, cmp_pk, cmp_wv, cmp_pv):
    b, s, _ = q.shape
    dt = q.dtype
    f32 = jnp.float32
    g_, hg, dh = NSA_KV_HEADS, NSA_GROUP, NSA_DH
    qh = (q * (dh ** -0.5)).reshape(b, s, g_, hg, dh)
    k_cmp, v_cmp, k_slc, v_slc, k_win, v_win = [t.reshape(b, s, g_, dh) for t in jnp.split(kv, 6, axis=-1)]
    pos = jnp.arange(s)

    n_cmp = (s - CMP_LEN) // CMP_STRIDE + 1
    blk_start = jnp.arange(n_cmp) * CMP_STRIDE
    gidx = blk_start[:, None] + jnp.arange(CMP_LEN)[None, :]
    kc = jnp.einsum('bnlgd,lde->bnge', k_cmp[:, gidx] + cmp_pk[:, None, :], cmp_wk)
    vc = jnp.einsum('bnlgd,lde->bnge', v_cmp[:, gidx] + cmp_pv[:, None, :], cmp_wv)
    s_cmp = jnp.einsum('bsghd,bngd->bghsn', qh, kc).astype(f32)
    cmp_valid = (blk_start + CMP_LEN - 1)[None, :] <= pos[:, None]
    p_cmp = jax.nn.softmax(jnp.where(cmp_valid, s_cmp, MASK_NEG), axis=-1) * cmp_valid
    o_cmp = jnp.einsum('bghsn,bngd->bsghd', p_cmp.astype(dt), vc)

    n_sel = s // SEL_LEN
    top_k = min(SEL_TOPK, n_sel)
    sel_start_np = np.arange(n_sel) * SEL_LEN
    cmp_start_np = np.arange(n_cmp) * CMP_STRIDE
    overlap = ((cmp_start_np[None, :] < sel_start_np[:, None] + SEL_LEN)
               & (cmp_start_np[None, :] + CMP_LEN > sel_start_np[:, None])).astype(np.float32)
    imp = jnp.einsum('bghsn,jn->bgsj', p_cmp, jnp.asarray(overlap))
    blk = jnp.arange(n_sel)[None, :]
    cur = (pos // SEL_LEN)[:, None]
    sel_valid = blk <= cur
    forced = (blk == 0) | (blk == cur) | (blk == cur - 1)
    score = jnp.where(sel_valid, imp + FORCE_BONUS * forced, MASK_NEG)
    _, sel_idx = lax.top_k(score, top_k)

    ks = k_slc.reshape(b, n_sel, SEL_LEN, g_, dh).transpose(0, 3, 1, 2, 4)
    vs = v_slc.reshape(b, n_sel, SEL_LEN, g_, dh).transpose(0, 3, 1, 2, 4)
    kw = jnp.pad(k_win, ((0, 0), (WINDOW, 0), (0, 0), (0, 0)))
    vw = jnp.pad(v_win, ((0, 0), (WINDOW, 0), (0, 0), (0, 0)))
    b_ix = jnp.arange(b)[:, None, None, None]
    g_ix = jnp.arange(g_)[None, :, None, None]

    def query_block(qb):
        q0 = qb * Q_BLOCK
        qt = lax.dynamic_slice_in_dim(qh, q0, Q_BLOCK, axis=1)
        tq = q0 + jnp.arange(Q_BLOCK)
        idx = lax.dynamic_slice_in_dim(sel_idx, q0, Q_BLOCK, axis=2)
        kg = ks[b_ix, g_ix, idx]
        vg = vs[b_ix, g_ix, idx]
        kpos = idx[..., None] * SEL_LEN + jnp.arange(SEL_LEN)
        smask = kpos <= tq[None, None, :, None, None]
        ss = jnp.einsum('bqghd,bgqkld->bghqkl', qt, kg).astype(f32)
        ss = jnp.where(smask[:, :, None], ss, MASK_NEG)
        ps = jax.nn.softmax(ss.reshape(b, g_, hg, Q_BLOCK, -1), axis=-1).reshape(ss.shape).astype(dt)
        o_s = jnp.einsum('bghqkl,bgqkld->bqghd', ps, vg)
        kwt = lax.dynamic_slice_in_dim(kw, q0, WINDOW + Q_BLOCK, axis=1)
        vwt = lax.dynamic_slice_in_dim(vw, q0, WINDOW + Q_BLOCK, axis=1)
        spos = q0 - WINDOW + jnp.arange(WINDOW + Q_BLOCK)
        dist = tq[:, None] - spos[None, :]
        wmask = (dist >= 0) & (dist < WINDOW) & (spos[None, :] >= 0)
        sw = jnp.einsum('bqghd,bsgd->bghqs', qt, kwt).astype(f32)
        pw = jax.nn.softmax(jnp.where(wmask, sw, MASK_NEG), axis=-1).astype(dt)
        o_w = jnp.einsum('bghqs,bsgd->bqghd', pw, vwt)
        return o_s, o_w

    o_slc, o_win = lax.map(query_block, jnp.arange(s // Q_BLOCK))
    o_slc = jnp.moveaxis(o_slc, 0, 1).reshape(b, s, g_, hg, dh)
    o_win = jnp.moveaxis(o_win, 0, 1).reshape(b, s, g_, hg, dh)
    gates = jax.nn.sigmoid(gate_logits.astype(f32)).reshape(b, s, g_, hg, 3).astype(dt)
    o = gates[..., 0:1] * o_cmp + gates[..., 1:2] * o_slc + gates[..., 2:3] * o_win
    return o.reshape(b, s, NSA_W)

def stick_breaking_attention(q, k, v):
    b, s, _ = q.shape
    f32 = jnp.float32
    qh = (q * (SB_DH ** -0.5)).reshape(b, s, SB_HEADS, SB_DH)
    kh = k.reshape(b, s, SB_HEADS, SB_DH)
    vh = v.reshape(b, s, SB_HEADS, SB_DH)
    spos = jnp.arange(s)

    def query_block(qb):
        q0 = qb * Q_BLOCK
        qt = lax.dynamic_slice_in_dim(qh, q0, Q_BLOCK, axis=1)
        tq = q0 + jnp.arange(Q_BLOCK)
        z = jnp.einsum('bqhd,bshd->bhqs', qt, kh).astype(f32)
        causal = spos[None, :] < tq[:, None]
        cum = jnp.cumsum(jnp.where(causal, jax.nn.log_sigmoid(-z), 0.0), axis=-1)
        log_a = jax.nn.log_sigmoid(z) + cum[..., -1:] - cum
        a = jnp.where(causal, jnp.exp(log_a), 0.0).astype(v.dtype)
        return jnp.einsum('bhqs,bshd->bqhd', a, vh)

    o = lax.map(query_block, jnp.arange(s // Q_BLOCK))
    return jnp.moveaxis(o, 0, 1).reshape(b, s, SB_W)

def hybrid_mixer(h, w_in, gdn_conv_w, gdn_a_log, gdn_dt_bias, gdn_norm_g,
                 nsa_cmp_wk, nsa_cmp_pk, nsa_cmp_wv, nsa_cmp_pv,
                 w_br_gdn, w_br_nsa, w_br_sb, w_out):
    b, s, _ = h.shape
    split_points = [int(p) for p in np.cumsum(IN_SPLITS)[:-1]]
    (gq, gk, gv, gz, ga, gb, nq, nkv, ngate, sq, sk, sv, merge_logits) = jnp.split(h @ w_in, split_points, axis=-1)
    y_a = gated_deltanet(gq, gk, gv, gz, ga, gb, gdn_conv_w, gdn_a_log, gdn_dt_bias, gdn_norm_g)
    y_b = native_sparse_attention(nq, nkv, ngate, nsa_cmp_wk, nsa_cmp_pk, nsa_cmp_wv, nsa_cmp_pv)
    y_c = stick_breaking_attention(sq, sk, sv)
    gate = jax.nn.sigmoid(merge_logits.astype(jnp.float32)).astype(h.dtype).reshape(b, s, N_BRANCH, D_MODEL)
    merged = (gate[:, :, 0] * (y_a @ w_br_gdn) + gate[:, :, 1] * (y_b @ w_br_nsa)
              + gate[:, :, 2] * (y_c @ w_br_sb))
    return merged @ w_out

def squared_relu_mlp(h, w1, w2):
    return jnp.square(jax.nn.relu(h @ w1)) @ w2

def setup_inputs(seed: int = 0) -> dict:
    key = jax.random.key(seed)
    k = jax.random.split(key, 24)
    f32 = jnp.float32

    def dense(kk, shape, fan_in):
        return jax.random.normal(kk, shape, f32) * (fan_in ** -0.5)

    def gain(kk, n):
        return 1.0 + 0.02 * jax.random.normal(kk, (DEPTH, n), f32)

    dt = jnp.exp(jax.random.uniform(k[7], (DEPTH, GDN_HEADS), f32, -6.9077553, -2.3025851))
    return {
        'x': jax.random.normal(k[0], (BATCH, SEQ, D_MODEL), f32),
        'g_mix_pre': gain(k[1], D_MODEL),
        'g_mix_post': gain(k[2], D_MODEL),
        'g_ff_pre': gain(k[3], D_MODEL),
        'g_ff_post': gain(k[4], D_MODEL),
        'w_in': dense(k[5], (DEPTH, D_MODEL, N_IN), D_MODEL),
        'gdn_conv_w': dense(k[6], (DEPTH, GDN_CONV, 2 * GDN_QK_W + GDN_V_W), GDN_CONV),
        'gdn_a_log': jnp.log(jax.random.uniform(k[8], (DEPTH, GDN_HEADS), f32, 1.0, 16.0)),
        'gdn_dt_bias': dt + jnp.log(-jnp.expm1(-dt)),
        'gdn_norm_g': gain(k[9], GDN_DV),
        'nsa_cmp_wk': dense(k[10], (DEPTH, CMP_LEN, NSA_DH, NSA_DH), CMP_LEN * NSA_DH),
        'nsa_cmp_pk': 0.1 * jax.random.normal(k[11], (DEPTH, CMP_LEN, NSA_DH), f32),
        'nsa_cmp_wv': dense(k[12], (DEPTH, CMP_LEN, NSA_DH, NSA_DH), CMP_LEN * NSA_DH),
        'nsa_cmp_pv': 0.1 * jax.random.normal(k[13], (DEPTH, CMP_LEN, NSA_DH), f32),
        'w_br_gdn': dense(k[14], (DEPTH, GDN_V_W, D_MODEL), GDN_V_W),
        'w_br_nsa': dense(k[15], (DEPTH, NSA_W, D_MODEL), NSA_W),
        'w_br_sb': dense(k[16], (DEPTH, SB_W, D_MODEL), SB_W),
        'w_out': dense(k[17], (DEPTH, D_MODEL, D_MODEL), D_MODEL),
        'w_ff1': dense(k[18], (DEPTH, D_MODEL, D_FF), D_MODEL),
        'w_ff2': dense(k[19], (DEPTH, D_FF, D_MODEL), D_FF),
    }

def reference(x, g_mix_pre, g_mix_post, g_ff_pre, g_ff_post, w_in, gdn_conv_w, gdn_a_log,
              gdn_dt_bias, gdn_norm_g, nsa_cmp_wk, nsa_cmp_pk, nsa_cmp_wv, nsa_cmp_pv,
              w_br_gdn, w_br_nsa, w_br_sb, w_out, w_ff1, w_ff2):
    for l in range(DEPTH):
        h = rms_norm(x, g_mix_pre[l])
        y = hybrid_mixer(h, w_in[l], gdn_conv_w[l], gdn_a_log[l], gdn_dt_bias[l], gdn_norm_g[l],
                         nsa_cmp_wk[l], nsa_cmp_pk[l], nsa_cmp_wv[l], nsa_cmp_pv[l],
                         w_br_gdn[l], w_br_nsa[l], w_br_sb[l], w_out[l])
        x = x + rms_norm(y, g_mix_post[l])
        h = rms_norm(x, g_ff_pre[l])
        x = x + rms_norm(squared_relu_mlp(h, w_ff1[l], w_ff2[l]), g_ff_post[l])
    return x


_drawn_inputs = setup_inputs


def setup_inputs(seed=0):
    import zlib

    import numpy as np

    out = dict(_drawn_inputs(seed))
    spreads = {}
    factors = {'g_mix_post': 3.726,
     'g_ff_pre': 14.847,
     'g_ff_post': 18.345,
     'gdn_norm_g': 5.174,
     'nsa_cmp_pk': 64.0,
     'nsa_cmp_pv': 3.249}
    for name, (base, spread) in spreads.items():
        noise = np.random.default_rng([zlib.crc32(name.encode()), seed]).standard_normal(out[name].shape)
        drawn = base * np.exp(spread * noise) if base else spread * noise
        out[name] = jnp.asarray(drawn.astype(out[name].dtype))
    for name, factor in factors.items():
        out[name] = (out[name] * factor).astype(out[name].dtype)
    return out
```

```python
from contextlib import ExitStack

import numpy as np

import concourse.bass as bass
from concourse import mybir

F32 = mybir.dt.float32
F32R = mybir.dt.float32r
ALU = mybir.AluOpType
ACT = mybir.ActivationFunctionType
AX_X = mybir.AxisListType.X

P = 128
D = 1024
T = 1024
KT = D // P
TB = T // P
FF = 4 * D
SB0 = 16544
EPS = 1e-6
NEG = -1e30
PIECE = KT * P

GH, GD, GC = 4, 128, 64
NH, NG, ND = 8, 2, 64
NM = NH // NG
CL, CS = 32, 16
NCMP = (T - CL) // CS + 1
SL, TOPK = 64, 8
NSEL = T // SL
WIN = 512
WT = WIN // P + 1
SH, SD = 8, 64

SPLITS = [512, 512, 512, 512, 4, 4, 512, 768, 24, 512, 512, 512, 3072]
OFF = [sum(SPLITS[:i]) for i in range(len(SPLITS))]
(O_GQ, O_GK, O_GV, O_GZ, O_GA, O_GB, O_NQ, O_NKV, O_NGATE, O_SQ, O_SK, O_SV, O_MERGE) = OFF
N_IN = sum(SPLITS)


def shape_constants():
    i = np.arange(P)
    row, col = i[:, None], i[None, :]
    chunk = (row // GC) == (col // GC)
    f = lambda m: m.astype(np.float32)
    neg = lambda m: np.where(m, 0.0, NEG).astype(np.float32)
    gdn = [f(chunk & (row <= col)), neg(chunk & (row <= col)), f(chunk & (row < col))]
    for level in range(6):
        b = 1 << level
        gdn.append(f((row // b % 2 == 0) & (col // b == row // b + 1)))
    gdn += [f(chunk), np.ones((P, P), np.float32), f(row // GC == 0) * np.ones((1, P), np.float32),
            f(row // GC == 1) * np.ones((1, P), np.float32)]
    j = np.arange(NSEL)
    lower = f(j[None, :] < j[:, None]).reshape(1, -1) * np.ones((P, 1), np.float32)
    pos = np.arange(T).reshape(TB, P)
    start = np.arange(64) * CS
    valid = (start + CL - 1)[None, None, :] <= pos[:, :, None]
    valid = valid & (np.arange(64) < NCMP)
    valid = valid.transpose(1, 0, 2)
    cur = (pos // SL)[:, :, None]
    forced = (j == 0) | (j == cur) | (j == cur - 1)
    bias = np.where(j <= cur, 1e3 * forced, NEG).astype(np.float32).transpose(1, 0, 2)
    nsa = [neg(col <= row), neg(col > row), lower, neg(valid).reshape(P, -1), f(valid).reshape(P, -1),
           bias.reshape(P, -1)]
    sb = [f(col < row), neg(col < row)]
    cat = lambda x: np.ascontiguousarray(np.concatenate(x, 1))
    return np.eye(P, dtype=np.float32), cat(gdn), cat(nsa), cat(sb)


class Steps:

    def __init__(self, sem, names, base=0):
        self.sem, self.names, self.base = sem, names, base

    def done(self, i, name):
        return self.base + i * len(self.names) + self.names.index(name) + 1

    def wait(self, eng, i, name):
        eng.wait_ge(self.sem, self.done(i, name))


def build(nc, A, out):
    ctx = ExitStack()
    with ctx:
        def at(name, kb, shape, dt=F32):
            return nc.alloc_sbuf_tensor_at(name, [P] + list(shape), dt, offset=SB0 + int(kb * 1024))

        def sem(name):
            return ctx.enter_context(nc.semaphore(name))

        hT_hi = at("hT_hi", 0, [KT, T], F32R)
        hT_lo = at("hT_lo", 32, [KT, T], F32R)
        w_raw = [at(f"w_raw{i}", 64 + 4 * i, [KT, P]) for i in range(2)]
        w_hi = [at(f"w_hi{i}", 72 + 4 * i, [KT, P], F32R) for i in range(2)]
        w_lo = [at(f"w_lo{i}", 80 + 4 * i, [KT, P], F32R) for i in range(2)]
        mT = at("mT", 88, [KT, T])
        yT = at("yT", 120, [4, T])
        small = at("small", 194, [1152])
        ident = at("ident", 198.5, [P])
        consts = at("consts", 199, [1664])
        PS = ctx.enter_context(nc.psum_tensor("PS", [P, 8, 512], F32))

        def pair(k):
            return PS[:, 2 * k:2 * k + 2, :].rearrange("p a b -> p (a b)")

        w_loaded = [sem("w_loaded0"), sem("w_loaded1")]
        w_high = sem("w_high")
        w_split = sem("w_split")
        tile_done = sem("tile_done")
        tile_evac = [sem("tile_evac0"), sem("tile_evac1")]
        phase = sem("phase")
        consts_in = sem("consts_in")
        dve_step, act_step, pool_step = sem("dve_step"), sem("act_step"), sem("pool_step")

        counts = {"dve": 0, "act": 0, "phase": {}}

        def dstep(ins):
            counts["dve"] += 1
            ins.then_inc(dve_step, 1)
            nc.vector.wait_ge(dve_step, counts["dve"])

        def astep(ins):
            counts["act"] += 1
            ins.then_inc(act_step, 1)
            nc.scalar.wait_ge(act_step, counts["act"])

        def end_phase(eng, name):
            n = counts["phase"].get(name, 0) + 1
            counts["phase"][name] = n
            eng.drain().then_inc(phase, 1)
            eng.wait_ge(phase, 5 * n)

        w_in = A["w_in"][0].rearrange("(k p) n -> p k n", p=P)

        pieces = []
        def cols(o, n=P):
            return lambda dst, eng: eng.dma_start(dst[:, :, 0:n], w_in[:, :, o:o + n])
        for c in range(12):
            pieces.append((cols(O_GQ + c * P), KT))
        def gates_piece(dst, eng):
            eng.dma_start(dst[:, :, 0:2 * GH], w_in[:, :, O_GA:O_GA + 2 * GH]).then_inc(w_loaded[P_SMALL % 2], 16)
            return eng.dma_start(dst[:, :, 8:8 + 3 * NH], w_in[:, :, O_NGATE:O_NGATE + 3 * NH])
        P_SMALL = len(pieces)
        pieces.append((gates_piece, KT))
        P_GZ = len(pieces)
        for c in range(4):
            pieces.append((cols(O_GZ + c * P), KT))
        P_MERGE = [len(pieces)]
        def merge_pieces(b, name, rows=None):
            wb = A[name][0]
            for c in range(KT):
                pieces.append((cols(O_MERGE + b * D + c * P), KT))
                if rows is None:
                    v = wb.rearrange("(k p) n -> p k n", p=P)
                    pieces.append(((lambda v, c: lambda dst, eng: eng.dma_start(dst[:, 0:4, :], v[:, :, c * P:(c + 1) * P]))(v, c), 4))
                else:
                    def two(c):
                        par = len(pieces) % 2

                        def go(dst, eng):
                            v = wb.rearrange("(g m d) n -> g d m n", g=NG, m=NM)
                            eng.dma_start(dst[0:ND, 0:4, :], v[0, :, :, c * P:(c + 1) * P]).then_inc(w_loaded[par], 16)
                            return eng.dma_start(dst[ND:P, 0:4, :], v[1, :, :, c * P:(c + 1) * P])
                        return go
                    pieces.append((two(c), 4))
        merge_pieces(0, "w_br_gdn")
        P_NSA = len(pieces)
        nq_v = A["w_in"][0][:, O_NQ:O_NQ + 512].rearrange("(k p) (g m d) -> g m p k d", p=P, g=NG, m=NM)
        for c in range(6):
            pieces.append((cols(O_NKV + c * P), KT))
        def nq_piece(m):
            par = len(pieces) % 2

            def go(dst, eng):
                eng.dma_start(dst[:, :, 0:ND], nq_v[0, m]).then_inc(w_loaded[par], 16)
                return eng.dma_start(dst[:, :, ND:P], nq_v[1, m])
            return go
        for m in range(NM):
            pieces.append((nq_piece(m), KT))
        P_MERGE.append(len(pieces))
        merge_pieces(1, "w_br_nsa", rows=True)
        P_SB = len(pieces)
        for m in range(4):
            for o in (O_SQ, O_SK, O_SV):
                pieces.append((cols(o + m * P), KT))
        P_MERGE.append(len(pieces))
        merge_pieces(2, "w_br_sb")
        P_OUT = len(pieces)
        wo_v = A["w_out"][0].rearrange("(k p) n -> p k n", p=P)
        for c in range(KT):
            pieces.append(((lambda c: lambda dst, eng: eng.dma_start(dst[:], wo_v[:, :, c * P:(c + 1) * P]))(c), KT))
        P_MLP = len(pieces)
        two_dma = {P_SMALL} | {P_NSA + 6 + m for m in range(NM)} | {P_MERGE[1] + 2 * c + 1 for c in range(KT)}
        loaded_at = []
        loaded = [0, 0]
        for p in range(P_MLP):
            loaded[p % 2] += 32 if p in two_dma else 16
            loaded_at.append(loaded[p % 2])
        CH = FF // D
        w1_v = A["w_ff1"][0].rearrange("(k p) (f n) -> f p k n", p=P, n=P)
        w2_v = A["w_ff2"][0].rearrange("(i k p) (c n) -> i c p k n", k=KT, p=P, n=P)

        def load_pieces(sp, lo, hi):
            for p in range(lo, hi):
                if p >= 2:
                    sp.wait_ge(w_split, p - 1)
                pieces[p][0](w_raw[p % 2], sp).then_inc(w_loaded[p % 2], 16)

        def split_pieces(pool, lo, hi):
            for p in range(lo, hi):
                b, k = p % 2, pieces[p][1]
                pool.wait_ge(w_loaded[b], loaded_at[p])
                if p >= 2:
                    pool.wait_ge(tile_done, p - 1)
                nc.gpsimd.tensor_copy(w_hi[b][:, 0:k], w_raw[b][:, 0:k]).then_inc(w_high, 1)
                pool.wait_ge(w_high, p + 1)
                nc.gpsimd.tensor_tensor(w_lo[b][:, 0:k], w_raw[b][:, 0:k], w_hi[b][:, 0:k].bitcast(F32),
                                        ALU.subtract).then_inc(w_split, 1)

        def job(pe, p, rhs_hi, rhs_lo, ktiles=KT, par=None, waits=None):
            b = p % 2 if par is None else par
            dst = 2 * b
            last = None
            for k in range(ktiles):
                for w, r, first, end in ((w_hi, rhs_hi, True, False), (w_hi, rhs_lo, False, False),
                                         (w_lo, rhs_hi, False, True)):
                    for h in range(2):
                        last = nc.tensor.matmul(PS[:, dst + h, :], w[b][:, k, :], r[:, k, h * 512:(h + 1) * 512],
                                                start=(k == 0 and first), stop=(k == ktiles - 1 and end))
            last.then_inc(tile_done, 1)

        def run_job(pe, p, rhs_hi=None, rhs_lo=None):
            pe.wait_ge(w_split, p + 1)
            if p >= 2:
                pe.wait_ge(tile_evac[p % 2], p // 2)
            job(pe, p, hT_hi if rhs_hi is None else rhs_hi, hT_lo if rhs_lo is None else rhs_lo, pieces[p][1])

        def evac_done(ins, p):
            ins.then_inc(tile_evac[p % 2], 1)

        xin = [at(f"xin{i}", 136 + 4 * i, [D]) for i in range(2)]
        xs = [at(f"xs{i}", 144 + 4 * i, [D]) for i in range(2)]
        g_pre = at("g_pre", 152, [D])
        junk0 = at("junk0", 156, [D])
        ss0 = small[:, 0:TB]
        rt0 = small[:, TB:2 * TB]
        rr0 = small[:, 2 * TB:3 * TB]
        eps_t = small[:, 1151:1152]
        x_v = A["x"][0].rearrange("(t p) d -> t p d", p=P)
        x_in = [sem("x_in0"), sem("x_in1")]
        x_ss, x_norm, x_tr, x_hi, x_lo, eps_set = (sem(n) for n in (
            "x_ss", "x_norm", "x_tr", "x_hi", "x_lo", "eps_set"))

        def bc(ap, n):
            return ap.rearrange("(a n) -> a n", a=1).to_broadcast([P, n])

        def sp_phase0(sp):
            sp.dma_start(ident[:], A["c_ident"]).then_inc(consts_in, 16)
            sp.dma_start(g_pre[:], bc(A["g_mix_pre"][0], D)).then_inc(consts_in, 16)
            for t in range(TB):
                if t >= 2:
                    sp.wait_ge(x_norm, t - 1)
                sp.dma_start(xin[t % 2][:], x_v[t]).then_inc(x_in[t % 2], 16)

        def act_phase0(act):
            act.wait_ge(eps_set, 1)
            for t in range(TB):
                act.wait_ge(x_in[t % 2], 16 * (t // 2 + 1))
                astep(nc.scalar.activation(junk0[:], xin[t % 2][:], ACT.Square, accum_out=ss0[:, t:t + 1]))
                nc.scalar.activation(rt0[:, t:t + 1], ss0[:, t:t + 1], ACT.Sqrt, scale=1.0 / D,
                                     bias=eps_t).then_inc(x_ss, 1)
                if t >= 1:
                    act_split_x(act, t - 1)
            act_split_x(act, TB - 1)

        def act_split_x(act, t):
            act.wait_ge(x_tr, t + 1)
            nc.scalar.activation(hT_hi[:, :, t * P:(t + 1) * P],
                                 pair(t % 2).rearrange("p (k n) -> p k n", n=P), ACT.Copy).then_inc(x_hi, 1)

        def dve_phase0(dve):
            nc.vector.memset(eps_t, EPS).then_inc(eps_set, 1)
            nc.vector.memset(small[:, 1150:1151], 0.0)
            dve.wait_ge(consts_in, 32)
            for t in range(TB + 1):
                if t < TB:
                    dve.wait_ge(x_ss, t + 1)
                    dstep(nc.vector.reciprocal(rr0[:, t:t + 1], rt0[:, t:t + 1]))
                    if t >= 2:
                        dve.wait_ge(x_tr, t - 1)
                    nc.vector.scalar_tensor_tensor(out=xs[t % 2][:], in0=xin[t % 2][:], scalar=rr0[:, t:t + 1],
                                                   in1=g_pre[:], op0=ALU.mult, op1=ALU.mult).then_inc(x_norm, 1)
                if t >= 1:
                    dve_split_x(dve, t - 1)

        def dve_split_x(dve, t):
            dve.wait_ge(x_hi, t + 1)
            s = slice(t * P, (t + 1) * P)
            nc.vector.tensor_tensor(hT_lo[:, :, s], pair(t % 2).rearrange("p (k n) -> p k n", n=P),
                                    hT_hi[:, :, s].bitcast(F32), ALU.subtract).then_inc(x_lo, 1)

        def pe_phase0(pe):
            pe.wait_ge(consts_in, 32)
            for t in range(TB):
                pe.wait_ge(x_norm, t + 1)
                if t >= 2:
                    pe.wait_ge(x_lo, t - 1)
                for k in range(KT):
                    last = nc.tensor.transpose(PS[:, 2 * (t % 2) + k // 4, (k % 4) * P:(k % 4 + 1) * P],
                                               xs[t % 2][:, k * P:(k + 1) * P], ident[:])
                last.then_inc(x_tr, 1)

        cT = at("cT", 136, [12, T])
        xpad = [at(f"xpad{i}", 88 + 5 * i, [T + 3]) for i in range(2)]
        acc = [at(f"acc{i}", 98 + 4 * i, [T]) for i in range(2)]
        abT = at("abT", 106, [T])
        cw_in = at("cw_in", 110, [P])
        sq = [at(f"sq{i}", 111 + 4 * i, [T]) for i in range(2)]
        slot = lambda name, i, shape, n=1: at(name, 88 + 2 * i if i < 16 else 184 + 2 * (i - 16), shape)
        qn, kn, kb, kbg = (slot(n, i, [GH, P]) for i, n in enumerate(("qn", "kn", "kb", "kbg")))
        kd, vb = slot("kd", 4, [GH, P]), slot("vb", 5, [GH, P])
        qkb = slot("qkb", 6, [GH, 2, P])
        knT, DT, DsT, attnT, AT, X, Z = (slot(n, 8 + i, [GH, P]) for i, n in enumerate(
            ("knT", "DT", "DsT", "attnT", "AT", "X", "Z")))
        Y, U, uu = slot("Y", 0, [GH, P]), slot("U", 1, [GH, P]), slot("uu", 2, [GH, P])
        trig = slot("trig", 15, [GH, P])
        wq = slot("wq", 16, [GH, 2 * P])
        S, vnew, qS = slot("S", 18, [GH, P]), slot("vnew", 19, [GH, P]), slot("qS", 20, [GH, P])
        o_all = at("o_all", 120, [TB, GH, P])
        zT = at("zT", 136, [GH, T])
        y_hi, y_lo = at("y_hi", 152, [4, T], F32R), at("y_lo", 168, [4, T], F32R)
        ytmp = [at(f"ytmp{i}", 184 + 4 * i, [T]) for i in range(2)]
        osq = at("osq", 88, [TB, GH, P])

        def scal(o, n=TB * GH):
            return small[:, o:o + n]
        abn = scal(24, 256).rearrange("p (t c) -> p t c", c=32)
        s4 = lambda o: scal(o).rearrange("p (t h) -> p t h", h=GH)
        beta, graw, gcs, dgl, eg, ekd, rq, skb, skbg, skd, egl0, egl1, sp_a, sp_b, sp_c = (
            s4(280 + 32 * i) for i in range(15))
        rr = scal(760, 64).rearrange("p (t c) -> p t c", c=8)
        alog, dtb = scal(824, 4), scal(828, 4)
        normg = scal(832, 1)
        cw = scal(840, 48)
        nsa_gate = scal(888, 192).rearrange("p (t c) -> p t c", c=24)
        oss = s4(280)
        ort = s4(312)

        GI = {n: i * P for i, n in enumerate(("tri", "dneg", "strict", "l0", "l1", "l2", "l3", "l4", "l5",
                                              "chunk", "ones", "c0", "c1"))}
        gc = lambda n: consts[:, GI[n]:GI[n] + P]
        overh = lambda ap: ap.unsqueeze(1).to_broadcast([P, GH, P])
        overd = lambda ap: ap.unsqueeze(2).to_broadcast([P, GH, P])

        (g_small_in, cw_tr, cw_ok, pads_ok, conv_sum, conv_act, ab_tr, ab_tok) = (sem(n) for n in (
            "g_small_in", "cw_tr", "cw_ok", "pads_ok", "conv_sum", "conv_act", "ab_tr", "ab_tok"))
        gs_a, gs_d, gs_p, sq_ok, ss_ok = (sem(n) for n in ("gs_a", "gs_d", "gs_p", "sq_ok", "ss_ok"))

        def sp_gdn(sp):
            sp.dma_start(consts[:], A["c_gdn"]).then_inc(g_small_in, 16)
            sp.dma_start(cw_in[0:48, :], A["gdn_conv_w"][0].rearrange("i (c p) -> (i c) p", p=P)).then_inc(g_small_in, 16)
            sp.dma_start(alog, bc(A["gdn_a_log"][0], GH)).then_inc(g_small_in, 16)
            sp.dma_start(dtb, bc(A["gdn_dt_bias"][0], GH)).then_inc(g_small_in, 16)
            sp.dma_start(normg, A["gdn_norm_g"][0].rearrange("(p a) -> p a", a=1)).then_inc(g_small_in, 16)
            load_pieces(sp, 0, P_SMALL + 1)

        def pool_gdn(pool):
            split_pieces(pool, 0, P_SMALL + 1)

        def pe_gdn(pe):
            pe.wait_ge(g_small_in, 80)
            nc.tensor.transpose(PS[:, 4, 0:48], cw_in[0:48, :], ident[0:48, 0:48]).then_inc(cw_tr, 1)
            for p in range(P_SMALL + 1):
                run_job(pe, p)
            pe.wait_ge(tile_evac[P_SMALL % 2], P_SMALL // 2 + 1)
            pe.wait_ge(cw_ok, 1)
            for t in range(TB):
                last = nc.tensor.transpose(PS[:, 5, t * 32:t * 32 + 32], abT[0:32, t * P:(t + 1) * P],
                                           ident[0:32, 0:32])
            last.then_inc(ab_tr, 1)
            pe.wait_ge(gs_d, 3)
            for k, n in enumerate(("tri", "chunk", "c0", "c1")):
                last = nc.tensor.matmul(PS[:, 7, 32 * k:32 * k + 32], gc(n), scal(280 + 32), start=True, stop=True)
            last.then_inc(gs_p, 1)
            for c in range(8):
                pe.wait_ge(sq_ok, c + 1)
                for t in range(TB):
                    last = nc.tensor.matmul(PS[:, 6, t * 8 + c:t * 8 + c + 1], sq[c % 2][:, t * P:(t + 1) * P],
                                            gc("ones")[:, 0:1], start=True, stop=True)
                last.then_inc(ss_ok, 1)

        def act_gdn(act):
            for c in range(12 + 1):
                if c < 12:
                    act.wait_ge(tile_done, c + 1)
                    if c == 0:
                        act.wait_ge(pads_ok, 2)
                    if c >= 2:
                        act.wait_ge(conv_sum, c - 1)
                    evac_done(nc.scalar.activation(xpad[c % 2][:, 3:], pair(c % 2), ACT.Copy), c)
                if c >= 1:
                    act.wait_ge(conv_sum, c)
                    nc.scalar.activation(cT[:, c - 1], acc[(c - 1) % 2][:], ACT.Silu).then_inc(conv_act, 1)
            act.wait_ge(tile_done, P_SMALL + 1)
            evac_done(nc.scalar.activation(abT[0:32, :], pair(P_SMALL % 2)[0:32, :], ACT.Copy), P_SMALL)
            act.wait_ge(ab_tok, 1)
            astep(nc.scalar.activation(beta, abn[:, :, 4:8], ACT.Sigmoid))
            astep(nc.scalar.activation(nsa_gate, abn[:, :, 8:32], ACT.Sigmoid))
            act.wait_ge(gs_d, 1)
            astep(nc.scalar.activation(sp_b, sp_a, ACT.Abs))
            astep(nc.scalar.activation(sp_b, sp_b, ACT.Exp, scale=-1.0))
            astep(nc.scalar.activation(sp_b, sp_b, ACT.Ln, bias=1.0))
            nc.scalar.activation(alog, alog, ACT.Exp).then_inc(gs_a, 1)
            act.wait_ge(gs_p, 1)
            psg = lambda k: PS[:, 7, 32 * k:32 * k + 32].rearrange("p (t h) -> p t h", h=GH)
            nc.scalar.activation(eg, psg(0), ACT.Exp)
            nc.scalar.activation(egl0, psg(2), ACT.Exp)
            nc.scalar.activation(egl1, psg(3), ACT.Exp).then_inc(gs_a, 1)
            act.wait_ge(gs_d, 5)
            nc.scalar.activation(ekd, dgl, ACT.Exp).then_inc(gs_a, 1)
            for c in range(8):
                act.wait_ge(conv_act, c + 1)
                if c >= 2:
                    act.wait_ge(ss_ok, c - 1)
                nc.scalar.activation(sq[c % 2][:], cT[:, c], ACT.Square).then_inc(sq_ok, 1)
            act.wait_ge(ss_ok, 8)
            nc.scalar.activation(scal(760, 64), PS[:, 6, 0:64], ACT.Sqrt, bias=eps_t).then_inc(gs_a, 1)

        def dve_gdn(dve):
            nc.vector.memset(xpad[0][:, 0:3], 0.0).then_inc(pads_ok, 1)
            nc.vector.memset(xpad[1][:, 0:3], 0.0).then_inc(pads_ok, 1)
            dve.wait_ge(cw_tr, 1)
            nc.vector.tensor_copy(cw, PS[:, 4, 0:48]).then_inc(cw_ok, 1)
            dve.wait_ge(cw_ok, 1)
            for c in range(12):
                x, a = xpad[c % 2], acc[c % 2]
                dve.wait_ge(tile_evac[c % 2], c // 2 + 1)
                if c >= 2:
                    dve.wait_ge(conv_act, c - 1)
                w = lambda i: cw[:, i * 12 + c:i * 12 + c + 1]
                dstep(nc.vector.tensor_scalar(a[:], x[:, 3:T + 3], w(3), None, ALU.mult))
                for i in (2, 1):
                    dstep(nc.vector.scalar_tensor_tensor(out=a[:], in0=x[:, i:T + i], scalar=w(i), in1=a[:],
                                                         op0=ALU.mult, op1=ALU.add))
                nc.vector.scalar_tensor_tensor(out=a[:], in0=x[:, 0:T], scalar=w(0), in1=a[:],
                                               op0=ALU.mult, op1=ALU.add).then_inc(conv_sum, 1)
            dve.wait_ge(ab_tr, 1)
            nc.vector.tensor_copy(scal(24, 256), PS[:, 5, 0:256]).then_inc(ab_tok, 1)
            dve.wait_ge(ab_tok, 1)
            b8 = lambda ap: ap.unsqueeze(1).to_broadcast([P, TB, GH])
            dve.wait_ge(g_small_in, 80)
            nc.vector.tensor_tensor(sp_a, abn[:, :, 0:4], b8(dtb), ALU.add).then_inc(gs_d, 1)
            dve.wait_ge(gs_a, 1)
            dve.wait_ge(gs_d, 1)
            nc.vector.scalar_tensor_tensor(out=sp_c, in0=sp_a, scalar=0.0, in1=sp_b, op0=ALU.max,
                                           op1=ALU.add).then_inc(gs_d, 1)
            dve.wait_ge(gs_d, 2)
            nc.vector.scalar_tensor_tensor(out=graw, in0=sp_c, scalar=-1.0, in1=b8(alog), op0=ALU.mult,
                                           op1=ALU.mult).then_inc(gs_d, 1)
            dve.wait_ge(gs_p, 1)
            dve.wait_ge(gs_a, 2)
            psg = lambda k: PS[:, 7, 32 * k:32 * k + 32].rearrange("p (t h) -> p t h", h=GH)
            nc.vector.tensor_copy(gcs, psg(0)).then_inc(gs_d, 1)
            dve.wait_ge(gs_d, 4)
            nc.vector.tensor_tensor(dgl, psg(1), gcs, ALU.subtract).then_inc(gs_d, 1)
            dve.wait_ge(gs_a, 4)
            dstep(nc.vector.reciprocal(scal(760, 64), scal(760, 64)))
            dstep(nc.vector.tensor_scalar(rq, rr[:, :, 0:4], float(GD) ** -0.5, None, ALU.mult))
            dstep(nc.vector.tensor_tensor(skb, rr[:, :, 4:8], beta, ALU.mult))
            dstep(nc.vector.tensor_tensor(skbg, skb, eg, ALU.mult))
            dstep(nc.vector.tensor_tensor(skd, rr[:, :, 4:8], ekd, ALU.mult))

        LV = range(1, 6)
        GP = Steps(sem("gdn_pe"), ["tok", "tr", "gram", "xz"] + [f"{n}{l}" for l in LV for n in ("y", "z")] +
                   ["uw", "ws0", "st0", "ws1", "st1", "oi"])
        GA = Steps(sem("gdn_act"), ["trs", "exp", "x"] + [f"y{l}" for l in LV] + ["wq", "qs0", "qs1"])
        GV = Steps(sem("gdn_dve"), ["scaled", "trig", "dm", "dg", "ds", "attn", "at", "u0", "z0"] +
                   [f"{n}{l}" for l in LV for n in ("u", "x", "z")] +
                   ["u", "v0", "sd0", "s0", "v1", "sd1", "s1", "qe", "o"])

        def gstep(steps, ins):
            ins.then_inc(steps.sem, 1)

        def bank4(k):
            return PS[:, k, :].rearrange("p (h n) -> p h n", h=GH)

        def pe_gdn_blocks(pe):
            for t in range(TB):
                s = slice(t * P, (t + 1) * P)
                if t:
                    GV.wait(pe, t - 1, "o")
                for j in range(3):
                    for h in range(GH):
                        last = nc.tensor.transpose(bank4(j)[:, h], cT[:, 4 * j + h, s], ident[:])
                gstep(GP, last)
                GV.wait(pe, t, "scaled")
                for j, src in enumerate((qn, kn, kb)):
                    for h in range(GH):
                        last = nc.tensor.transpose(bank4(3 + j)[:, h], src[:, h], ident[:])
                gstep(GP, last)
                GV.wait(pe, t, "trig")
                nc.tensor.matmul(PS[:, 0, :], gc("ones"), trig[:].rearrange("p h n -> p (h n)"), start=True, stop=True)
                GA.wait(pe, t, "trs")
                for h in range(GH):
                    last = nc.tensor.matmul(PS[:, 6 + h // 2, (h % 2) * 256:(h % 2) * 256 + 256], knT[:, h],
                                            qkb[:, h].rearrange("p a n -> p (a n)"), start=True, stop=True)
                gstep(GP, last)
                GV.wait(pe, t, "z0")
                for h in range(GH):
                    last = nc.tensor.transpose(bank4(1)[:, h], Z[:, h], ident[:])
                gstep(GP, last)
                for l in LV:
                    GV.wait(pe, t, f"u{l}")
                    if l > 1:
                        GV.wait(pe, t, f"z{l - 1}")
                    else:
                        GA.wait(pe, t, "x")
                    for h in range(GH):
                        last = nc.tensor.matmul(bank4(2)[:, h], U[:, h], X[:, h], start=True, stop=True)
                    gstep(GP, last)
                    GA.wait(pe, t, f"y{l}")
                    for h in range(GH):
                        nc.tensor.matmul(bank4(3)[:, h], Z[:, h], Y[:, h], start=True, stop=True)
                    for h in range(GH):
                        last = nc.tensor.matmul(bank4(4)[:, h], Y[:, h], Z[:, h], start=True, stop=True)
                    gstep(GP, last)
                GV.wait(pe, t, "z5")
                for h in range(GH):
                    nc.tensor.matmul(bank4(5)[:, h], Z[:, h], vb[:, h], start=True, stop=True)
                for h in range(GH):
                    last = nc.tensor.matmul(bank4(0)[:, h], kbg[:, h], Z[:, h], start=True, stop=True)
                gstep(GP, last)
                for c in range(2):
                    r = slice(GC * c, GC * c + GC)
                    GA.wait(pe, t, "wq" if c == 0 else "qs0")
                    GV.wait(pe, t, "u" if c == 0 else "s0")
                    for h in range(GH):
                        last = nc.tensor.matmul(bank4(6)[:, h], wq[:, h, c * P:(c + 1) * P], S[:, h], start=True, stop=True)
                    gstep(GP, last)
                    GV.wait(pe, t, f"v{c}")
                    for h in range(GH):
                        last = nc.tensor.matmul(bank4(7)[:, h], kd[r, h], vnew[r, h], start=True, stop=True)
                    gstep(GP, last)
                for h in range(GH):
                    last = nc.tensor.matmul(bank4(1)[:, h], attnT[:, h], vnew[:, h], start=True, stop=True)
                gstep(GP, last)

        def act_gdn_blocks(act):
            for t in range(TB):
                GP.wait(act, t, "tr")
                nc.scalar.activation(qkb[:, :, 0, :], bank4(3), ACT.Copy)
                nc.scalar.activation(qkb[:, :, 1, :], bank4(5), ACT.Copy)
                gstep(GA, nc.scalar.activation(knT[:], bank4(4), ACT.Copy))
                GV.wait(act, t, "dg")
                gstep(GA, nc.scalar.activation(DT[:], DT[:], ACT.Exp))
                GP.wait(act, t, "xz")
                gstep(GA, nc.scalar.activation(X[:], bank4(1), ACT.Copy))
                for l in LV:
                    GP.wait(act, t, f"y{l}")
                    gstep(GA, nc.scalar.activation(Y[:], bank4(2), ACT.Copy))
                GP.wait(act, t, "uw")
                nc.scalar.activation(wq[:, :, 0:64], bank4(0)[:, :, 0:64], ACT.Copy)
                nc.scalar.activation(wq[:, :, 192:256], bank4(0)[:, :, 64:128], ACT.Copy)
                gstep(GA, nc.scalar.activation(wq[:, :, 64:192], qkb[:, :, 0, :], ACT.Copy))
                for c in range(2):
                    GP.wait(act, t, f"ws{c}")
                    GV.wait(act, t, f"v{c}")
                    gstep(GA, nc.scalar.activation(qS[GC * c:GC * c + GC], bank4(6)[GC * (1 - c):GC * (1 - c) + GC],
                                                   ACT.Copy))

        def dve_gdn_blocks(dve):
            tt = nc.vector.tensor_tensor
            dstep(nc.vector.memset(S[:], 0.0))
            for t in range(TB):
                if t:
                    GV.wait(dve, t - 1, "o")
                GP.wait(dve, t, "tok")
                rk = rr[:, t, 4:8]
                tt(qn[:], bank4(0), overd(rq[:, t]), ALU.mult)
                tt(kn[:], bank4(1), overd(rk), ALU.mult)
                tt(kb[:], bank4(1), overd(skb[:, t]), ALU.mult)
                tt(kbg[:], bank4(1), overd(skbg[:, t]), ALU.mult)
                tt(kd[:], bank4(1), overd(skd[:, t]), ALU.mult)
                gstep(GV, tt(vb[:], bank4(2), overd(beta[:, t]), ALU.mult))
                gstep(GV, tt(trig[:], overh(gc("tri")), overd(graw[:, t]), ALU.mult))
                GP.wait(dve, t, "gram")
                gstep(GV, tt(DT[:], bank4(0), overh(gc("dneg")), ALU.add))
                GV.wait(dve, t, "dm")
                gstep(GV, tt(DT[:], DT[:], overd(gcs[:, t]), ALU.subtract))
                GA.wait(dve, t, "exp")
                gstep(GV, tt(DsT[:], DT[:], overh(gc("strict")), ALU.mult))
                gq = PS[:, 6:8, :].rearrange("p a (b c n) -> p (a b) c n", b=2, c=2)
                gstep(GV, tt(attnT[:], gq[:, :, 0, :], DT[:], ALU.mult))
                GV.wait(dve, t, "ds")
                gstep(GV, tt(AT[:], gq[:, :, 1, :], DsT[:], ALU.mult))
                GV.wait(dve, t, "at")
                gstep(GV, tt(U[:], AT[:], overh(gc("l0")), ALU.mult))
                GV.wait(dve, t, "u0")
                gstep(GV, tt(Z[:], overh(ident[:]), U[:], ALU.subtract))
                for l in LV:
                    if l > 1:
                        GP.wait(dve, t, f"y{l - 1}")
                    else:
                        GV.wait(dve, t, "z0")
                    gstep(GV, tt(U[:], AT[:], overh(gc(f"l{l}")), ALU.mult))
                    GP.wait(dve, t, f"z{l}")
                    gstep(GV, tt(X[:], X[:], bank4(3), ALU.subtract))
                    gstep(GV, tt(Z[:], Z[:], bank4(4), ALU.subtract))
                    GV.wait(dve, t, f"z{l}")
                GP.wait(dve, t, "uw")
                gstep(GV, nc.vector.tensor_copy(uu[:], bank4(5)))
                GV.wait(dve, t, "u")
                for c in range(2):
                    r = slice(GC * c, GC * c + GC)
                    GP.wait(dve, t, f"ws{c}")
                    gstep(GV, tt(vnew[r], uu[r], bank4(6)[r], ALU.subtract))
                    gstep(GV, tt(S[:], S[:], overd((egl0, egl1)[c][:, t]), ALU.mult))
                    GP.wait(dve, t, f"st{c}")
                    GV.wait(dve, t, f"sd{c}")
                    gstep(GV, tt(S[:], S[:], bank4(7), ALU.add))
                    GV.wait(dve, t, f"s{c}")
                GA.wait(dve, t, "qs1")
                gstep(GV, tt(qS[:], qS[:], overd(eg[:, t]), ALU.mult))
                GP.wait(dve, t, "oi")
                GV.wait(dve, t, "qe")
                gstep(GV, tt(o_all[:, t], qS[:], bank4(1), ALU.add))

        o_ss, o_r, o_nrm, o_tr, y_mul, y_hi_ok, y_lo_ok = (sem(n) for n in (
            "o_ss", "o_r", "o_nrm", "o_tr", "y_mul", "y_hi_ok", "y_lo_ok"))

        def sp_gdn_out(sp):
            load_pieces(sp, P_GZ, P_GZ + 4)

        def pool_gdn_out(pool):
            split_pieces(pool, P_GZ, P_GZ + 4)

        def pe_gdn_out(pe):
            for h in range(GH):
                run_job(pe, P_GZ + h)
            pe.wait_ge(o_nrm, 1)
            for h in range(GH):
                if h >= 2:
                    pe.wait_ge(y_mul, h - 1)
                for t in range(TB):
                    last = nc.tensor.transpose(PS[:, 4 + 2 * (h % 2) + t // 4, (t % 4) * P:(t % 4 + 1) * P],
                                               o_all[:, t, h], ident[:])
                last.then_inc(o_tr, 1)

        def split_y(act, k, src):
            nc.scalar.activation(y_hi[:, k], src, ACT.Copy).then_inc(y_hi_ok, 1)

        def act_gdn_out(act):
            nc.scalar.activation(osq[:], o_all[:], ACT.Square).then_inc(o_ss, 1)
            act.wait_ge(o_r, 1)
            nc.scalar.activation(ort, oss, ACT.Sqrt, scale=1.0 / GD, bias=eps_t).then_inc(o_ss, 1)
            for h in range(GH):
                p = P_GZ + h
                act.wait_ge(tile_done, p + 1)
                evac_done(nc.scalar.activation(zT[:, h], pair(p % 2), ACT.Silu), p)
            for h in range(GH):
                act.wait_ge(y_mul, h + 1)
                split_y(act, h, ytmp[h % 2][:])

        def dve_gdn_out(dve):
            dve.wait_ge(o_ss, 1)
            nc.vector.tensor_reduce(oss, osq[:], AX_X, ALU.add).then_inc(o_r, 1)
            dve.wait_ge(o_ss, 2)
            dstep(nc.vector.reciprocal(ort, ort))
            nc.vector.tensor_tensor(o_all[:], o_all[:], ort.unsqueeze(3).to_broadcast([P, TB, GH, P]),
                                    ALU.mult).then_inc(o_nrm, 1)
            for h in range(GH):
                p = P_GZ + h
                dve.wait_ge(o_tr, h + 1)
                dve.wait_ge(tile_evac[p % 2], p // 2 + 1)
                if h >= 2:
                    dve.wait_ge(y_lo_ok, h - 1)
                nc.vector.scalar_tensor_tensor(out=ytmp[h % 2][:], in0=pair(2 + h % 2), scalar=normg, in1=zT[:, h],
                                               op0=ALU.mult, op1=ALU.mult).then_inc(y_mul, 1)
                dve.wait_ge(y_hi_ok, h + 1)
                nc.vector.tensor_tensor(y_lo[:, h], ytmp[h % 2][:], y_hi[:, h].bitcast(F32),
                                        ALU.subtract).then_inc(y_lo_ok, 1)

        G = [at(f"G{i}", 136 + 4 * i, [T]) for i in range(2)]
        mtmp = at("mtmp", 144, [T])
        gate_ok, merged = sem("gate_ok"), sem("merged")

        def sp_merge(sp, b):
            load_pieces(sp, P_MERGE[b], P_MERGE[b] + 2 * KT)

        def pool_merge(pool, b):
            split_pieces(pool, P_MERGE[b], P_MERGE[b] + 2 * KT)

        def pe_merge(pe, b):
            for c in range(KT):
                run_job(pe, P_MERGE[b] + 2 * c)
                run_job(pe, P_MERGE[b] + 2 * c + 1, y_hi, y_lo)

        def act_merge(act, b):
            for c in range(KT):
                p, n = P_MERGE[b] + 2 * c, b * KT + c
                act.wait_ge(tile_done, p + 1)
                if n >= 2:
                    act.wait_ge(merged, n - 1)
                evac_done(nc.scalar.activation(G[c % 2][:], pair(p % 2), ACT.Sigmoid), p)

        def dve_merge(dve, b):
            for c in range(KT):
                p, n = P_MERGE[b] + 2 * c, b * KT + c
                dve.wait_ge(tile_done, p + 2)
                dve.wait_ge(tile_evac[p % 2], p // 2 + 1)
                dst = mT[:, c] if b == 0 else mtmp[:]
                evac_done(nc.vector.tensor_tensor(dst, pair((p + 1) % 2), G[c % 2][:], ALU.mult), p + 1)
                dve.wait_ge(tile_evac[(p + 1) % 2], (p + 1) // 2 + 1)
                if b == 0:
                    nc.vector.tensor_copy(mtmp[:, 0:1], mT[:, c, 0:1]).then_inc(merged, 1)
                else:
                    nc.vector.tensor_tensor(mT[:, c], mT[:, c], mtmp[:], ALU.add).then_inc(merged, 1)
                dve.wait_ge(merged, n + 1)
        QT = at("QT", 136, [NM, T])
        kslc, kwin = at("kslc", 152, [T]), at("kwin", 156, [T])
        vslc, vwin = at("vslc", 160, [TB, P]), at("vwin", 164, [TB, P])
        cmpT = [at("kcmpT", 168, [T]), at("vcmpT", 172, [T])]
        vT = [at(f"vT{i}", 176 + 4 * i, [T]) for i in range(2)]
        window = at("window", 184, [CL, 64])
        wcmp = at("wcmp", 120, [CL, P])
        pos_in = at("pos_in", 192, [2, P])
        posT = at("posT", 193, [2, CL])
        kcT, vcT = at("kcT", 205.5, [64]), at("vcT", 205.75, [2, 64])
        vc = at("vc", 206.25, [P])
        P4 = at("P4", 206.75, [NG, 68])
        msel = at("msel", 207.28125, [NG, NSEL])
        score = at("score", 207.40625, [NG, NSEL])
        maskw = at("maskw", 188, [WT, P])
        maskg = at("maskg", 168, [NG, T])
        sbuf = [at(f"sbuf{i}", 176 + 4 * i, [T]) for i in range(2)]
        pT = at("pT", 184, [TB, P])
        oacc = at("oacc", 192, [NM, NG, ND])
        sc = at("sc", 176, [NH, 64])
        pcT = at("pcT", 180, [NH // 2, P])
        cgt, ceq = at("cgt", 184, [NG, NSEL, NSEL]), at("ceq", 186, [NG, NSEL, NSEL])
        c8 = lambda o: scal(o, 8)
        cmx, csm = c8(0), c8(8)
        nmx, rsum = scal(1080, 2), scal(1082, 2)
        wrow = scal(1084, 2)
        NI = {}
        o = 0
        for n, k in (("causal", P), ("old", P), ("lower", NSEL * NSEL), ("cneg", TB * 64), ("cval", TB * 64),
                     ("bias", TB * NSEL)):
            NI[n] = (o, o + k)
            o += k
        ncst = lambda n: consts[:, NI[n][0]:NI[n][1]]

        (n_in, pos_tr, pos_ok, v_tr, v_tok, win_ok, kc_ok, kc_evac, vc_tr, vc_ok, wc_zero, mw_ok) = (
            sem(n) for n in ("n_in", "pos_tr", "pos_ok", "v_tr", "v_tok", "win_ok", "kc_ok", "kc_evac", "vc_tr",
                             "vc_ok", "wc_zero", "mw_ok"))
        wc_in = sem("wc_in")

        def load_wcmp(sp, name):
            src = A[name][0].rearrange("l d e -> d l e")
            for g in range(NG):
                r = slice(ND * g, ND * g + ND)
                sp.dma_start(wcmp[r, :, r], src).then_inc(wc_in, 16)

        def sp_nsa(sp):
            sp.dma_start(consts[:], A["c_nsa"]).then_inc(n_in, 16)
            for i, n in enumerate(("nsa_cmp_pk", "nsa_cmp_pv")):
                for g in range(NG):
                    sp.dma_start(pos_in[0:CL, i, ND * g:ND * g + ND], A[n][0]).then_inc(n_in, 16)
            sp.wait_ge(wc_zero, 1)
            load_wcmp(sp, "nsa_cmp_wk")
            load_pieces(sp, P_NSA, P_NSA + 10)
            sp.wait_ge(kc_ok, 1)
            load_wcmp(sp, "nsa_cmp_wv")

        def pool_nsa(pool):
            nc.gpsimd.memset(wcmp[:], 0.0).then_inc(wc_zero, 1)
            split_pieces(pool, P_NSA, P_NSA + 10)
            for k in range(2):
                pool.wait_ge(tile_evac[(P_NSA + k) % 2], (P_NSA + k) // 2 + 1)
                pool.wait_ge(pos_ok, 2)
                if k == 1:
                    pool.wait_ge(kc_ok, 1)
                for half in range(2):
                    ins = nc.gpsimd.tensor_tensor(
                        window[:, 16 * half:16 * half + 16, 0:NCMP],
                        cmpT[k][:, 16 * half:16 * half + 16 * NCMP].rearrange("p (n s) -> p s n", s=CS),
                        posT[:, k, 16 * half:16 * half + 16].unsqueeze(2).to_broadcast([P, 16, NCMP]), ALU.add)
                ins.then_inc(win_ok, 1)

        def pe_nsa(pe):
            pe.wait_ge(n_in, 80)
            for i in range(2):
                nc.tensor.transpose(PS[:, 4, CL * i:CL * i + CL], pos_in[0:CL, i], ident[0:CL, 0:CL]).then_inc(pos_tr, 1)
            for p in range(P_NSA, P_NSA + 10):
                run_job(pe, p)
                if p - P_NSA in (4, 6):
                    i = (p - P_NSA - 4) // 2
                    q = P_NSA + 3 + 2 * i
                    pe.wait_ge(tile_evac[q % 2], q // 2 + 1)
                    if i:
                        pe.wait_ge(v_tok, 1)
                    for t in range(TB):
                        last = nc.tensor.transpose(PS[:, 6 + t // 4, (t % 4) * P:(t % 4 + 1) * P],
                                                   vT[i][:, t * P:(t + 1) * P], ident[:])
                    last.then_inc(v_tr, 1)
            for k in range(2):
                pe.wait_ge(win_ok, k + 1)
                pe.wait_ge(wc_in, 32 * (k + 1))
                for l in range(CL):
                    last = nc.tensor.matmul(PS[:, 4 + k, 0:NCMP], wcmp[:, l], window[:, l, 0:NCMP],
                                            start=(l == 0), stop=(l == CL - 1))
                last.then_inc(kc_ok, 1)
            pe.wait_ge(kc_evac, 2)
            pe.wait_ge(v_tok, 2)
            nc.tensor.transpose(PS[:, 6, 0:P], vcT[:].rearrange("p a n -> p (a n)"), ident[:]).then_inc(vc_tr, 1)

        def act_nsa(act):
            for k in range(10):
                p = P_NSA + k
                act.wait_ge(tile_done, p + 1)
                dst = (cmpT[0], cmpT[1], kslc, vT[0], kwin, vT[1])[k][:] if k < 6 else QT[:, k - 6]
                evac_done(nc.scalar.activation(dst, pair(p % 2), ACT.Copy, scale=1.0 if k < 6 else float(ND) ** -0.5), p)
            act.wait_ge(mw_ok, 3)
            act.wait_ge(kc_ok, 1)
            nc.scalar.activation(kcT[:, 0:NCMP], PS[:, 4, 0:NCMP], ACT.Copy).then_inc(kc_evac, 1)
            act.wait_ge(kc_ok, 2)
            nc.scalar.activation(vcT[:, :, 0:NCMP], PS[:, 5, 0:NCMP].unsqueeze(1).to_broadcast([P, 2, NCMP]),
                                 ACT.Copy).then_inc(kc_evac, 1)
            act.wait_ge(vc_tr, 1)
            nc.scalar.activation(vc[:], PS[:, 6, 0:P], ACT.Copy).then_inc(vc_ok, 1)

        def dve_nsa(dve):
            for i in range(2):
                dve.wait_ge(pos_tr, 2)
                nc.vector.tensor_copy(posT[:, i], PS[:, 4, CL * i:CL * i + CL]).then_inc(pos_ok, 1)
            for zero in (P4[:], kcT[:], vcT[:]):
                nc.vector.memset(zero, 0.0).then_inc(mw_ok, 1)
            for i, dst in enumerate((vslc, vwin)):
                dve.wait_ge(v_tr, i + 1)
                nc.vector.tensor_copy(dst[:].rearrange("p t n -> p (t n)"), pair(3)).then_inc(v_tok, 1)

        CP = Steps(sem("cmp_pe"), ["s", "t", "o", "yt"])
        CA = Steps(sem("cmp_act"), ["e", "pt", "y"])
        CV = Steps(sem("cmp_dve"), ["s", "mx", "sub", "sm", "r", "p", "pv", "oacc", "p4", "i", "i2", "sc", "gt", "eq",
                                    "low", "rank", "sum", "sel"])
        CG = Steps(sem("cmp_pool"), ["m", "mc"])
        UP = Steps(sem("unit_pe"), ["s", "t", "o"])
        UA = Steps(sem("unit_act"), ["e", "pt"])
        UV = Steps(sem("unit_dve"), ["s", "mx", "r", "w", "o"])
        NU = 2 * NH

        def unit(u):
            t, r = divmod(u, NU)
            g, r = divmod(r, 2 * NM)
            m, kind = divmod(r, 2)
            first = 0 if kind == 0 else max(0, t - WT + 1)
            n = t + 1 - first
            mask = maskg[:, g, 0:n * P] if kind == 0 else maskw[:, WT - n:WT].rearrange("p a b -> p (a b)")
            return t, g, m, kind, first, n, (kslc, kwin)[kind], (vslc, vwin)[kind], mask

        def pe_cmp(pe, t):
            for g in range(NG):
                r = slice(ND * g, ND * g + ND)
                for m in range(NM):
                    hh = g * NM + m
                    last = nc.tensor.matmul(PS[:, 4 + g, 64 * m:64 * m + 64], QT[r, m, t * P:(t + 1) * P],
                                            kcT[r, :], start=True, stop=True)
            gstep(CP, last)
            CV.wait(pe, t, "pv")
            for k in range(NH // 2):
                last = nc.tensor.transpose(PS[:, 6, k * P:(k + 1) * P],
                                           sc[:, 2 * k:2 * k + 2].rearrange("p a n -> p (a n)"), ident[:])
            gstep(CP, last)
            CA.wait(pe, t, "pt")
            for hh in range(NH):
                g, r = hh // NM, slice(64 * (hh % 2), 64 * (hh % 2) + 64)
                last = nc.tensor.matmul(PS[:, 4 + hh % 2, ND * (hh // 2):ND * (hh // 2) + ND], pcT[r, hh // 2], vc[r, ND * g:ND * g + ND],
                                        start=True, stop=True)
            gstep(CP, last)

        def pe_scores(pe, u):
            t, g, m, kind, first, n, keys, vals, mask = unit(u)
            r = slice(ND * g, ND * g + ND)
            if u >= 2:
                UV.wait(pe, u - 2, "s")
            for a in range(0, n * P, 512):
                w = min(512, n * P - a)
                last = nc.tensor.matmul(pair(u % 2)[:, a:a + w], QT[r, m, t * P:(t + 1) * P],
                                        keys[r, first * P + a:first * P + a + w], start=True, stop=True)
            gstep(UP, last)

        def pe_values(pe, u):
            t, g, m, kind, first, n, keys, vals, mask = unit(u)
            UA.wait(pe, u, "e")
            if u >= 1:
                UA.wait(pe, u - 1, "pt")
            for k in range(n):
                last = nc.tensor.transpose(pair(2)[:, k * P:(k + 1) * P], sbuf[u % 2][:, k * P:(k + 1) * P], ident[:])
            gstep(UP, last)
            UA.wait(pe, u, "pt")
            if u >= 2:
                UV.wait(pe, u - 2, "o")
            for k in range(n):
                last = nc.tensor.matmul(PS[:, 6 + u % 2, 0:ND], pT[:, k], vals[:, first + k, ND * g:ND * g + ND],
                                        start=(k == 0), stop=(k == n - 1))
            gstep(UP, last)

        def pe_nsa_attn(pe):
            for t in range(TB):
                u0 = t * NU
                if t:
                    CA.wait(pe, t - 1, "y")
                pe_cmp(pe, t)
                CV.wait(pe, t, "oacc")
                for u in range(u0, u0 + NU):
                    pe_scores(pe, u)
                    pe_values(pe, u)
                UV.wait(pe, u0 + NU - 1, "o")
                for m in range(NM):
                    last = nc.tensor.transpose(PS[:, 4, m * P:(m + 1) * P], oacc[:, m].rearrange("p g d -> p (g d)"), ident[:])
                gstep(CP, last)

        def act_nsa_attn(act):
            for t in range(TB):
                u0 = t * NU
                CV.wait(act, t, "sub")
                gstep(CA, nc.scalar.activation(sc[:], sc[:], ACT.Exp))
                CP.wait(act, t, "t")
                gstep(CA, nc.scalar.activation(pcT[:].rearrange("p h n -> p (h n)"), PS[:, 6, :], ACT.Copy))
                for u in range(u0, u0 + NU):
                    n = unit(u)[5]
                    b = u % 2
                    UV.wait(act, u, "mx")
                    nc_s = sbuf[b][:, 0:n * P]
                    gstep(UA, nc.scalar.activation(nc_s, nc_s, ACT.Exp, bias=nmx[:, b:b + 1], accum_out=rsum[:, b:b + 1]))
                    UP.wait(act, u, "t")
                    if u >= 1:
                        UP.wait(act, u - 1, "o")
                    gstep(UA, nc.scalar.activation(pT[:, 0:n].rearrange("p k n -> p (k n)"), pair(2)[:, 0:n * P], ACT.Copy))
                CP.wait(act, t, "yt")
                gstep(CA, nc.scalar.activation(yT[:, :, t * P:(t + 1) * P],
                                               PS[:, 4, :].rearrange("p (m n) -> p m n", m=NM), ACT.Copy))

        def pool_nsa_attn(pool):
            for t in range(TB):
                if t:
                    UV.wait(pool, t * NU - 1, "s")
                    CG.wait(pool, t - 1, "mc")
                CV.wait(pool, t, "sel")
                for g in range(NG):
                    ins = nc.gpsimd.tensor_copy(maskg[:, g, 0:(t + 1) * P].rearrange("p (j l) -> p j l", l=SL),
                                                msel[:, g, 0:2 * (t + 1)].unsqueeze(2).to_broadcast([P, 2 * (t + 1), SL]))
                gstep(CG, ins)
                CG.wait(pool, t, "m")
                last = maskg[:, :, t * P:(t + 1) * P]
                gstep(CG, nc.gpsimd.tensor_tensor(last, last, ncst("causal").unsqueeze(1).to_broadcast([P, NG, P]), ALU.add))

        def dve_cmp(dve, t):
            tt, red = nc.vector.tensor_tensor, nc.vector.tensor_reduce
            scn = sc[:]
            sc4 = sc[:].rearrange("p (g m) n -> p g m n", g=NG)
            over8 = lambda n: ncst(n)[:, 64 * t:64 * t + 64].unsqueeze(1).unsqueeze(1).to_broadcast([P, NG, NM, 64])
            along = lambda ap: ap.unsqueeze(2).to_broadcast([P, NH, 64])
            step = lambda n, ins: (gstep(CV, ins), CV.wait(dve, t, n))
            CP.wait(dve, t, "s")
            step("s", tt(sc4, PS[:, 4:6, 0:256].rearrange("p g (m n) -> p g m n", m=NM), over8("cneg"), ALU.add))
            step("mx", red(cmx, scn, AX_X, ALU.max))
            step("sub", tt(scn, scn, along(cmx), ALU.subtract))
            CA.wait(dve, t, "e")
            step("sm", red(csm, scn, AX_X, ALU.add))
            step("r", nc.vector.reciprocal(csm, csm))
            step("p", tt(scn, scn, along(csm), ALU.mult))
            step("pv", tt(sc4, sc4, over8("cval"), ALU.mult))
            CP.wait(dve, t, "o")
            gates = nsa_gate[:, t].rearrange("p (g k a c) -> p a g k c", g=NG, a=2, c=3)[:, :, :, :, 0]
            for par in range(2):
                ins = tt(oacc[:].rearrange("p (k a) g d -> p a g k d", a=2)[:, par],
                         PS[:, 4 + par, 0:256].rearrange("p (g k d) -> p g k d", g=NG, k=2),
                         gates[:, par].unsqueeze(3).to_broadcast([P, NG, 2, ND]), ALU.mult)
            step("oacc", ins)
            imp = score[:]
            step("p4", red(P4[:, :, 1:1 + NCMP], sc[:].rearrange("p (g m) n -> p g n m", g=NG)[:, :, 0:NCMP, :], AX_X,
                           ALU.add))
            step("i", red(imp, P4[:, :, 0:64].rearrange("p g (j f) -> p g j f", f=4), AX_X, ALU.add))
            step("i2", tt(imp, imp, P4[:, :, 4:68].rearrange("p g (j f) -> p g j f", f=4)[:, :, :, 0], ALU.add))
            step("sc", tt(imp, imp, ncst("bias")[:, NSEL * t:NSEL * (t + 1)].unsqueeze(1).to_broadcast([P, NG, NSEL]),
                          ALU.add))
            full = [P, NG, NSEL, NSEL]
            si, sj = imp.unsqueeze(2).to_broadcast(full), imp.unsqueeze(3).to_broadcast(full)
            step("gt", tt(cgt[:], si, sj, ALU.is_gt))
            step("eq", tt(ceq[:], si, sj, ALU.is_equal))
            step("low", tt(ceq[:], ceq[:], ncst("lower").rearrange("p (j i) -> p j i", i=NSEL).unsqueeze(1)
                           .to_broadcast(full), ALU.mult))
            step("rank", tt(cgt[:], cgt[:], ceq[:], ALU.add))
            step("sum", red(msel[:], cgt[:], AX_X, ALU.add))
            step("sel", nc.vector.tensor_scalar(msel[:], msel[:], float(TOPK), NEG, ALU.is_ge, ALU.mult))

        def dve_nsa_attn(dve):
            dstep(nc.vector.memset(maskw[:], 0.0))
            dve.wait_ge(n_in, 80)
            dstep(nc.vector.tensor_copy(maskw[:, 0], ncst("old")))
            dstep(nc.vector.tensor_copy(maskw[:, WT - 1], ncst("causal")))
            for t in range(TB):
                if t:
                    CA.wait(dve, t - 1, "y")
                    CG.wait(dve, t - 1, "mc")
                dve_cmp(dve, t)
                for u in range(t * NU, (t + 1) * NU):
                    _, g, m, kind, first, n, keys, vals, mask = unit(u)
                    b, s = u % 2, sbuf[u % 2][:, 0:n * P]
                    UP.wait(dve, u, "s")
                    if u % NU == 0:
                        CG.wait(dve, t, "mc")
                    if u >= 2:
                        UP.wait(dve, u - 2, "t")
                    gstep(UV, nc.vector.tensor_tensor(s, pair(b)[:, 0:n * P], mask, ALU.add))
                    UV.wait(dve, u, "s")
                    gstep(UV, nc.vector.tensor_reduce(nmx[:, b:b + 1], s, AX_X, ALU.max, negate=True))
                    UA.wait(dve, u, "e")
                    gstep(UV, nc.vector.reciprocal(wrow[:, b:b + 1], rsum[:, b:b + 1]))
                    UV.wait(dve, u, "r")
                    gate = nsa_gate[:, t, 3 * (g * NM + m) + 1 + kind:3 * (g * NM + m) + 2 + kind]
                    gstep(UV, nc.vector.tensor_tensor(wrow[:, b:b + 1], wrow[:, b:b + 1], gate, ALU.mult))
                    UP.wait(dve, u, "o")
                    UV.wait(dve, u, "w")
                    o = oacc[:, m, g]
                    gstep(UV, nc.vector.scalar_tensor_tensor(out=o, in0=PS[:, 6 + b, 0:ND], scalar=wrow[:, b:b + 1], in1=o,
                                                             op0=ALU.mult, op1=ALU.add))
                    UV.wait(dve, u, "o")

        def act_split_y(act, b):
            for k in range(4):
                split_y(act, k, yT[:, k])

        def dve_split_y(dve, b):
            for k in range(4):
                dve.wait_ge(y_hi_ok, 4 * b + k + 1)
                nc.vector.tensor_tensor(y_lo[:, k], yT[:, k], y_hi[:, k].bitcast(F32),
                                        ALU.subtract).then_inc(y_lo_ok, 1)

        sqT = [at(f"sqT{i}", 136 + 4 * i, [T]) for i in range(2)]
        skT = [at(f"skT{i}", 144 + 4 * i, [T]) for i in range(2)]
        svT = at("svT", 152, [T])
        sv_tok = [at(f"sv_tok{i}", 156 + 4 * i, [TB, P]) for i in range(2)]
        sp_ = [at(f"sp_{i}", 164 + 4 * i, [T]) for i in range(2)]
        cum = at("cum", 172, [T + 8])
        spT = at("spT", 177, [TB, P])
        otok = [at(f"otok{i}", 181 + 4 * i, [TB, P]) for i in range(2)]
        ntot = scal(1086, 2)
        sb_in, cum0, sv_tr, sv_ok, oy_tr = (sem(n) for n in ("sb_in", "cum0", "sv_tr", "sv_ok", "oy_tr"))
        oy_ok = sem("oy_ok")
        BP = Steps(sem("sb_pe"), ["z", "t", "o"])
        BA = Steps(sem("sb_act"), ["e", "l", "x", "pt"])
        BV = Steps(sem("sb_dve"), ["c", "sp", "m", "cum", "tot", "add", "neg", "o"])
        BU = 2 * TB
        smul, sneg = consts[:, 0:P], consts[:, P:2 * P]
        ZMAX = 40.0

        def sb_unit(u):
            m, r = divmod(u, BU)
            t, a = divmod(r, 2)
            return m, t, a, t + 1

        def sp_sb(sp):
            sp.dma_start(consts[:, 0:2 * P], A["c_sb"]).then_inc(sb_in, 16)
            load_pieces(sp, P_SB, P_SB + 12)

        def pool_sb(pool):
            split_pieces(pool, P_SB, P_SB + 12)

        def pe_sb(pe):
            for m in range(4):
                for j in range(3):
                    run_job(pe, P_SB + 3 * m + j)
                q = P_SB + 3 * m + 2
                pe.wait_ge(tile_evac[q % 2], q // 2 + 1)
                if m:
                    pe.wait_ge(oy_ok, m)
                for t in range(TB):
                    last = nc.tensor.transpose(pair(3)[:, t * P:(t + 1) * P], svT[:, t * P:(t + 1) * P], ident[:])
                last.then_inc(sv_tr, 1)
                pe.wait_ge(sv_ok, m + 1)
                for u in range(m * BU, (m + 1) * BU):
                    _, t, a, n = sb_unit(u)
                    r = slice(SD * a, SD * a + SD)
                    if u >= 2:
                        BV.wait(pe, u - 2, "add")
                    for c in range(0, n * P, 512):
                        w = min(512, n * P - c)
                        last = nc.tensor.matmul(pair(u % 2)[:, c:c + w], sqT[m % 2][r, t * P:(t + 1) * P],
                                                skT[m % 2][r, c:c + w], start=True, stop=True)
                    gstep(BP, last)
                    BA.wait(pe, u, "x")
                    if u:
                        BA.wait(pe, u - 1, "pt")
                    for k in range(n):
                        last = nc.tensor.transpose(pair(2)[:, k * P:(k + 1) * P], sp_[u % 2][:, k * P:(k + 1) * P], ident[:])
                    gstep(BP, last)
                    BA.wait(pe, u, "pt")
                    if u >= 2:
                        BV.wait(pe, u - 2, "o")
                    for k in range(n):
                        last = nc.tensor.matmul(PS[:, 6 + u % 2, 0:SD], spT[:, k], sv_tok[m % 2][:, k, r],
                                                start=(k == 0), stop=(k == n - 1))
                    gstep(BP, last)
                BV.wait(pe, (m + 1) * BU - 1, "o")
                for t in range(TB):
                    last = nc.tensor.transpose(pair(3)[:, t * P:(t + 1) * P], otok[m % 2][:, t], ident[:])
                last.then_inc(oy_tr, 1)

        def act_sb(act):
            for m in range(4):
                for j, dst in enumerate((sqT[m % 2], skT[m % 2], svT)):
                    p = P_SB + 3 * m + j
                    act.wait_ge(tile_done, p + 1)
                    evac_done(nc.scalar.activation(dst[:], pair(p % 2), ACT.Copy,
                                                   scale=float(SD) ** -0.5 if j == 0 else 1.0), p)
                for u in range(m * BU, (m + 1) * BU):
                    n = sb_unit(u)[3]
                    b = u % 2
                    s = sp_[b][:, 0:n * P]
                    BV.wait(act, u, "c")
                    gstep(BA, nc.scalar.activation(s, s, ACT.Exp))
                    BA.wait(act, u, "e")
                    gstep(BA, nc.scalar.activation(s, s, ACT.Ln, bias=1.0))
                    BV.wait(act, u, "neg")
                    gstep(BA, nc.scalar.activation(s, s, ACT.Exp, bias=ntot[:, b:b + 1]))
                    BP.wait(act, u, "t")
                    if u:
                        BP.wait(act, u - 1, "o")
                    gstep(BA, nc.scalar.activation(spT[:, 0:n].rearrange("p k n -> p (k n)"), pair(2)[:, 0:n * P], ACT.Copy))
                act.wait_ge(oy_tr, m + 1)
                nc.scalar.activation(yT[:, m], pair(3), ACT.Copy).then_inc(oy_ok, 1)

        def dve_sb(dve):
            tt = nc.vector.tensor_tensor
            nc.vector.memset(cum[:, 0:1], 0.0).then_inc(cum0, 1)
            dve.wait_ge(sb_in, 16)
            for m in range(4):
                dve.wait_ge(sv_tr, m + 1)
                nc.vector.tensor_copy(sv_tok[m % 2][:].rearrange("p t n -> p (t n)"), pair(3)).then_inc(sv_ok, 1)
                for u in range(m * BU, (m + 1) * BU):
                    _, t, a, n = sb_unit(u)
                    b = u % 2
                    w = n * P
                    s, z, diag = sp_[b][:, 0:w], pair(b)[:, 0:w], sp_[b][:, w - P:w]
                    BP.wait(dve, u, "z")
                    if u >= 2:
                        BP.wait(dve, u - 2, "t")
                    gstep(BV, nc.vector.tensor_scalar(s, z, ZMAX, None, ALU.min))
                    BA.wait(dve, u, "l")
                    gstep(BV, tt(s, z, s, ALU.max))
                    BV.wait(dve, u, "sp")
                    gstep(BV, tt(diag, diag, smul, ALU.mult))
                    BV.wait(dve, u, "m")
                    gstep(BV, nc.vector.tensor_tensor_scan(cum[:, 1:w + 1], s, s, 0.0, ALU.add, ALU.max))
                    BV.wait(dve, u, "cum")
                    gstep(BV, nc.vector.tensor_scalar(ntot[:, b:b + 1], cum[:, w:w + 1], -1.0, None, ALU.mult))
                    gstep(BV, tt(s, z, cum[:, 0:w], ALU.add))
                    BV.wait(dve, u, "add")
                    gstep(BV, tt(diag, diag, sneg, ALU.add))
                    BP.wait(dve, u, "o")
                    gstep(BV, nc.vector.tensor_copy(otok[m % 2][:, t, SD * a:SD * a + SD], PS[:, 6 + b, 0:SD]))

        YT = at("YT", 120, [KT, T])
        xb = [at(f"xb{i}", 152 + 4 * i, [D]) for i in range(2)]
        nrm = [at(f"nrm{i}", 160 + 4 * i, [D]) for i in range(2)]
        x1 = [at(f"x1_{i}", 168 + 4 * i, [D]) for i in range(2)]
        g_post, g_ff = at("g_post", 176, [D]), at("g_ff", 180, [D])
        junk = at("junk", 184, [D])
        x1_dram = nc.dram_tensor("x1_scratch", (T, D), F32).ap().rearrange("(t p) d -> t p d", p=P)
        mt_hi, mt_lo, gains_in = sem("mt_hi"), sem("mt_lo"), sem("gains_in")
        xb_in = [sem("xb_in0"), sem("xb_in1")]
        x1_out = [sem("x1_out0"), sem("x1_out1")]

        def act_split_m(act):
            for k in range(KT):
                nc.scalar.activation(hT_hi[:, k], mT[:, k], ACT.Copy).then_inc(mt_hi, 1)

        def dve_split_m(dve):
            for k in range(KT):
                dve.wait_ge(mt_hi, k + 1)
                nc.vector.tensor_tensor(hT_lo[:, k], mT[:, k], hT_hi[:, k].bitcast(F32), ALU.subtract).then_inc(mt_lo, 1)

        def sp_wout(sp):
            load_pieces(sp, P_OUT, P_OUT + KT)

        def pool_wout(pool):
            split_pieces(pool, P_OUT, P_OUT + KT)

        def pe_wout(pe):
            for c in range(KT):
                run_job(pe, P_OUT + c)

        def act_wout(act):
            for c in range(KT):
                p = P_OUT + c
                act.wait_ge(tile_done, p + 1)
                evac_done(nc.scalar.activation(YT[:, c], pair(p % 2), ACT.Copy), p)

        NP = Steps(sem("res_pe"), ["y", "h"])
        NA = Steps(sem("res_act"), ["ss", "rt", "ss1", "rt1", "hi"])
        NV = Steps(sem("res_dve"), ["r", "n", "x1", "r1", "h", "lo"])
        sq1 = scal(0, 4)

        def sp_res(sp):
            sp.dma_start(g_post[:], bc(A["g_mix_post"][0], D)).then_inc(gains_in, 16)
            sp.dma_start(g_ff[:], bc(A["g_ff_pre"][0], D)).then_inc(gains_in, 16)
            for t in range(TB + 1):
                if t < TB:
                    if t >= 2:
                        NV.wait(sp, t - 2, "x1")
                    sp.dma_start(xb[t % 2][:], x_v[t]).then_inc(xb_in[t % 2], 16)
                if t >= 1:
                    NV.wait(sp, t - 1, "x1")
                    sp.dma_start(x1_dram[t - 1], x1[(t - 1) % 2][:]).then_inc(x1_out[(t - 1) % 2], 16)
            for i in range(2):
                sp.wait_ge(x1_out[i], 16 * TB // 2)

        def pe_res(pe):
            for t in range(TB):
                if t >= 2:
                    NV.wait(pe, t - 2, "n")
                for k in range(KT):
                    last = nc.tensor.transpose(pair(t % 2)[:, k * P:(k + 1) * P], YT[:, k, t * P:(t + 1) * P], ident[:])
                gstep(NP, last)
                NV.wait(pe, t, "h")
                if t >= 2:
                    NV.wait(pe, t - 2, "lo")
                for k in range(KT):
                    last = nc.tensor.transpose(pair(2 + t % 2)[:, k * P:(k + 1) * P], nrm[t % 2][:, k * P:(k + 1) * P], ident[:])
                gstep(NP, last)

        def act_res(act):
            for t in range(TB):
                b = t % 2
                NP.wait(act, t, "y")
                if t:
                    NA.wait(act, t - 1, "hi")
                gstep(NA, nc.scalar.activation(junk[:], pair(b), ACT.Square, accum_out=sq1[:, 0:1]))
                NA.wait(act, t, "ss")
                gstep(NA, nc.scalar.activation(sq1[:, 1:2], sq1[:, 0:1], ACT.Sqrt, scale=1.0 / D, bias=eps_t))
                NV.wait(act, t, "x1")
                gstep(NA, nc.scalar.activation(junk[:], x1[b][:], ACT.Square, accum_out=sq1[:, 2:3]))
                NA.wait(act, t, "ss1")
                gstep(NA, nc.scalar.activation(sq1[:, 3:4], sq1[:, 2:3], ACT.Sqrt, scale=1.0 / D, bias=eps_t))
                NP.wait(act, t, "h")
                gstep(NA, nc.scalar.activation(hT_hi[:, :, t * P:(t + 1) * P],
                                               pair(2 + b).rearrange("p (k n) -> p k n", n=P), ACT.Copy))

        def dve_res(dve):
            dve.wait_ge(gains_in, 32)
            for t in range(TB):
                b = t % 2
                NA.wait(dve, t, "rt")
                gstep(NV, nc.vector.reciprocal(sq1[:, 1:2], sq1[:, 1:2]))
                NV.wait(dve, t, "r")
                if t >= 2:
                    NP.wait(dve, t - 2, "h")
                gstep(NV, nc.vector.scalar_tensor_tensor(out=nrm[b][:], in0=pair(b), scalar=sq1[:, 1:2], in1=g_post[:],
                                                         op0=ALU.mult, op1=ALU.mult))
                NV.wait(dve, t, "n")
                dve.wait_ge(xb_in[b], 16 * (t // 2 + 1))
                if t >= 2:
                    dve.wait_ge(x1_out[b], 16 * (t // 2))
                gstep(NV, nc.vector.tensor_tensor(x1[b][:], xb[b][:], nrm[b][:], ALU.add))
                NA.wait(dve, t, "rt1")
                gstep(NV, nc.vector.reciprocal(sq1[:, 3:4], sq1[:, 3:4]))
                NV.wait(dve, t, "r1")
                gstep(NV, nc.vector.scalar_tensor_tensor(out=nrm[b][:], in0=x1[b][:], scalar=sq1[:, 3:4], in1=g_ff[:],
                                                         op0=ALU.mult, op1=ALU.mult))
                NA.wait(dve, t, "hi")
                s = slice(t * P, (t + 1) * P)
                gstep(NV, nc.vector.tensor_tensor(hT_lo[:, :, s], pair(2 + b).rearrange("p (k n) -> p k n", n=P),
                                                  hT_hi[:, :, s].bitcast(F32), ALU.subtract))

        aT_hi, aT_lo = at("aT_hi", 88, [KT, T], F32R), at("aT_lo", 120, [KT, T], F32R)
        FT = at("FT", 152, [KT, T])
        relu = [at(f"relu{i}", 184 + 4 * i, [T]) for i in range(2)]
        r_ok, s_ok, a_hi_ok, a_lo_ok, ft_zero = (sem(n) for n in ("relu_ok", "square_ok", "a_hi_ok", "a_lo_ok", "ft_zero"))
        JOBS = 2 * KT
        PM = P_MLP
        L0 = [loaded[0], loaded[1]]

        def pc(i, j):
            return i * JOBS + (PM + j)

        zero1 = small[:, 1150:1151]

        def sp_mlp(sp):
            with sp.Fori(0, CH) as i:
                for j in range(JOBS):
                    b = (PM + j) % 2
                    sp.wait_ge(w_split, pc(i, j) - 1)
                    src = w1_v[i * KT + j] if j < KT else w2_v[i, j - KT]
                    sp.dma_start(w_raw[b][:], src).then_inc(w_loaded[b], 16)

        def pool_mlp(pool):
            with pool.Fori(0, CH) as i:
                for j in range(JOBS):
                    b = (PM + j) % 2
                    pool.wait_ge(w_loaded[b], i * (8 * JOBS) + (L0[b] + 16 * (j // 2 + 1)))
                    pool.wait_ge(tile_done, pc(i, j) - 1)
                    nc.gpsimd.tensor_tensor(w_hi[b][:], w_raw[b][:], zero1.unsqueeze(2).to_broadcast([P, KT, P]),
                                            ALU.add).then_inc(w_high, 1)
                    pool.wait_ge(w_high, pc(i, j) + 1)
                    nc.gpsimd.tensor_tensor(w_lo[b][:], w_raw[b][:], w_hi[b][:].bitcast(F32),
                                            ALU.subtract).then_inc(w_split, 1)

        def evacs(i, j):
            return i * (JOBS // 2) + (PM + j) // 2

        def pe_mlp(pe):
            with pe.Fori(0, CH) as i:
                for j in range(JOBS):
                    b = (PM + j) % 2
                    pe.wait_ge(w_split, pc(i, j) + 1)
                    pe.wait_ge(tile_evac[b], evacs(i, j))
                    if j == KT:
                        pe.wait_ge(a_lo_ok, i * KT + (KT + 2))
                    job(pe, None, *((hT_hi, hT_lo) if j < KT else (aT_hi, aT_lo)), par=b)

        def act_mlp(act):
            with act.Fori(0, CH) as i:
                for j in range(KT):
                    b = (PM + j) % 2
                    act.wait_ge(tile_done, pc(i, j) + 1)
                    act.wait_ge(a_lo_ok, i * KT + j + 1)
                    nc.scalar.activation(relu[j % 2][:], pair(b), ACT.Relu).then_inc(tile_evac[b], 1)
                    act.wait_ge(s_ok, i * KT + j + 1)
                    nc.scalar.activation(aT_hi[:, j], relu[j % 2][:], ACT.Copy).then_inc(a_hi_ok, 1)

        def dve_mlp(dve):
            nc.vector.memset(FT[:], 0.0).then_inc(ft_zero, 1)
            for b in range(2):
                nc.vector.memset(relu[b][:, 0:1], 0.0).then_inc(a_lo_ok, 1)
            dve.wait_ge(ft_zero, 1)
            with dve.Fori(0, CH) as i:
                for j in range(KT):
                    b = (PM + j) % 2
                    r = relu[j % 2]
                    dve.wait_ge(tile_evac[b], evacs(i, j) + 1)
                    nc.vector.tensor_tensor(r[:], r[:], r[:], ALU.mult).then_inc(s_ok, 1)
                    dve.wait_ge(s_ok, i * KT + j + 1)
                    dve.wait_ge(a_hi_ok, i * KT + j + 1)
                    nc.vector.tensor_tensor(aT_lo[:, j], r[:], aT_hi[:, j].bitcast(F32), ALU.subtract).then_inc(a_lo_ok, 1)
                for j in range(KT, JOBS):
                    b = (PM + j) % 2
                    dve.wait_ge(tile_done, pc(i, j) + 1)
                    nc.vector.tensor_tensor(FT[:, j - KT], FT[:, j - KT], pair(b), ALU.add).then_inc(tile_evac[b], 1)
                dve.wait_ge(tile_evac[(PM + JOBS - 1) % 2], evacs(i, JOBS - 1) + 1)

        xf = [at(f"xf{i}", 88 + 4 * i, [D]) for i in range(2)]
        fn = [at(f"fn{i}", 96 + 4 * i, [D]) for i in range(2)]
        of = [at(f"of{i}", 104 + 4 * i, [D]) for i in range(2)]
        g_last, junkf = at("g_last", 112, [D]), at("junkf", 116, [D])
        out_v = out[0].rearrange("(t p) d -> t p d", p=P)
        gl_in = sem("gl_in")
        xf_in = [sem("xf_in0"), sem("xf_in1")]
        of_out = [sem("of_out0"), sem("of_out1")]
        FP = Steps(sem("fin_pe"), ["y"])
        FA = Steps(sem("fin_act"), ["ss", "rt"])
        FV = Steps(sem("fin_dve"), ["r", "n", "o"])

        def sp_fin(sp):
            sp.dma_start(g_last[:], bc(A["g_ff_post"][0], D)).then_inc(gl_in, 16)
            for t in range(TB + 1):
                if t < TB:
                    if t >= 2:
                        FV.wait(sp, t - 2, "o")
                    sp.dma_start(xf[t % 2][:], x1_dram[t]).then_inc(xf_in[t % 2], 16)
                if t >= 1:
                    FV.wait(sp, t - 1, "o")
                    sp.dma_start(out_v[t - 1], of[(t - 1) % 2][:]).then_inc(of_out[(t - 1) % 2], 16)
            for i in range(2):
                sp.wait_ge(of_out[i], 16 * TB // 2)

        def pe_fin(pe):
            for t in range(TB):
                if t >= 2:
                    FV.wait(pe, t - 2, "n")
                for k in range(KT):
                    last = nc.tensor.transpose(pair(t % 2)[:, k * P:(k + 1) * P], FT[:, k, t * P:(t + 1) * P], ident[:])
                gstep(FP, last)

        def act_fin(act):
            for t in range(TB):
                b = t % 2
                FP.wait(act, t, "y")
                if t >= 2:
                    FV.wait(act, t - 2, "n")
                if t:
                    FA.wait(act, t - 1, "rt")
                gstep(FA, nc.scalar.activation(junkf[:], pair(b), ACT.Square, accum_out=sq1[:, b:b + 1]))
                FA.wait(act, t, "ss")
                gstep(FA, nc.scalar.activation(sq1[:, 2 + b:3 + b], sq1[:, b:b + 1], ACT.Sqrt, scale=1.0 / D, bias=eps_t))

        def dve_fin(dve):
            dve.wait_ge(gl_in, 16)
            for t in range(TB):
                b = t % 2
                FA.wait(dve, t, "rt")
                gstep(FV, nc.vector.reciprocal(sq1[:, 2 + b:3 + b], sq1[:, 2 + b:3 + b]))
                FV.wait(dve, t, "r")
                gstep(FV, nc.vector.scalar_tensor_tensor(out=fn[b][:], in0=pair(b), scalar=sq1[:, 2 + b:3 + b], in1=g_last[:],
                                                         op0=ALU.mult, op1=ALU.mult))
                FV.wait(dve, t, "n")
                dve.wait_ge(xf_in[b], 16 * (t // 2 + 1))
                if t >= 2:
                    dve.wait_ge(of_out[b], 16 * (t // 2))
                gstep(FV, nc.vector.tensor_tensor(of[b][:], xf[b][:], fn[b][:], ALU.add))

        block = ctx.enter_context(nc.Block())
        both = lambda f, g, b: lambda e: (f(e, b), g(e, b))
        progs = {
            "sync": [sp_phase0, sp_gdn, None, sp_gdn_out, lambda e: sp_merge(e, 0), sp_nsa, None, None,
                     lambda e: sp_merge(e, 1), sp_sb, None, lambda e: sp_merge(e, 2), None, sp_wout, sp_res, sp_mlp,
                     sp_fin],
            "gpsimd": [None, pool_gdn, None, pool_gdn_out, lambda e: pool_merge(e, 0), pool_nsa, pool_nsa_attn, None,
                       lambda e: pool_merge(e, 1), pool_sb, None, lambda e: pool_merge(e, 2), None, pool_wout, None,
                       pool_mlp, None],
            "scalar": [act_phase0, act_gdn, act_gdn_blocks, act_gdn_out, lambda e: act_merge(e, 0), act_nsa,
                       act_nsa_attn, lambda e: act_split_y(e, 1), lambda e: act_merge(e, 1), act_sb,
                       lambda e: act_split_y(e, 2), lambda e: act_merge(e, 2), act_split_m, act_wout, act_res,
                       act_mlp, act_fin],
            "vector": [dve_phase0, dve_gdn, dve_gdn_blocks, dve_gdn_out, lambda e: dve_merge(e, 0), dve_nsa,
                       dve_nsa_attn, lambda e: dve_split_y(e, 1), lambda e: dve_merge(e, 1), dve_sb,
                       lambda e: dve_split_y(e, 2), lambda e: dve_merge(e, 2), dve_split_m, None, dve_res, dve_mlp,
                       dve_fin],
            "tensor": [pe_phase0, pe_gdn, pe_gdn_blocks, pe_gdn_out, lambda e: pe_merge(e, 0), pe_nsa,
                       pe_nsa_attn, None, lambda e: pe_merge(e, 1), pe_sb, None, lambda e: pe_merge(e, 2), None,
                       pe_wout, pe_res, pe_mlp, pe_fin],
        }

        def run(eng, name):
            for f in progs[name]:
                if f:
                    f(eng)
                end_phase(eng, name)

        @block.sync
        def _(sp):
            run(sp, "sync")

        @block.gpsimd
        def _(pool):
            run(pool, "gpsimd")

        @block.scalar
        def _(act):
            run(act, "scalar")

        @block.vector
        def _(dve):
            run(dve, "vector")

        @block.tensor
        def _(pe):
            run(pe, "tensor")


_INS = ["x", "g_mix_pre", "g_mix_post", "g_ff_pre", "g_ff_post", "w_in", "gdn_conv_w", "gdn_a_log", "gdn_dt_bias",
        "gdn_norm_g", "nsa_cmp_wk", "nsa_cmp_pk", "nsa_cmp_wv", "nsa_cmp_pv", "w_br_gdn", "w_br_nsa", "w_br_sb",
        "w_out", "w_ff1", "w_ff2"]
_CONSTS = ["c_ident", "c_gdn", "c_nsa", "c_sb"]


def kernel(**inputs):
    import numpy as _np
    import concourse.bacc as _bacc
    from concourse import mybir as _mybir
    from concourse.bass_utils import run_bass_kernel_spmd as _run

    nc = _bacc.Bacc("TRN2", target_bir_lowering=False, num_devices=1)
    arrays, A = {}, {}
    for name in _INS:
        arrays[f"in_{name}"] = _np.ascontiguousarray(inputs[name])
    for name, table in zip(_CONSTS, shape_constants()):
        arrays[f"in_{name}"] = table
    for name in _INS + _CONSTS:
        a = arrays[f"in_{name}"]
        A[name] = nc.dram_tensor(f"in_{name}", a.shape, _mybir.dt.from_np(a.dtype), kind="ExternalInput").ap()
    out = nc.dram_tensor("out_0_dram", (1, T, D), _mybir.dt.float32, kind="ExternalOutput").ap()
    build(nc, A, out)
    r = _run(nc, [arrays], core_ids=[0])
    return r.results[0]["out_0_dram"]
```

```python
from contextlib import ExitStack

import numpy as np

import concourse.bass as bass
from concourse import mybir

F32 = mybir.dt.float32
F32R = mybir.dt.float32r
ALU = mybir.AluOpType
ACT = mybir.ActivationFunctionType
AX_X = mybir.AxisListType.X

P = 128
D = 1024
T = 1024
KT = D // P
TB = T // P
FF = 4 * D
SB0 = 16544
EPS = 1e-6
NEG = -1e30
PIECE = KT * P

GH, GD, GC = 4, 128, 64
NH, NG, ND = 8, 2, 64
NM = NH // NG
CL, CS = 32, 16
NCMP = (T - CL) // CS + 1
SL, TOPK = 64, 8
NSEL = T // SL
WIN = 512
WT = WIN // P + 1
SH, SD = 8, 64

SPLITS = [512, 512, 512, 512, 4, 4, 512, 768, 24, 512, 512, 512, 3072]
OFF = [sum(SPLITS[:i]) for i in range(len(SPLITS))]
(O_GQ, O_GK, O_GV, O_GZ, O_GA, O_GB, O_NQ, O_NKV, O_NGATE, O_SQ, O_SK, O_SV, O_MERGE) = OFF
N_IN = sum(SPLITS)


def shape_constants():
    i = np.arange(P)
    row, col = i[:, None], i[None, :]
    chunk = (row // GC) == (col // GC)
    f = lambda m: m.astype(np.float32)
    neg = lambda m: np.where(m, 0.0, NEG).astype(np.float32)
    gdn = [f(chunk & (row <= col)), neg(chunk & (row <= col)), f(chunk & (row < col))]
    for level in range(6):
        b = 1 << level
        gdn.append(f((row // b % 2 == 0) & (col // b == row // b + 1)))
    gdn += [f(chunk), np.ones((P, P), np.float32), f(row // GC == 0) * np.ones((1, P), np.float32),
            f(row // GC == 1) * np.ones((1, P), np.float32)]
    j = np.arange(NSEL)
    lower = f(j[None, :] < j[:, None]).reshape(1, -1) * np.ones((P, 1), np.float32)
    pos = np.arange(T).reshape(TB, P)
    start = np.arange(64) * CS
    valid = (start + CL - 1)[None, None, :] <= pos[:, :, None]
    valid = valid & (np.arange(64) < NCMP)
    valid = valid.transpose(1, 0, 2)
    cur = (pos // SL)[:, :, None]
    forced = (j == 0) | (j == cur) | (j == cur - 1)
    bias = np.where(j <= cur, 1e3 * forced, NEG).astype(np.float32).transpose(1, 0, 2)
    nsa = [neg(col <= row), neg(col > row), lower, neg(valid).reshape(P, -1), f(valid).reshape(P, -1),
           bias.reshape(P, -1)]
    sb = [neg(col < row)]
    cat = lambda x: np.ascontiguousarray(np.concatenate(x, 1))
    return np.eye(P, dtype=np.float32), cat(gdn), cat(nsa), cat(sb)


class Steps:

    def __init__(self, sem, names, base=0):
        self.sem, self.names, self.base = sem, names, base

    def done(self, i, name):
        return self.base + i * len(self.names) + self.names.index(name) + 1

    def wait(self, eng, i, name):
        eng.wait_ge(self.sem, self.done(i, name))


class Stages:

    def __init__(self, sem, prefix, names):
        self.sems = {n: sem(f"{prefix}_{n}") for n in names}

    def wait(self, eng, i, name):
        eng.wait_ge(self.sems[name], i + 1)

    def done(self, name, ins):
        ins.then_inc(self.sems[name], 1)


def build(nc, A, out):
    ctx = ExitStack()
    with ctx:
        def at(name, kb, shape, dt=F32):
            return nc.alloc_sbuf_tensor_at(name, [P] + list(shape), dt, offset=SB0 + int(kb * 1024))

        def sem(name):
            return ctx.enter_context(nc.semaphore(name))

        hT_hi = at("hT_hi", 0, [KT, T], F32R)
        hT_lo = at("hT_lo", 32, [KT, T], F32R)
        w_raw = [at(f"w_raw{i}", 64 + 4 * i, [KT, P]) for i in range(2)]
        w_hi = [at(f"w_hi{i}", 72 + 4 * i, [KT, P], F32R) for i in range(2)]
        w_lo = [at(f"w_lo{i}", 80 + 4 * i, [KT, P], F32R) for i in range(2)]
        mT = at("mT", 88, [KT, T])
        yT = at("yT", 120, [4, T])
        small = at("small", 194, [1152])
        ident = at("ident", 198.5, [P])
        consts = at("consts", 199, [1664])
        PS = ctx.enter_context(nc.psum_tensor("PS", [P, 8, 512], F32))

        def pair(k):
            return PS[:, 2 * k:2 * k + 2, :].rearrange("p a b -> p (a b)")

        w_loaded = [sem("w_loaded0"), sem("w_loaded1")]
        w_high = sem("w_high")
        w_split = sem("w_split")
        tile_done = sem("tile_done")
        tile_evac = [sem("tile_evac0"), sem("tile_evac1")]
        phase = sem("phase")
        consts_in = sem("consts_in")
        dve_step, act_step, pool_step = sem("dve_step"), sem("act_step"), sem("pool_step")

        counts = {"dve": 0, "act": 0, "phase": {}}

        def dstep(ins):
            counts["dve"] += 1
            ins.then_inc(dve_step, 1)
            nc.vector.wait_ge(dve_step, counts["dve"])

        def astep(ins):
            counts["act"] += 1
            ins.then_inc(act_step, 1)
            nc.scalar.wait_ge(act_step, counts["act"])

        def end_phase(eng, name):
            n = counts["phase"].get(name, 0) + 1
            counts["phase"][name] = n
            eng.drain().then_inc(phase, 1)
            eng.wait_ge(phase, 5 * n)

        w_in = A["w_in"][0].rearrange("(k p) n -> p k n", p=P)

        pieces = []
        def cols(o, n=P):
            return lambda dst, eng: eng.dma_start(dst[:, :, 0:n], w_in[:, :, o:o + n])
        for c in range(12):
            pieces.append((cols(O_GQ + c * P), KT))
        def gates_piece(dst, eng):
            eng.dma_start(dst[:, :, 0:2 * GH], w_in[:, :, O_GA:O_GA + 2 * GH]).then_inc(w_loaded[P_SMALL % 2], 16)
            return eng.dma_start(dst[:, :, 8:8 + 3 * NH], w_in[:, :, O_NGATE:O_NGATE + 3 * NH])
        P_SMALL = len(pieces)
        pieces.append((gates_piece, KT))
        P_GZ = len(pieces)
        for c in range(4):
            pieces.append((cols(O_GZ + c * P), KT))
        P_MERGE = [len(pieces)]
        def merge_pieces(b, name, rows=None):
            wb = A[name][0]
            for c in range(KT):
                pieces.append((cols(O_MERGE + b * D + c * P), KT))
                if rows is None:
                    v = wb.rearrange("(k p) n -> p k n", p=P)
                    pieces.append(((lambda v, c: lambda dst, eng: eng.dma_start(dst[:, 0:4, :], v[:, :, c * P:(c + 1) * P]))(v, c), 4))
                else:
                    def two(c):
                        par = len(pieces) % 2

                        def go(dst, eng):
                            v = wb.rearrange("(g m d) n -> g d m n", g=NG, m=NM)
                            eng.dma_start(dst[0:ND, 0:4, :], v[0, :, :, c * P:(c + 1) * P]).then_inc(w_loaded[par], 16)
                            return eng.dma_start(dst[ND:P, 0:4, :], v[1, :, :, c * P:(c + 1) * P])
                        return go
                    pieces.append((two(c), 4))
        merge_pieces(0, "w_br_gdn")
        P_NSA = len(pieces)
        nq_v = A["w_in"][0][:, O_NQ:O_NQ + 512].rearrange("(k p) (g m d) -> g m p k d", p=P, g=NG, m=NM)
        for c in range(6):
            pieces.append((cols(O_NKV + c * P), KT))
        def nq_piece(m):
            par = len(pieces) % 2

            def go(dst, eng):
                eng.dma_start(dst[:, :, 0:ND], nq_v[0, m]).then_inc(w_loaded[par], 16)
                return eng.dma_start(dst[:, :, ND:P], nq_v[1, m])
            return go
        for m in range(NM):
            pieces.append((nq_piece(m), KT))
        P_MERGE.append(len(pieces))
        merge_pieces(1, "w_br_nsa", rows=True)
        P_SB = len(pieces)
        for m in range(4):
            for o in (O_SQ, O_SK, O_SV):
                pieces.append((cols(o + m * P), KT))
        P_MERGE.append(len(pieces))
        merge_pieces(2, "w_br_sb")
        P_OUT = len(pieces)
        wo_v = A["w_out"][0].rearrange("(k p) n -> p k n", p=P)
        for c in range(KT):
            pieces.append(((lambda c: lambda dst, eng: eng.dma_start(dst[:], wo_v[:, :, c * P:(c + 1) * P]))(c), KT))
        P_MLP = len(pieces)
        two_dma = {P_SMALL} | {P_NSA + 6 + m for m in range(NM)} | {P_MERGE[1] + 2 * c + 1 for c in range(KT)}
        loaded_at = []
        loaded = [0, 0]
        for p in range(P_MLP):
            loaded[p % 2] += 32 if p in two_dma else 16
            loaded_at.append(loaded[p % 2])
        CH = FF // D
        w1_v = A["w_ff1"][0].rearrange("(k p) (f n) -> f p k n", p=P, n=P)
        w2_v = A["w_ff2"][0].rearrange("(i k p) (c n) -> i c p k n", k=KT, p=P, n=P)

        def load_pieces(sp, lo, hi):
            for p in range(lo, hi):
                if p >= 2:
                    sp.wait_ge(w_split, p - 1)
                pieces[p][0](w_raw[p % 2], sp).then_inc(w_loaded[p % 2], 16)

        def split_pieces(pool, lo, hi):
            for p in range(lo, hi):
                b, k = p % 2, pieces[p][1]
                pool.wait_ge(w_loaded[b], loaded_at[p])
                if p >= 2:
                    pool.wait_ge(tile_done, p - 1)
                nc.gpsimd.tensor_copy(w_hi[b][:, 0:k], w_raw[b][:, 0:k]).then_inc(w_high, 1)
                pool.wait_ge(w_high, p + 1)
                nc.gpsimd.tensor_tensor(w_lo[b][:, 0:k], w_raw[b][:, 0:k], w_hi[b][:, 0:k].bitcast(F32),
                                        ALU.subtract).then_inc(w_split, 1)

        def job(pe, p, rhs_hi, rhs_lo, ktiles=KT, par=None, waits=None):
            b = p % 2 if par is None else par
            dst = 2 * b
            last = None
            for k in range(ktiles):
                for w, r, first, end in ((w_hi, rhs_hi, True, False), (w_hi, rhs_lo, False, False),
                                         (w_lo, rhs_hi, False, True)):
                    for h in range(2):
                        last = nc.tensor.matmul(PS[:, dst + h, :], w[b][:, k, :], r[:, k, h * 512:(h + 1) * 512],
                                                start=(k == 0 and first), stop=(k == ktiles - 1 and end))
            last.then_inc(tile_done, 1)

        def run_job(pe, p, rhs_hi=None, rhs_lo=None):
            pe.wait_ge(w_split, p + 1)
            if p >= 2:
                pe.wait_ge(tile_evac[p % 2], p // 2)
            job(pe, p, hT_hi if rhs_hi is None else rhs_hi, hT_lo if rhs_lo is None else rhs_lo, pieces[p][1])

        def evac_done(ins, p):
            ins.then_inc(tile_evac[p % 2], 1)

        xin = [at(f"xin{i}", 136 + 4 * i, [D]) for i in range(2)]
        xs = [at(f"xs{i}", 144 + 4 * i, [D]) for i in range(2)]
        g_pre = at("g_pre", 152, [D])
        junk0 = at("junk0", 156, [D])
        ss0 = small[:, 0:TB]
        rt0 = small[:, TB:2 * TB]
        rr0 = small[:, 2 * TB:3 * TB]
        eps_t = small[:, 1151:1152]
        x_v = A["x"][0].rearrange("(t p) d -> t p d", p=P)
        x_in = [sem("x_in0"), sem("x_in1")]
        x_ss, x_norm, x_tr, x_hi, x_lo, eps_set = (sem(n) for n in (
            "x_ss", "x_norm", "x_tr", "x_hi", "x_lo", "eps_set"))

        def bc(ap, n):
            return ap.rearrange("(a n) -> a n", a=1).to_broadcast([P, n])

        def sp_phase0(sp):
            sp.dma_start(ident[:], A["c_ident"]).then_inc(consts_in, 16)
            sp.dma_start(g_pre[:], bc(A["g_mix_pre"][0], D)).then_inc(consts_in, 16)
            for t in range(TB):
                if t >= 2:
                    sp.wait_ge(x_norm, t - 1)
                sp.dma_start(xin[t % 2][:], x_v[t]).then_inc(x_in[t % 2], 16)

        def act_phase0(act):
            act.wait_ge(eps_set, 1)
            for t in range(TB):
                act.wait_ge(x_in[t % 2], 16 * (t // 2 + 1))
                astep(nc.scalar.activation(junk0[:], xin[t % 2][:], ACT.Square, accum_out=ss0[:, t:t + 1]))
                nc.scalar.activation(rt0[:, t:t + 1], ss0[:, t:t + 1], ACT.Sqrt, scale=1.0 / D,
                                     bias=eps_t).then_inc(x_ss, 1)
                if t >= 1:
                    act_split_x(act, t - 1)
            act_split_x(act, TB - 1)

        def act_split_x(act, t):
            act.wait_ge(x_tr, t + 1)
            nc.scalar.activation(hT_hi[:, :, t * P:(t + 1) * P],
                                 pair(t % 2).rearrange("p (k n) -> p k n", n=P), ACT.Copy).then_inc(x_hi, 1)

        def dve_phase0(dve):
            nc.vector.memset(eps_t, EPS).then_inc(eps_set, 1)
            nc.vector.memset(small[:, 1150:1151], 0.0)
            dve.wait_ge(consts_in, 32)
            for t in range(TB + 1):
                if t < TB:
                    dve.wait_ge(x_ss, t + 1)
                    dstep(nc.vector.reciprocal(rr0[:, t:t + 1], rt0[:, t:t + 1]))
                    if t >= 2:
                        dve.wait_ge(x_tr, t - 1)
                    nc.vector.scalar_tensor_tensor(out=xs[t % 2][:], in0=xin[t % 2][:], scalar=rr0[:, t:t + 1],
                                                   in1=g_pre[:], op0=ALU.mult, op1=ALU.mult).then_inc(x_norm, 1)
                if t >= 1:
                    dve_split_x(dve, t - 1)

        def dve_split_x(dve, t):
            dve.wait_ge(x_hi, t + 1)
            s = slice(t * P, (t + 1) * P)
            nc.vector.tensor_tensor(hT_lo[:, :, s], pair(t % 2).rearrange("p (k n) -> p k n", n=P),
                                    hT_hi[:, :, s].bitcast(F32), ALU.subtract).then_inc(x_lo, 1)

        def pe_phase0(pe):
            pe.wait_ge(consts_in, 32)
            for t in range(TB):
                pe.wait_ge(x_norm, t + 1)
                if t >= 2:
                    pe.wait_ge(x_lo, t - 1)
                for k in range(KT):
                    last = nc.tensor.transpose(PS[:, 2 * (t % 2) + k // 4, (k % 4) * P:(k % 4 + 1) * P],
                                               xs[t % 2][:, k * P:(k + 1) * P], ident[:])
                last.then_inc(x_tr, 1)

        cT = at("cT", 136, [12, T])
        xpad = [at(f"xpad{i}", 88 + 5 * i, [T + 3]) for i in range(2)]
        acc = [at(f"acc{i}", 98 + 4 * i, [T]) for i in range(2)]
        abT = at("abT", 106, [T])
        cw_in = at("cw_in", 110, [P])
        sq = [at(f"sq{i}", 111 + 4 * i, [T]) for i in range(2)]
        slot = lambda name, i, shape, n=1: at(name, 88 + 2 * i if i < 16 else 184 + 2 * (i - 16), shape)
        qn, kn, kb, kbg = (slot(n, i, [GH, P]) for i, n in enumerate(("qn", "kn", "kb", "kbg")))
        kd, vb = slot("kd", 4, [GH, P]), slot("vb", 5, [GH, P])
        qkb = slot("qkb", 6, [GH, 2, P])
        knT, DT, DsT, attnT, AT, X, Z = (slot(n, 8 + i, [GH, P]) for i, n in enumerate(
            ("knT", "DT", "DsT", "attnT", "AT", "X", "Z")))
        Y, U, uu = slot("Y", 0, [GH, P]), slot("U", 1, [GH, P]), slot("uu", 2, [GH, P])
        trig = slot("trig", 15, [GH, P])
        wq = slot("wq", 16, [GH, 2 * P])
        S, vnew, qS = slot("S", 18, [GH, P]), slot("vnew", 19, [GH, P]), slot("qS", 20, [GH, P])
        o_all = at("o_all", 120, [TB, GH, P])
        zT = at("zT", 136, [GH, T])
        y_hi, y_lo = at("y_hi", 152, [4, T], F32R), at("y_lo", 168, [4, T], F32R)
        ytmp = [at(f"ytmp{i}", 184 + 4 * i, [T]) for i in range(2)]
        osq = at("osq", 88, [TB, GH, P])

        def scal(o, n=TB * GH):
            return small[:, o:o + n]
        abn = scal(24, 256).rearrange("p (t c) -> p t c", c=32)
        s4 = lambda o: scal(o).rearrange("p (t h) -> p t h", h=GH)
        beta, graw, gcs, dgl, eg, ekd, rq, skb, skbg, skd, egl0, egl1, sp_a, sp_b, sp_c = (
            s4(280 + 32 * i) for i in range(15))
        rr = scal(760, 64).rearrange("p (t c) -> p t c", c=8)
        alog, dtb = scal(824, 4), scal(828, 4)
        normg = scal(832, 1)
        cw = scal(840, 48)
        nsa_gate = scal(888, 192).rearrange("p (t c) -> p t c", c=24)
        oss = s4(280)
        ort = s4(312)

        GI = {n: i * P for i, n in enumerate(("tri", "dneg", "strict", "l0", "l1", "l2", "l3", "l4", "l5",
                                              "chunk", "ones", "c0", "c1"))}
        gc = lambda n: consts[:, GI[n]:GI[n] + P]
        overh = lambda ap: ap.unsqueeze(1).to_broadcast([P, GH, P])
        overd = lambda ap: ap.unsqueeze(2).to_broadcast([P, GH, P])

        (g_small_in, cw_tr, cw_ok, pads_ok, conv_sum, conv_act, ab_tr, ab_tok) = (sem(n) for n in (
            "g_small_in", "cw_tr", "cw_ok", "pads_ok", "conv_sum", "conv_act", "ab_tr", "ab_tok"))
        gs_a, gs_d, gs_p, sq_ok, ss_ok = (sem(n) for n in ("gs_a", "gs_d", "gs_p", "sq_ok", "ss_ok"))

        def sp_gdn(sp):
            sp.dma_start(consts[:], A["c_gdn"]).then_inc(g_small_in, 16)
            sp.dma_start(cw_in[0:48, :], A["gdn_conv_w"][0].rearrange("i (c p) -> (i c) p", p=P)).then_inc(g_small_in, 16)
            sp.dma_start(alog, bc(A["gdn_a_log"][0], GH)).then_inc(g_small_in, 16)
            sp.dma_start(dtb, bc(A["gdn_dt_bias"][0], GH)).then_inc(g_small_in, 16)
            sp.dma_start(normg, A["gdn_norm_g"][0].rearrange("(p a) -> p a", a=1)).then_inc(g_small_in, 16)
            load_pieces(sp, 0, P_SMALL + 1)

        def pool_gdn(pool):
            split_pieces(pool, 0, P_SMALL + 1)

        def pe_gdn(pe):
            pe.wait_ge(g_small_in, 80)
            nc.tensor.transpose(PS[:, 4, 0:48], cw_in[0:48, :], ident[0:48, 0:48]).then_inc(cw_tr, 1)
            for p in range(P_SMALL + 1):
                run_job(pe, p)
            pe.wait_ge(tile_evac[P_SMALL % 2], P_SMALL // 2 + 1)
            pe.wait_ge(cw_ok, 1)
            for t in range(TB):
                last = nc.tensor.transpose(PS[:, 5, t * 32:t * 32 + 32], abT[0:32, t * P:(t + 1) * P],
                                           ident[0:32, 0:32])
            last.then_inc(ab_tr, 1)
            pe.wait_ge(gs_d, 3)
            for k, n in enumerate(("tri", "chunk", "c0", "c1")):
                last = nc.tensor.matmul(PS[:, 7, 32 * k:32 * k + 32], gc(n), scal(280 + 32), start=True, stop=True)
            last.then_inc(gs_p, 1)
            for c in range(8):
                pe.wait_ge(sq_ok, c + 1)
                for t in range(TB):
                    last = nc.tensor.matmul(PS[:, 6, t * 8 + c:t * 8 + c + 1], sq[c % 2][:, t * P:(t + 1) * P],
                                            gc("ones")[:, 0:1], start=True, stop=True)
                last.then_inc(ss_ok, 1)

        def act_gdn(act):
            for c in range(12 + 1):
                if c < 12:
                    act.wait_ge(tile_done, c + 1)
                    if c == 0:
                        act.wait_ge(pads_ok, 2)
                    if c >= 2:
                        act.wait_ge(conv_sum, c - 1)
                    evac_done(nc.scalar.activation(xpad[c % 2][:, 3:], pair(c % 2), ACT.Copy), c)
                if c >= 1:
                    act.wait_ge(conv_sum, c)
                    nc.scalar.activation(cT[:, c - 1], acc[(c - 1) % 2][:], ACT.Silu).then_inc(conv_act, 1)
            act.wait_ge(tile_done, P_SMALL + 1)
            evac_done(nc.scalar.activation(abT[0:32, :], pair(P_SMALL % 2)[0:32, :], ACT.Copy), P_SMALL)
            act.wait_ge(ab_tok, 1)
            astep(nc.scalar.activation(beta, abn[:, :, 4:8], ACT.Sigmoid))
            astep(nc.scalar.activation(nsa_gate, abn[:, :, 8:32], ACT.Sigmoid))
            act.wait_ge(gs_d, 1)
            astep(nc.scalar.activation(sp_b, sp_a, ACT.Abs))
            astep(nc.scalar.activation(sp_b, sp_b, ACT.Exp, scale=-1.0))
            astep(nc.scalar.activation(sp_b, sp_b, ACT.Ln, bias=1.0))
            nc.scalar.activation(alog, alog, ACT.Exp).then_inc(gs_a, 1)
            act.wait_ge(gs_p, 1)
            psg = lambda k: PS[:, 7, 32 * k:32 * k + 32].rearrange("p (t h) -> p t h", h=GH)
            nc.scalar.activation(eg, psg(0), ACT.Exp)
            nc.scalar.activation(egl0, psg(2), ACT.Exp)
            nc.scalar.activation(egl1, psg(3), ACT.Exp).then_inc(gs_a, 1)
            act.wait_ge(gs_d, 5)
            nc.scalar.activation(ekd, dgl, ACT.Exp).then_inc(gs_a, 1)
            for c in range(8):
                act.wait_ge(conv_act, c + 1)
                if c >= 2:
                    act.wait_ge(ss_ok, c - 1)
                nc.scalar.activation(sq[c % 2][:], cT[:, c], ACT.Square).then_inc(sq_ok, 1)
            act.wait_ge(ss_ok, 8)
            nc.scalar.activation(scal(760, 64), PS[:, 6, 0:64], ACT.Sqrt, bias=eps_t).then_inc(gs_a, 1)

        def dve_gdn(dve):
            nc.vector.memset(xpad[0][:, 0:3], 0.0).then_inc(pads_ok, 1)
            nc.vector.memset(xpad[1][:, 0:3], 0.0).then_inc(pads_ok, 1)
            dve.wait_ge(cw_tr, 1)
            nc.vector.tensor_copy(cw, PS[:, 4, 0:48]).then_inc(cw_ok, 1)
            dve.wait_ge(cw_ok, 1)
            for c in range(12):
                x, a = xpad[c % 2], acc[c % 2]
                dve.wait_ge(tile_evac[c % 2], c // 2 + 1)
                if c >= 2:
                    dve.wait_ge(conv_act, c - 1)
                w = lambda i: cw[:, i * 12 + c:i * 12 + c + 1]
                dstep(nc.vector.tensor_scalar(a[:], x[:, 3:T + 3], w(3), None, ALU.mult))
                for i in (2, 1):
                    dstep(nc.vector.scalar_tensor_tensor(out=a[:], in0=x[:, i:T + i], scalar=w(i), in1=a[:],
                                                         op0=ALU.mult, op1=ALU.add))
                nc.vector.scalar_tensor_tensor(out=a[:], in0=x[:, 0:T], scalar=w(0), in1=a[:],
                                               op0=ALU.mult, op1=ALU.add).then_inc(conv_sum, 1)
            dve.wait_ge(ab_tr, 1)
            nc.vector.tensor_copy(scal(24, 256), PS[:, 5, 0:256]).then_inc(ab_tok, 1)
            dve.wait_ge(ab_tok, 1)
            b8 = lambda ap: ap.unsqueeze(1).to_broadcast([P, TB, GH])
            dve.wait_ge(g_small_in, 80)
            nc.vector.tensor_tensor(sp_a, abn[:, :, 0:4], b8(dtb), ALU.add).then_inc(gs_d, 1)
            dve.wait_ge(gs_a, 1)
            dve.wait_ge(gs_d, 1)
            nc.vector.scalar_tensor_tensor(out=sp_c, in0=sp_a, scalar=0.0, in1=sp_b, op0=ALU.max,
                                           op1=ALU.add).then_inc(gs_d, 1)
            dve.wait_ge(gs_d, 2)
            nc.vector.scalar_tensor_tensor(out=graw, in0=sp_c, scalar=-1.0, in1=b8(alog), op0=ALU.mult,
                                           op1=ALU.mult).then_inc(gs_d, 1)
            dve.wait_ge(gs_p, 1)
            dve.wait_ge(gs_a, 2)
            psg = lambda k: PS[:, 7, 32 * k:32 * k + 32].rearrange("p (t h) -> p t h", h=GH)
            nc.vector.tensor_copy(gcs, psg(0)).then_inc(gs_d, 1)
            dve.wait_ge(gs_d, 4)
            nc.vector.tensor_tensor(dgl, psg(1), gcs, ALU.subtract).then_inc(gs_d, 1)
            dve.wait_ge(gs_a, 4)
            dstep(nc.vector.reciprocal(scal(760, 64), scal(760, 64)))
            dstep(nc.vector.tensor_scalar(rq, rr[:, :, 0:4], float(GD) ** -0.5, None, ALU.mult))
            dstep(nc.vector.tensor_tensor(skb, rr[:, :, 4:8], beta, ALU.mult))
            dstep(nc.vector.tensor_tensor(skbg, skb, eg, ALU.mult))
            dstep(nc.vector.tensor_tensor(skd, rr[:, :, 4:8], ekd, ALU.mult))

        LV = range(1, 6)
        GP = Steps(sem("gdn_pe"), ["tok", "tr", "gram", "xz"] + [f"{n}{l}" for l in LV for n in ("y", "z")] +
                   ["uw", "ws0", "st0", "ws1", "st1", "oi"])
        GA = Steps(sem("gdn_act"), ["trs", "exp", "x"] + [f"y{l}" for l in LV] + ["wq", "qs0", "qs1"])
        GV = Steps(sem("gdn_dve"), ["scaled", "trig", "dm", "dg", "ds", "attn", "at", "u0", "z0"] +
                   [f"{n}{l}" for l in LV for n in ("u", "x", "z")] +
                   ["u", "v0", "sd0", "s0", "v1", "sd1", "s1", "qe", "o"])

        def gstep(steps, ins):
            ins.then_inc(steps.sem, 1)

        def bank4(k):
            return PS[:, k, :].rearrange("p (h n) -> p h n", h=GH)

        def pe_gdn_blocks(pe):
            for t in range(TB):
                s = slice(t * P, (t + 1) * P)
                if t:
                    GV.wait(pe, t - 1, "o")
                for j in range(3):
                    for h in range(GH):
                        last = nc.tensor.transpose(bank4(j)[:, h], cT[:, 4 * j + h, s], ident[:])
                gstep(GP, last)
                GV.wait(pe, t, "scaled")
                for j, src in enumerate((qn, kn, kb)):
                    for h in range(GH):
                        last = nc.tensor.transpose(bank4(3 + j)[:, h], src[:, h], ident[:])
                gstep(GP, last)
                GV.wait(pe, t, "trig")
                nc.tensor.matmul(PS[:, 0, :], gc("ones"), trig[:].rearrange("p h n -> p (h n)"), start=True, stop=True)
                GA.wait(pe, t, "trs")
                for h in range(GH):
                    last = nc.tensor.matmul(PS[:, 6 + h // 2, (h % 2) * 256:(h % 2) * 256 + 256], knT[:, h],
                                            qkb[:, h].rearrange("p a n -> p (a n)"), start=True, stop=True)
                gstep(GP, last)
                GV.wait(pe, t, "z0")
                for h in range(GH):
                    last = nc.tensor.transpose(bank4(1)[:, h], Z[:, h], ident[:])
                gstep(GP, last)
                for l in LV:
                    GV.wait(pe, t, f"u{l}")
                    if l > 1:
                        GV.wait(pe, t, f"z{l - 1}")
                    else:
                        GA.wait(pe, t, "x")
                    for h in range(GH):
                        last = nc.tensor.matmul(bank4(2)[:, h], U[:, h], X[:, h], start=True, stop=True)
                    gstep(GP, last)
                    GA.wait(pe, t, f"y{l}")
                    for h in range(GH):
                        nc.tensor.matmul(bank4(3)[:, h], Z[:, h], Y[:, h], start=True, stop=True)
                    for h in range(GH):
                        last = nc.tensor.matmul(bank4(4)[:, h], Y[:, h], Z[:, h], start=True, stop=True)
                    gstep(GP, last)
                GV.wait(pe, t, "z5")
                for h in range(GH):
                    nc.tensor.matmul(bank4(5)[:, h], Z[:, h], vb[:, h], start=True, stop=True)
                for h in range(GH):
                    last = nc.tensor.matmul(bank4(0)[:, h], kbg[:, h], Z[:, h], start=True, stop=True)
                gstep(GP, last)
                for c in range(2):
                    r = slice(GC * c, GC * c + GC)
                    GA.wait(pe, t, "wq" if c == 0 else "qs0")
                    GV.wait(pe, t, "u" if c == 0 else "s0")
                    for h in range(GH):
                        last = nc.tensor.matmul(bank4(6)[:, h], wq[:, h, c * P:(c + 1) * P], S[:, h], start=True, stop=True)
                    gstep(GP, last)
                    GV.wait(pe, t, f"v{c}")
                    for h in range(GH):
                        last = nc.tensor.matmul(bank4(7)[:, h], kd[r, h], vnew[r, h], start=True, stop=True)
                    gstep(GP, last)
                for h in range(GH):
                    last = nc.tensor.matmul(bank4(1)[:, h], attnT[:, h], vnew[:, h], start=True, stop=True)
                gstep(GP, last)

        def act_gdn_blocks(act):
            for t in range(TB):
                GP.wait(act, t, "tr")
                nc.scalar.activation(qkb[:, :, 0, :], bank4(3), ACT.Copy)
                nc.scalar.activation(qkb[:, :, 1, :], bank4(5), ACT.Copy)
                gstep(GA, nc.scalar.activation(knT[:], bank4(4), ACT.Copy))
                GV.wait(act, t, "dg")
                gstep(GA, nc.scalar.activation(DT[:], DT[:], ACT.Exp))
                GP.wait(act, t, "xz")
                gstep(GA, nc.scalar.activation(X[:], bank4(1), ACT.Copy))
                for l in LV:
                    GP.wait(act, t, f"y{l}")
                    gstep(GA, nc.scalar.activation(Y[:], bank4(2), ACT.Copy))
                GP.wait(act, t, "uw")
                nc.scalar.activation(wq[:, :, 0:64], bank4(0)[:, :, 0:64], ACT.Copy)
                nc.scalar.activation(wq[:, :, 192:256], bank4(0)[:, :, 64:128], ACT.Copy)
                gstep(GA, nc.scalar.activation(wq[:, :, 64:192], qkb[:, :, 0, :], ACT.Copy))
                for c in range(2):
                    GP.wait(act, t, f"ws{c}")
                    GV.wait(act, t, f"v{c}")
                    gstep(GA, nc.scalar.activation(qS[GC * c:GC * c + GC], bank4(6)[GC * (1 - c):GC * (1 - c) + GC],
                                                   ACT.Copy))

        def dve_gdn_blocks(dve):
            tt = nc.vector.tensor_tensor
            dstep(nc.vector.memset(S[:], 0.0))
            for t in range(TB):
                if t:
                    GV.wait(dve, t - 1, "o")
                GP.wait(dve, t, "tok")
                rk = rr[:, t, 4:8]
                tt(qn[:], bank4(0), overd(rq[:, t]), ALU.mult)
                tt(kn[:], bank4(1), overd(rk), ALU.mult)
                tt(kb[:], bank4(1), overd(skb[:, t]), ALU.mult)
                tt(kbg[:], bank4(1), overd(skbg[:, t]), ALU.mult)
                tt(kd[:], bank4(1), overd(skd[:, t]), ALU.mult)
                gstep(GV, tt(vb[:], bank4(2), overd(beta[:, t]), ALU.mult))
                gstep(GV, tt(trig[:], overh(gc("tri")), overd(graw[:, t]), ALU.mult))
                GP.wait(dve, t, "gram")
                gstep(GV, tt(DT[:], bank4(0), overh(gc("dneg")), ALU.add))
                GV.wait(dve, t, "dm")
                gstep(GV, tt(DT[:], DT[:], overd(gcs[:, t]), ALU.subtract))
                GA.wait(dve, t, "exp")
                gstep(GV, tt(DsT[:], DT[:], overh(gc("strict")), ALU.mult))
                gq = PS[:, 6:8, :].rearrange("p a (b c n) -> p (a b) c n", b=2, c=2)
                gstep(GV, tt(attnT[:], gq[:, :, 0, :], DT[:], ALU.mult))
                GV.wait(dve, t, "ds")
                gstep(GV, tt(AT[:], gq[:, :, 1, :], DsT[:], ALU.mult))
                GV.wait(dve, t, "at")
                gstep(GV, tt(U[:], AT[:], overh(gc("l0")), ALU.mult))
                GV.wait(dve, t, "u0")
                gstep(GV, tt(Z[:], overh(ident[:]), U[:], ALU.subtract))
                for l in LV:
                    if l > 1:
                        GP.wait(dve, t, f"y{l - 1}")
                    else:
                        GV.wait(dve, t, "z0")
                    gstep(GV, tt(U[:], AT[:], overh(gc(f"l{l}")), ALU.mult))
                    GP.wait(dve, t, f"z{l}")
                    gstep(GV, tt(X[:], X[:], bank4(3), ALU.subtract))
                    gstep(GV, tt(Z[:], Z[:], bank4(4), ALU.subtract))
                    GV.wait(dve, t, f"z{l}")
                GP.wait(dve, t, "uw")
                gstep(GV, nc.vector.tensor_copy(uu[:], bank4(5)))
                GV.wait(dve, t, "u")
                for c in range(2):
                    r = slice(GC * c, GC * c + GC)
                    GP.wait(dve, t, f"ws{c}")
                    gstep(GV, tt(vnew[r], uu[r], bank4(6)[r], ALU.subtract))
                    gstep(GV, tt(S[:], S[:], overd((egl0, egl1)[c][:, t]), ALU.mult))
                    GP.wait(dve, t, f"st{c}")
                    GV.wait(dve, t, f"sd{c}")
                    gstep(GV, tt(S[:], S[:], bank4(7), ALU.add))
                    GV.wait(dve, t, f"s{c}")
                GA.wait(dve, t, "qs1")
                gstep(GV, tt(qS[:], qS[:], overd(eg[:, t]), ALU.mult))
                GP.wait(dve, t, "oi")
                GV.wait(dve, t, "qe")
                gstep(GV, tt(o_all[:, t], qS[:], bank4(1), ALU.add))

        o_ss, o_r, o_nrm, o_tr, y_mul, y_hi_ok, y_lo_ok = (sem(n) for n in (
            "o_ss", "o_r", "o_nrm", "o_tr", "y_mul", "y_hi_ok", "y_lo_ok"))

        def sp_gdn_out(sp):
            load_pieces(sp, P_GZ, P_GZ + 4)

        def pool_gdn_out(pool):
            split_pieces(pool, P_GZ, P_GZ + 4)

        def pe_gdn_out(pe):
            for h in range(GH):
                run_job(pe, P_GZ + h)
            pe.wait_ge(o_nrm, 1)
            for h in range(GH):
                if h >= 2:
                    pe.wait_ge(y_mul, h - 1)
                for t in range(TB):
                    last = nc.tensor.transpose(PS[:, 4 + 2 * (h % 2) + t // 4, (t % 4) * P:(t % 4 + 1) * P],
                                               o_all[:, t, h], ident[:])
                last.then_inc(o_tr, 1)

        def split_y(act, k, src):
            nc.scalar.activation(y_hi[:, k], src, ACT.Copy).then_inc(y_hi_ok, 1)

        def act_gdn_out(act):
            nc.scalar.activation(osq[:], o_all[:], ACT.Square).then_inc(o_ss, 1)
            act.wait_ge(o_r, 1)
            nc.scalar.activation(ort, oss, ACT.Sqrt, scale=1.0 / GD, bias=eps_t).then_inc(o_ss, 1)
            for h in range(GH):
                p = P_GZ + h
                act.wait_ge(tile_done, p + 1)
                evac_done(nc.scalar.activation(zT[:, h], pair(p % 2), ACT.Silu), p)
            for h in range(GH):
                act.wait_ge(y_mul, h + 1)
                split_y(act, h, ytmp[h % 2][:])

        def dve_gdn_out(dve):
            dve.wait_ge(o_ss, 1)
            nc.vector.tensor_reduce(oss, osq[:], AX_X, ALU.add).then_inc(o_r, 1)
            dve.wait_ge(o_ss, 2)
            dstep(nc.vector.reciprocal(ort, ort))
            nc.vector.tensor_tensor(o_all[:], o_all[:], ort.unsqueeze(3).to_broadcast([P, TB, GH, P]),
                                    ALU.mult).then_inc(o_nrm, 1)
            for h in range(GH):
                p = P_GZ + h
                dve.wait_ge(o_tr, h + 1)
                dve.wait_ge(tile_evac[p % 2], p // 2 + 1)
                if h >= 2:
                    dve.wait_ge(y_lo_ok, h - 1)
                nc.vector.scalar_tensor_tensor(out=ytmp[h % 2][:], in0=pair(2 + h % 2), scalar=normg, in1=zT[:, h],
                                               op0=ALU.mult, op1=ALU.mult).then_inc(y_mul, 1)
                dve.wait_ge(y_hi_ok, h + 1)
                nc.vector.tensor_tensor(y_lo[:, h], ytmp[h % 2][:], y_hi[:, h].bitcast(F32),
                                        ALU.subtract).then_inc(y_lo_ok, 1)

        G = [at(f"G{i}", 136 + 4 * i, [T]) for i in range(2)]
        mtmp = at("mtmp", 144, [T])
        gate_ok, merged = sem("gate_ok"), sem("merged")

        def sp_merge(sp, b):
            load_pieces(sp, P_MERGE[b], P_MERGE[b] + 2 * KT)

        def pool_merge(pool, b):
            split_pieces(pool, P_MERGE[b], P_MERGE[b] + 2 * KT)

        def pe_merge(pe, b):
            for c in range(KT):
                run_job(pe, P_MERGE[b] + 2 * c)
                run_job(pe, P_MERGE[b] + 2 * c + 1, y_hi, y_lo)

        def act_merge(act, b):
            for c in range(KT):
                p, n = P_MERGE[b] + 2 * c, b * KT + c
                act.wait_ge(tile_done, p + 1)
                if n >= 2:
                    act.wait_ge(merged, n - 1)
                evac_done(nc.scalar.activation(G[c % 2][:], pair(p % 2), ACT.Sigmoid), p)

        def dve_merge(dve, b):
            for c in range(KT):
                p, n = P_MERGE[b] + 2 * c, b * KT + c
                dve.wait_ge(tile_done, p + 2)
                dve.wait_ge(tile_evac[p % 2], p // 2 + 1)
                dst = mT[:, c] if b == 0 else mtmp[:]
                evac_done(nc.vector.tensor_tensor(dst, pair((p + 1) % 2), G[c % 2][:], ALU.mult), p + 1)
                dve.wait_ge(tile_evac[(p + 1) % 2], (p + 1) // 2 + 1)
                if b == 0:
                    nc.vector.tensor_copy(mtmp[:, 0:1], mT[:, c, 0:1]).then_inc(merged, 1)
                else:
                    nc.vector.tensor_tensor(mT[:, c], mT[:, c], mtmp[:], ALU.add).then_inc(merged, 1)
                dve.wait_ge(merged, n + 1)
        QT = at("QT", 136, [NM, T])
        kslc, kwin = at("kslc", 152, [T]), at("kwin", 156, [T])
        vslc, vwin = at("vslc", 160, [TB, P]), at("vwin", 164, [TB, P])
        cmpT = [at("kcmpT", 168, [T]), at("vcmpT", 172, [T])]
        vT = [at(f"vT{i}", 176 + 4 * i, [T]) for i in range(2)]
        window = at("window", 184, [CL, 64])
        wcmp = at("wcmp", 120, [CL, P])
        pos_in = at("pos_in", 192, [2, P])
        posT = at("posT", 193, [2, CL])
        kcT, vcT = at("kcT", 205.5, [64]), at("vcT", 205.75, [2, 64])
        vc = at("vc", 206.25, [P])
        P4 = at("P4", 206.75, [NG, 68])
        msel_all = at("msel_all", 192, [TB, NG, NSEL])
        score = at("score", 207.40625, [NG, NSEL])
        maskw = at("maskw", 188, [WT, P])
        maskg = at("maskg", 168, [NG, T])
        sbuf = [at(f"sbuf{i}", o, [T]) for i, o in enumerate((176, 180, 64))]
        pT = [at(f"pT{i}", o, [TB, P]) for i, o in enumerate((184, 68))]
        oall = at("oall", 120, [TB, NM, NG, ND])
        sc = at("sc", 176, [NH, 64])
        pcT = at("pcT", 180, [NH // 2, P])
        cgt, ceq = at("cgt", 184, [NG, NSEL, NSEL]), at("ceq", 186, [NG, NSEL, NSEL])
        c8 = lambda o: scal(o, 8)
        cmx, csm = c8(0), c8(8)
        nmx, rsum, wrow = scal(1080, 4), scal(1084, 4), scal(1088, 4)
        NI = {}
        o = 0
        for n, k in (("causal", P), ("old", P), ("lower", NSEL * NSEL), ("cneg", TB * 64), ("cval", TB * 64),
                     ("bias", TB * NSEL)):
            NI[n] = (o, o + k)
            o += k
        ncst = lambda n: consts[:, NI[n][0]:NI[n][1]]

        (n_in, pos_tr, pos_ok, v_tr, v_tok, win_ok, kc_ok, kc_evac, vc_tr, vc_ok, wc_zero, mw_ok) = (
            sem(n) for n in ("n_in", "pos_tr", "pos_ok", "v_tr", "v_tok", "win_ok", "kc_ok", "kc_evac", "vc_tr",
                             "vc_ok", "wc_zero", "mw_ok"))
        wc_in = sem("wc_in")

        def load_wcmp(sp, name):
            src = A[name][0].rearrange("l d e -> d l e")
            for g in range(NG):
                r = slice(ND * g, ND * g + ND)
                sp.dma_start(wcmp[r, :, r], src).then_inc(wc_in, 16)

        def sp_nsa(sp):
            sp.dma_start(consts[:], A["c_nsa"]).then_inc(n_in, 16)
            for i, n in enumerate(("nsa_cmp_pk", "nsa_cmp_pv")):
                for g in range(NG):
                    sp.dma_start(pos_in[0:CL, i, ND * g:ND * g + ND], A[n][0]).then_inc(n_in, 16)
            sp.wait_ge(wc_zero, 1)
            load_wcmp(sp, "nsa_cmp_wk")
            load_pieces(sp, P_NSA, P_NSA + 10)
            sp.wait_ge(kc_ok, 1)
            load_wcmp(sp, "nsa_cmp_wv")

        def pool_nsa(pool):
            nc.gpsimd.memset(wcmp[:], 0.0).then_inc(wc_zero, 1)
            split_pieces(pool, P_NSA, P_NSA + 10)
            for k in range(2):
                pool.wait_ge(tile_evac[(P_NSA + k) % 2], (P_NSA + k) // 2 + 1)
                pool.wait_ge(pos_ok, 2)
                if k == 1:
                    pool.wait_ge(kc_ok, 1)
                for half in range(2):
                    ins = nc.gpsimd.tensor_tensor(
                        window[:, 16 * half:16 * half + 16, 0:NCMP],
                        cmpT[k][:, 16 * half:16 * half + 16 * NCMP].rearrange("p (n s) -> p s n", s=CS),
                        posT[:, k, 16 * half:16 * half + 16].unsqueeze(2).to_broadcast([P, 16, NCMP]), ALU.add)
                ins.then_inc(win_ok, 1)

        def pe_nsa(pe):
            pe.wait_ge(n_in, 80)
            for i in range(2):
                nc.tensor.transpose(PS[:, 4, CL * i:CL * i + CL], pos_in[0:CL, i], ident[0:CL, 0:CL]).then_inc(pos_tr, 1)
            for p in range(P_NSA, P_NSA + 10):
                run_job(pe, p)
                if p - P_NSA in (4, 6):
                    i = (p - P_NSA - 4) // 2
                    q = P_NSA + 3 + 2 * i
                    pe.wait_ge(tile_evac[q % 2], q // 2 + 1)
                    if i:
                        pe.wait_ge(v_tok, 1)
                    for t in range(TB):
                        last = nc.tensor.transpose(PS[:, 6 + t // 4, (t % 4) * P:(t % 4 + 1) * P],
                                                   vT[i][:, t * P:(t + 1) * P], ident[:])
                    last.then_inc(v_tr, 1)
            for k in range(2):
                pe.wait_ge(win_ok, k + 1)
                pe.wait_ge(wc_in, 32 * (k + 1))
                for l in range(CL):
                    last = nc.tensor.matmul(PS[:, 4 + k, 0:NCMP], wcmp[:, l], window[:, l, 0:NCMP],
                                            start=(l == 0), stop=(l == CL - 1))
                last.then_inc(kc_ok, 1)
            pe.wait_ge(kc_evac, 2)
            pe.wait_ge(v_tok, 2)
            nc.tensor.transpose(PS[:, 6, 0:P], vcT[:].rearrange("p a n -> p (a n)"), ident[:]).then_inc(vc_tr, 1)

        def act_nsa(act):
            for k in range(10):
                p = P_NSA + k
                act.wait_ge(tile_done, p + 1)
                dst = (cmpT[0], cmpT[1], kslc, vT[0], kwin, vT[1])[k][:] if k < 6 else QT[:, k - 6]
                evac_done(nc.scalar.activation(dst, pair(p % 2), ACT.Copy, scale=1.0 if k < 6 else float(ND) ** -0.5), p)
            act.wait_ge(mw_ok, 3)
            act.wait_ge(kc_ok, 1)
            nc.scalar.activation(kcT[:, 0:NCMP], PS[:, 4, 0:NCMP], ACT.Copy).then_inc(kc_evac, 1)
            act.wait_ge(kc_ok, 2)
            nc.scalar.activation(vcT[:, :, 0:NCMP], PS[:, 5, 0:NCMP].unsqueeze(1).to_broadcast([P, 2, NCMP]),
                                 ACT.Copy).then_inc(kc_evac, 1)
            act.wait_ge(vc_tr, 1)
            nc.scalar.activation(vc[:], PS[:, 6, 0:P], ACT.Copy).then_inc(vc_ok, 1)

        def dve_nsa(dve):
            for i in range(2):
                dve.wait_ge(pos_tr, 2)
                nc.vector.tensor_copy(posT[:, i], PS[:, 4, CL * i:CL * i + CL]).then_inc(pos_ok, 1)
            for zero in (P4[:], kcT[:], vcT[:]):
                nc.vector.memset(zero, 0.0).then_inc(mw_ok, 1)
            for i, dst in enumerate((vslc, vwin)):
                dve.wait_ge(v_tr, i + 1)
                nc.vector.tensor_copy(dst[:].rearrange("p t n -> p (t n)"), pair(3)).then_inc(v_tok, 1)

        CP = Stages(sem, "cmp_pe", ["s", "t", "o"])
        CA = Stages(sem, "cmp_act", ["e", "pt"])
        CV = Stages(sem, "cmp_dve", ["s", "mx", "sub", "sm", "r", "p", "pv", "oacc", "p4", "i", "i2", "sc", "gt", "eq",
                                    "low", "rank", "sum", "sel"])
        CHOICE = ("p4", "i", "i2", "sc", "gt", "eq", "low", "rank", "sum")
        CVSKIP = TOPK // 2
        CG = Stages(sem, "mask", ["m", "mc"])
        UN = Stages(sem, "unit", ["scores", "masked", "max", "exp", "turned", "copied", "out", "recip", "weight", "sum"])
        NU = 2 * NH
        UALL = TB * NU

        def unit(u):
            t, r = divmod(u, NU)
            g, r = divmod(r, 2 * NM)
            m, kind = divmod(r, 2)
            first = 0 if kind == 0 else max(0, t - WT + 1)
            n = t + 1 - first
            mask = maskg[:, g, 0:n * P] if kind == 0 else maskw[:, WT - n:WT].rearrange("p a b -> p (a b)")
            return t, g, m, kind, first, n, (kslc, kwin)[kind], (vslc, vwin)[kind], mask

        def pe_cmp(pe, t):
            if t:
                CV.wait(pe, t - 1, "oacc")
            for g in range(NG):
                r = slice(ND * g, ND * g + ND)
                for m in range(NM):
                    last = nc.tensor.matmul(PS[:, 4 + g, 64 * m:64 * m + 64], QT[r, m, t * P:(t + 1) * P],
                                            kcT[r, :], start=True, stop=True)
            CP.done("s", last)
            CV.wait(pe, t, "pv")
            for k in range(NH // 2):
                last = nc.tensor.transpose(PS[:, 6, k * P:(k + 1) * P],
                                           sc[:, 2 * k:2 * k + 2].rearrange("p a n -> p (a n)"), ident[:])
            CP.done("t", last)
            CA.wait(pe, t, "pt")
            for hh in range(NH):
                g, r = hh // NM, slice(64 * (hh % 2), 64 * (hh % 2) + 64)
                last = nc.tensor.matmul(PS[:, 4 + hh % 2, ND * (hh // 2):ND * (hh // 2) + ND], pcT[r, hh // 2],
                                        vc[r, ND * g:ND * g + ND], start=True, stop=True)
            CP.done("o", last)

        def pe_nsa_cmp(pe):
            for t in range(TB):
                pe_cmp(pe, t)

        def act_nsa_cmp(act):
            for t in range(TB):
                CV.wait(act, t, "sub")
                CA.done("e", nc.scalar.activation(sc[:], sc[:], ACT.Exp))
                CP.wait(act, t, "t")
                CA.done("pt", nc.scalar.activation(pcT[:].rearrange("p h n -> p (h n)"), PS[:, 6, :], ACT.Copy))

        def dve_nsa_cmp(dve):
            for t in range(TB):
                dve_cmp(dve, t)

        def pe_nsa_attn(pe):
            for k in range(UALL + 3):
                if k < UALL:
                    u = k
                    t, g, m, kind, first, n, keys, vals, mask = unit(u)
                    r = slice(ND * g, ND * g + ND)
                    if u >= 2:
                        UN.wait(pe, u - 2, "masked")
                    for a in range(0, n * P, 512):
                        w = min(512, n * P - a)
                        last = nc.tensor.matmul(pair(u % 2)[:, a:a + w], QT[r, m, t * P:(t + 1) * P],
                                                keys[r, first * P + a:first * P + a + w], start=True, stop=True)
                    UN.done("scores", last)
                if 2 <= k < UALL + 2:
                    u = k - 2
                    n = unit(u)[5]
                    UN.wait(pe, u, "exp")
                    if u >= 1:
                        UN.wait(pe, u - 1, "copied")
                    for j in range(n):
                        last = nc.tensor.transpose(pair(2)[:, j * P:(j + 1) * P], sbuf[u % 3][:, j * P:(j + 1) * P],
                                                   ident[:])
                    UN.done("turned", last)
                if k >= 3:
                    u = k - 3
                    t, g, m, kind, first, n, keys, vals, mask = unit(u)
                    UN.wait(pe, u, "copied")
                    if u >= 2:
                        UN.wait(pe, u - 2, "sum")
                    for j in range(n):
                        last = nc.tensor.matmul(PS[:, 6 + u % 2, 0:ND], pT[u % 2][:, j],
                                                vals[:, first + j, ND * g:ND * g + ND],
                                                start=(j == 0), stop=(j == n - 1))
                    UN.done("out", last)

        def act_nsa_attn(act):
            for k in range(1, UALL + 2):
                if k <= UALL:
                    u = k - 1
                    s = sbuf[u % 3][:, 0:unit(u)[5] * P]
                    c = u % 4
                    UN.wait(act, u, "max")
                    if u >= 4:
                        UN.wait(act, u - 4, "recip")
                    UN.done("exp", nc.scalar.activation(s, s, ACT.Exp, bias=nmx[:, c:c + 1], accum_out=rsum[:, c:c + 1]))
                if k >= 2:
                    u = k - 2
                    n = unit(u)[5]
                    UN.wait(act, u, "turned")
                    if u >= 2:
                        UN.wait(act, u - 2, "out")
                    UN.done("copied", nc.scalar.activation(pT[u % 2][:, 0:n].rearrange("p k n -> p (k n)"),
                                                           pair(2)[:, 0:n * P], ACT.Copy))

        def pool_nsa_attn(pool):
            for t in range(TB):
                if t:
                    UN.wait(pool, t * NU - 1, "masked")
                for g in range(NG):
                    ins = nc.gpsimd.tensor_copy(maskg[:, g, 0:(t + 1) * P].rearrange("p (j l) -> p j l", l=SL),
                                                msel_all[:, t, g, 0:2 * (t + 1)].unsqueeze(2)
                                                .to_broadcast([P, 2 * (t + 1), SL]))
                CG.done("m", ins)
                CG.wait(pool, t, "m")
                last = maskg[:, :, t * P:(t + 1) * P]
                CG.done("mc", nc.gpsimd.tensor_tensor(last, last, ncst("causal").unsqueeze(1).to_broadcast([P, NG, P]),
                                                      ALU.add))

        def dve_cmp(dve, t):
            tt, red = nc.vector.tensor_tensor, nc.vector.tensor_reduce
            scn = sc[:]
            sc4 = sc[:].rearrange("p (g m) n -> p g m n", g=NG)
            over8 = lambda n: ncst(n)[:, 64 * t:64 * t + 64].unsqueeze(1).unsqueeze(1).to_broadcast([P, NG, NM, 64])
            along = lambda ap: ap.unsqueeze(2).to_broadcast([P, NH, 64])
            step = lambda n, ins: (ins.then_inc(CV.sems[n], 1), dve.wait_ge(CV.sems[n], t + 1 - (CVSKIP if n in CHOICE else 0)))
            CP.wait(dve, t, "s")
            step("s", tt(sc4, PS[:, 4:6, 0:256].rearrange("p g (m n) -> p g m n", m=NM), over8("cneg"), ALU.add))
            step("mx", red(cmx, scn, AX_X, ALU.max))
            step("sub", tt(scn, scn, along(cmx), ALU.subtract))
            CA.wait(dve, t, "e")
            step("sm", red(csm, scn, AX_X, ALU.add))
            step("r", nc.vector.reciprocal(csm, csm))
            step("p", tt(scn, scn, along(csm), ALU.mult))
            step("pv", tt(sc4, sc4, over8("cval"), ALU.mult))
            CP.wait(dve, t, "o")
            gates = nsa_gate[:, t].rearrange("p (g k a c) -> p a g k c", g=NG, a=2, c=3)[:, :, :, :, 0]
            for par in range(2):
                ins = tt(oall[:, t].rearrange("p (k a) g d -> p a g k d", a=2)[:, par],
                         PS[:, 4 + par, 0:256].rearrange("p (g k d) -> p g k d", g=NG, k=2),
                         gates[:, par].unsqueeze(3).to_broadcast([P, NG, 2, ND]), ALU.mult)
            step("oacc", ins)
            msel = msel_all[:, t]
            if 2 * (t + 1) <= TOPK:
                step("sel", nc.vector.memset(msel, 0.0))
                return
            imp = score[:]
            step("p4", red(P4[:, :, 1:1 + NCMP], sc[:].rearrange("p (g m) n -> p g n m", g=NG)[:, :, 0:NCMP, :], AX_X,
                           ALU.add))
            step("i", red(imp, P4[:, :, 0:64].rearrange("p g (j f) -> p g j f", f=4), AX_X, ALU.add))
            step("i2", tt(imp, imp, P4[:, :, 4:68].rearrange("p g (j f) -> p g j f", f=4)[:, :, :, 0], ALU.add))
            step("sc", tt(imp, imp, ncst("bias")[:, NSEL * t:NSEL * (t + 1)].unsqueeze(1).to_broadcast([P, NG, NSEL]),
                          ALU.add))
            full = [P, NG, NSEL, NSEL]
            si, sj = imp.unsqueeze(2).to_broadcast(full), imp.unsqueeze(3).to_broadcast(full)
            step("gt", tt(cgt[:], si, sj, ALU.is_gt))
            step("eq", tt(ceq[:], si, sj, ALU.is_equal))
            step("low", tt(ceq[:], ceq[:], ncst("lower").rearrange("p (j i) -> p j i", i=NSEL).unsqueeze(1)
                           .to_broadcast(full), ALU.mult))
            step("rank", tt(cgt[:], cgt[:], ceq[:], ALU.add))
            step("sum", red(msel, cgt[:], AX_X, ALU.add))
            step("sel", nc.vector.tensor_scalar(msel, msel, float(TOPK), NEG, ALU.is_ge, ALU.mult))

        def dve_nsa_attn(dve):
            dstep(nc.vector.memset(maskw[:], 0.0))
            dstep(nc.vector.tensor_copy(maskw[:, 0], ncst("old")))
            dstep(nc.vector.tensor_copy(maskw[:, WT - 1], ncst("causal")))
            for k in range(UALL + 3):
                if k < UALL:
                    u = k
                    t, g, m, kind, first, n, keys, vals, mask = unit(u)
                    c, s = u % 4, sbuf[u % 3][:, 0:n * P]
                    UN.wait(dve, u, "scores")
                    if u % NU == 0:
                        CG.wait(dve, t, "mc")
                    if u >= 3:
                        UN.wait(dve, u - 3, "turned")
                    UN.done("masked", nc.vector.tensor_tensor(s, pair(u % 2)[:, 0:n * P], mask, ALU.add))
                    UN.wait(dve, u, "masked")
                    UN.done("max", nc.vector.tensor_reduce(nmx[:, c:c + 1], s, AX_X, ALU.max, negate=True))
                if k >= 3:
                    u = k - 3
                    t, g, m, kind, first, n, keys, vals, mask = unit(u)
                    c = u % 4
                    UN.wait(dve, u, "exp")
                    UN.done("recip", nc.vector.reciprocal(wrow[:, c:c + 1], rsum[:, c:c + 1]))
                    UN.wait(dve, u, "recip")
                    gate = nsa_gate[:, t, 3 * (g * NM + m) + 1 + kind:3 * (g * NM + m) + 2 + kind]
                    UN.done("weight", nc.vector.tensor_tensor(wrow[:, c:c + 1], wrow[:, c:c + 1], gate, ALU.mult))
                    UN.wait(dve, u, "out")
                    UN.wait(dve, u, "weight")
                    if u:
                        UN.wait(dve, u - 1, "sum")
                    o = oall[:, t, m, g]
                    UN.done("sum", nc.vector.scalar_tensor_tensor(out=o, in0=PS[:, 6 + u % 2, 0:ND],
                                                                  scalar=wrow[:, c:c + 1], in1=o,
                                                                  op0=ALU.mult, op1=ALU.add))

        ny_tr = sem("ny_tr")

        def pe_turn_y(pe, b, src):
            for m in range(NM):
                if m >= 2:
                    pe.wait_ge(y_lo_ok, 4 * b + m - 1)
                for t in range(TB):
                    last = nc.tensor.transpose(pair(m % 2)[:, t * P:(t + 1) * P],
                                               src[:, t, m].rearrange("p g d -> p (g d)"), ident[:])
                last.then_inc(ny_tr, 1)

        def act_turn_y(act, b):
            for m in range(NM):
                act.wait_ge(ny_tr, 4 * (b - 1) + m + 1)
                split_y(act, m, pair(m % 2))

        def dve_turn_y(dve, b):
            for m in range(NM):
                dve.wait_ge(y_hi_ok, 4 * b + m + 1)
                nc.vector.tensor_tensor(y_lo[:, m], pair(m % 2), y_hi[:, m].bitcast(F32),
                                        ALU.subtract).then_inc(y_lo_ok, 1)
        sqT, skT, sv_tok = at("sqT", 136, [4, T]), at("skT", 152, [4, T]), at("sv_tok", 168, [4, TB, P])
        svT = [at(f"svT{i}", 184 + 4 * i, [T]) for i in range(2)]
        cum = [at(f"cum{i}", 184 + 4.5 * i, [T + 8]) for i in range(2)]
        sbw = [at(f"sbw{i}", 64 + 4 * i, [T]) for i in range(4)]
        spT = [at(f"spT{i}", 80 + 4 * i, [TB, P]) for i in range(2)]
        osb = at("osb", 120, [TB, 4, 2, SD])
        ntot = scal(1086, 4)
        sb_in, cum0, sv_tr, sv_ok = (sem(n) for n in ("sb_in", "cum0", "sv_tr", "sv_ok"))
        SB = Stages(sem, "sb", ["z", "abs", "exp", "log", "softplus", "prefix", "total", "added", "weights", "turned",
                                "copied", "out", "kept"])
        SU = 4 * TB * 2
        sneg = consts[:, 0:P]

        def sb_unit(u):
            m, r = divmod(u, 2 * TB)
            t, a = divmod(r, 2)
            return m, a, t, t + 1

        def sp_sb(sp):
            sp.dma_start(consts[:, 0:P], A["c_sb"]).then_inc(sb_in, 16)
            load_pieces(sp, P_SB, P_SB + 12)

        def pool_sb(pool):
            split_pieces(pool, P_SB, P_SB + 12)

        def pe_sb(pe):
            for m in range(4):
                for j in range(3):
                    run_job(pe, P_SB + 3 * m + j)
                q = P_SB + 3 * m + 2
                pe.wait_ge(tile_evac[q % 2], q // 2 + 1)
                if m >= 2:
                    pe.wait_ge(sv_ok, m - 1)
                for t in range(TB):
                    last = nc.tensor.transpose(pair(2 + m % 2)[:, t * P:(t + 1) * P], svT[m % 2][:, t * P:(t + 1) * P],
                                               ident[:])
                last.then_inc(sv_tr, 1)

        def act_sb(act):
            for m in range(4):
                for j, dst in enumerate((sqT[:, m], skT[:, m], svT[m % 2][:])):
                    p = P_SB + 3 * m + j
                    act.wait_ge(tile_done, p + 1)
                    if j == 2 and m >= 2:
                        act.wait_ge(sv_tr, m - 1)
                    evac_done(nc.scalar.activation(dst, pair(p % 2), ACT.Copy,
                                                   scale=float(SD) ** -0.5 if j == 0 else 1.0), p)

        def dve_sb(dve):
            for m in range(4):
                dve.wait_ge(sv_tr, m + 1)
                nc.vector.tensor_copy(sv_tok[:, m].rearrange("p t n -> p (t n)"), pair(2 + m % 2)).then_inc(sv_ok, 1)

        def pe_sb_attn(pe):
            pe.wait_ge(sb_in, 16)
            for k in range(SU + 4):
                if k < SU:
                    m, a, t, n = sb_unit(k)
                    r = slice(SD * a, SD * a + SD)
                    if k >= 2:
                        SB.wait(pe, k - 2, "added")
                    for c in range(0, n * P, 512):
                        w = min(512, n * P - c)
                        nc.tensor.matmul(pair(k % 2)[:, c:c + w], sqT[r, m, t * P:(t + 1) * P],
                                         skT[r, m, c:c + w], start=True, stop=(c + w < n * P))
                    SB.done("z", nc.tensor.matmul(pair(k % 2)[:, t * P:n * P], ident[:], sneg, start=False, stop=True))
                if 3 <= k < SU + 3:
                    u = k - 3
                    n = sb_unit(u)[3]
                    SB.wait(pe, u, "weights")
                    if u >= 1:
                        SB.wait(pe, u - 1, "copied")
                    for j in range(n):
                        last = nc.tensor.transpose(pair(2)[:, j * P:(j + 1) * P], sbw[u % 4][:, j * P:(j + 1) * P],
                                                   ident[:])
                    SB.done("turned", last)
                if k >= 4:
                    u = k - 4
                    m, a, t, n = sb_unit(u)
                    SB.wait(pe, u, "copied")
                    if u >= 2:
                        SB.wait(pe, u - 2, "kept")
                    for j in range(n):
                        last = nc.tensor.matmul(PS[:, 6 + u % 2, 0:SD], spT[u % 2][:, j],
                                                sv_tok[:, m, j, SD * a:SD * a + SD], start=(j == 0), stop=(j == n - 1))
                    SB.done("out", last)

        def sb_copy(eng, u, op):
            n = sb_unit(u)[3]
            SB.wait(eng, u, "turned")
            if u >= 2:
                SB.wait(eng, u - 2, "out")
            if u >= 1:
                SB.wait(eng, u - 1, "copied")
            SB.done("copied", op(spT[u % 2][:, 0:n].rearrange("p k n -> p (k n)"), pair(2)[:, 0:n * P]))

        def act_sb_attn(act):
            nc.scalar.preload_act_table_set("natural_log_exp_and_others")
            for k in range(SU + 4):
                if k < SU:
                    w = sb_unit(k)[3] * P
                    s = sbw[k % 4][:, 0:w]
                    SB.wait(act, k, "z")
                    if k >= 4:
                        SB.wait(act, k - 4, "turned")
                    SB.done("abs", nc.scalar.activation(s, pair(k % 2)[:, 0:w], ACT.Abs))
                if 1 <= k <= SU:
                    u = k - 1
                    s = sbw[u % 4][:, 0:sb_unit(u)[3] * P]
                    SB.wait(act, u, "added")
                    SB.wait(act, u, "total")
                    SB.done("weights", nc.scalar.activation(s, s, ACT.Exp, bias=ntot[:, u % 4:u % 4 + 1]))
                if k < SU:
                    s = sbw[k % 4][:, 0:sb_unit(k)[3] * P]
                    SB.wait(act, k, "abs")
                    SB.done("exp", nc.scalar.activation(s, s, ACT.Exp, scale=-1.0))
                if 3 <= k < SU + 3 and (k - 3) % 2 == 0:
                    sb_copy(act, k - 3, lambda o, i: nc.scalar.activation(o, i, ACT.Copy))
                if k < SU:
                    s = sbw[k % 4][:, 0:sb_unit(k)[3] * P]
                    SB.wait(act, k, "exp")
                    SB.done("log", nc.scalar.activation(s, s, ACT.Ln, bias=1.0))

        def dve_sb_attn(dve):
            tt = nc.vector.tensor_tensor
            nc.vector.memset(cum[0][:, 0:1], 0.0).then_inc(cum0, 1)
            nc.vector.memset(cum[1][:, 0:1], 0.0).then_inc(cum0, 1)
            dve.wait_ge(cum0, 2)
            for k in range(SU + 4):
                if 3 <= k < SU + 3 and (k - 3) % 2 == 1:
                    sb_copy(dve, k - 3, nc.vector.tensor_copy)
                if k < SU:
                    w = sb_unit(k)[3] * P
                    s, z, c = sbw[k % 4][:, 0:w], pair(k % 2)[:, 0:w], cum[k % 2]
                    SB.wait(dve, k, "log")
                    SB.done("softplus", nc.vector.scalar_tensor_tensor(out=s, in0=z, scalar=0.0, in1=s, op0=ALU.max,
                                                                       op1=ALU.add))
                if k >= 4:
                    u = k - 4
                    m, a, t, n = sb_unit(u)
                    SB.wait(dve, u, "out")
                    SB.done("kept", nc.vector.tensor_copy(osb[:, t, m, a], PS[:, 6 + u % 2, 0:SD]))
                if k < SU:
                    SB.wait(dve, k, "softplus")
                    if k >= 2:
                        SB.wait(dve, k - 2, "added")
                        SB.wait(dve, k - 2, "total")
                    SB.done("prefix", nc.vector.tensor_tensor_scan(c[:, 1:w + 1], s, s, 0.0, ALU.add, ALU.max))
                    SB.wait(dve, k, "prefix")
                    if k >= 4:
                        SB.wait(dve, k - 4, "weights")
                    SB.done("total", nc.vector.tensor_scalar(ntot[:, k % 4:k % 4 + 1], c[:, w:w + 1], -1.0, None,
                                                             ALU.mult))
                    SB.done("added", tt(s, z, c[:, 0:w], ALU.add))
        YT = at("YT", 120, [KT, T])
        xb = [at(f"xb{i}", 152 + 4 * i, [D]) for i in range(2)]
        nrm = [at(f"nrm{i}", 160 + 4 * i, [D]) for i in range(2)]
        x1 = [at(f"x1_{i}", 168 + 4 * i, [D]) for i in range(2)]
        g_post, g_ff = at("g_post", 176, [D]), at("g_ff", 180, [D])
        junk = at("junk", 184, [D])
        x1_dram = nc.dram_tensor("x1_scratch", (T, D), F32).ap().rearrange("(t p) d -> t p d", p=P)
        mt_hi, mt_lo, gains_in = sem("mt_hi"), sem("mt_lo"), sem("gains_in")
        xb_in = [sem("xb_in0"), sem("xb_in1")]
        x1_out = [sem("x1_out0"), sem("x1_out1")]

        def act_split_m(act):
            for k in range(KT):
                nc.scalar.activation(hT_hi[:, k], mT[:, k], ACT.Copy).then_inc(mt_hi, 1)

        def dve_split_m(dve):
            for k in range(KT):
                dve.wait_ge(mt_hi, k + 1)
                nc.vector.tensor_tensor(hT_lo[:, k], mT[:, k], hT_hi[:, k].bitcast(F32), ALU.subtract).then_inc(mt_lo, 1)

        def sp_wout(sp):
            load_pieces(sp, P_OUT, P_OUT + KT)

        def pool_wout(pool):
            split_pieces(pool, P_OUT, P_OUT + KT)

        def pe_wout(pe):
            for c in range(KT):
                run_job(pe, P_OUT + c)

        def act_wout(act):
            for c in range(KT):
                p = P_OUT + c
                act.wait_ge(tile_done, p + 1)
                evac_done(nc.scalar.activation(YT[:, c], pair(p % 2), ACT.Copy), p)

        NP = Steps(sem("res_pe"), ["y", "h"])
        NA = Steps(sem("res_act"), ["ss", "rt", "ss1", "rt1", "hi"])
        NV = Steps(sem("res_dve"), ["r", "n", "x1", "r1", "h", "lo"])
        sq1 = scal(0, 4)

        def sp_res(sp):
            sp.dma_start(g_post[:], bc(A["g_mix_post"][0], D)).then_inc(gains_in, 16)
            sp.dma_start(g_ff[:], bc(A["g_ff_pre"][0], D)).then_inc(gains_in, 16)
            for t in range(TB + 1):
                if t < TB:
                    if t >= 2:
                        NV.wait(sp, t - 2, "x1")
                    sp.dma_start(xb[t % 2][:], x_v[t]).then_inc(xb_in[t % 2], 16)
                if t >= 1:
                    NV.wait(sp, t - 1, "x1")
                    sp.dma_start(x1_dram[t - 1], x1[(t - 1) % 2][:]).then_inc(x1_out[(t - 1) % 2], 16)
            for i in range(2):
                sp.wait_ge(x1_out[i], 16 * TB // 2)

        def pe_res(pe):
            for t in range(TB):
                if t >= 2:
                    NV.wait(pe, t - 2, "n")
                for k in range(KT):
                    last = nc.tensor.transpose(pair(t % 2)[:, k * P:(k + 1) * P], YT[:, k, t * P:(t + 1) * P], ident[:])
                gstep(NP, last)
                NV.wait(pe, t, "h")
                if t >= 2:
                    NV.wait(pe, t - 2, "lo")
                for k in range(KT):
                    last = nc.tensor.transpose(pair(2 + t % 2)[:, k * P:(k + 1) * P], nrm[t % 2][:, k * P:(k + 1) * P], ident[:])
                gstep(NP, last)

        def act_res(act):
            for t in range(TB):
                b = t % 2
                NP.wait(act, t, "y")
                if t:
                    NA.wait(act, t - 1, "hi")
                gstep(NA, nc.scalar.activation(junk[:], pair(b), ACT.Square, accum_out=sq1[:, 0:1]))
                NA.wait(act, t, "ss")
                gstep(NA, nc.scalar.activation(sq1[:, 1:2], sq1[:, 0:1], ACT.Sqrt, scale=1.0 / D, bias=eps_t))
                NV.wait(act, t, "x1")
                gstep(NA, nc.scalar.activation(junk[:], x1[b][:], ACT.Square, accum_out=sq1[:, 2:3]))
                NA.wait(act, t, "ss1")
                gstep(NA, nc.scalar.activation(sq1[:, 3:4], sq1[:, 2:3], ACT.Sqrt, scale=1.0 / D, bias=eps_t))
                NP.wait(act, t, "h")
                gstep(NA, nc.scalar.activation(hT_hi[:, :, t * P:(t + 1) * P],
                                               pair(2 + b).rearrange("p (k n) -> p k n", n=P), ACT.Copy))

        def dve_res(dve):
            dve.wait_ge(gains_in, 32)
            for t in range(TB):
                b = t % 2
                NA.wait(dve, t, "rt")
                gstep(NV, nc.vector.reciprocal(sq1[:, 1:2], sq1[:, 1:2]))
                NV.wait(dve, t, "r")
                if t >= 2:
                    NP.wait(dve, t - 2, "h")
                gstep(NV, nc.vector.scalar_tensor_tensor(out=nrm[b][:], in0=pair(b), scalar=sq1[:, 1:2], in1=g_post[:],
                                                         op0=ALU.mult, op1=ALU.mult))
                NV.wait(dve, t, "n")
                dve.wait_ge(xb_in[b], 16 * (t // 2 + 1))
                if t >= 2:
                    dve.wait_ge(x1_out[b], 16 * (t // 2))
                gstep(NV, nc.vector.tensor_tensor(x1[b][:], xb[b][:], nrm[b][:], ALU.add))
                NA.wait(dve, t, "rt1")
                gstep(NV, nc.vector.reciprocal(sq1[:, 3:4], sq1[:, 3:4]))
                NV.wait(dve, t, "r1")
                gstep(NV, nc.vector.scalar_tensor_tensor(out=nrm[b][:], in0=x1[b][:], scalar=sq1[:, 3:4], in1=g_ff[:],
                                                         op0=ALU.mult, op1=ALU.mult))
                NA.wait(dve, t, "hi")
                s = slice(t * P, (t + 1) * P)
                gstep(NV, nc.vector.tensor_tensor(hT_lo[:, :, s], pair(2 + b).rearrange("p (k n) -> p k n", n=P),
                                                  hT_hi[:, :, s].bitcast(F32), ALU.subtract))

        aT_hi, aT_lo = at("aT_hi", 88, [KT, T], F32R), at("aT_lo", 120, [KT, T], F32R)
        FT = at("FT", 152, [KT, T])
        relu = [at(f"relu{i}", 184 + 4 * i, [T]) for i in range(2)]
        r_ok, s_ok, a_hi_ok, a_lo_ok, ft_zero = (sem(n) for n in ("relu_ok", "square_ok", "a_hi_ok", "a_lo_ok", "ft_zero"))
        JOBS = 2 * KT
        PM = P_MLP
        L0 = [loaded[0], loaded[1]]

        def pc(i, j):
            return i * JOBS + (PM + j)

        zero1 = small[:, 1150:1151]

        def sp_mlp(sp):
            with sp.Fori(0, CH) as i:
                for j in range(JOBS):
                    b = (PM + j) % 2
                    sp.wait_ge(w_split, pc(i, j) - 1)
                    src = w1_v[i * KT + j] if j < KT else w2_v[i, j - KT]
                    sp.dma_start(w_raw[b][:], src).then_inc(w_loaded[b], 16)

        def pool_mlp(pool):
            with pool.Fori(0, CH) as i:
                for j in range(JOBS):
                    b = (PM + j) % 2
                    pool.wait_ge(w_loaded[b], i * (8 * JOBS) + (L0[b] + 16 * (j // 2 + 1)))
                    pool.wait_ge(tile_done, pc(i, j) - 1)
                    nc.gpsimd.tensor_tensor(w_hi[b][:], w_raw[b][:], zero1.unsqueeze(2).to_broadcast([P, KT, P]),
                                            ALU.add).then_inc(w_high, 1)
                    pool.wait_ge(w_high, pc(i, j) + 1)
                    nc.gpsimd.tensor_tensor(w_lo[b][:], w_raw[b][:], w_hi[b][:].bitcast(F32),
                                            ALU.subtract).then_inc(w_split, 1)

        def evacs(i, j):
            return i * (JOBS // 2) + (PM + j) // 2

        def pe_mlp(pe):
            with pe.Fori(0, CH) as i:
                for j in range(JOBS):
                    b = (PM + j) % 2
                    pe.wait_ge(w_split, pc(i, j) + 1)
                    pe.wait_ge(tile_evac[b], evacs(i, j))
                    if j == KT:
                        pe.wait_ge(a_lo_ok, i * KT + (KT + 2))
                    job(pe, None, *((hT_hi, hT_lo) if j < KT else (aT_hi, aT_lo)), par=b)

        def act_mlp(act):
            with act.Fori(0, CH) as i:
                for j in range(KT):
                    b = (PM + j) % 2
                    act.wait_ge(tile_done, pc(i, j) + 1)
                    act.wait_ge(a_lo_ok, i * KT + j + 1)
                    nc.scalar.activation(relu[j % 2][:], pair(b), ACT.Relu).then_inc(tile_evac[b], 1)
                    act.wait_ge(s_ok, i * KT + j + 1)
                    nc.scalar.activation(aT_hi[:, j], relu[j % 2][:], ACT.Copy).then_inc(a_hi_ok, 1)

        def dve_mlp(dve):
            nc.vector.memset(FT[:], 0.0).then_inc(ft_zero, 1)
            for b in range(2):
                nc.vector.memset(relu[b][:, 0:1], 0.0).then_inc(a_lo_ok, 1)
            dve.wait_ge(ft_zero, 1)
            with dve.Fori(0, CH) as i:
                for j in range(KT):
                    b = (PM + j) % 2
                    r = relu[j % 2]
                    dve.wait_ge(tile_evac[b], evacs(i, j) + 1)
                    nc.vector.tensor_tensor(r[:], r[:], r[:], ALU.mult).then_inc(s_ok, 1)
                    dve.wait_ge(s_ok, i * KT + j + 1)
                    dve.wait_ge(a_hi_ok, i * KT + j + 1)
                    nc.vector.tensor_tensor(aT_lo[:, j], r[:], aT_hi[:, j].bitcast(F32), ALU.subtract).then_inc(a_lo_ok, 1)
                for j in range(KT, JOBS):
                    b = (PM + j) % 2
                    dve.wait_ge(tile_done, pc(i, j) + 1)
                    nc.vector.tensor_tensor(FT[:, j - KT], FT[:, j - KT], pair(b), ALU.add).then_inc(tile_evac[b], 1)
                dve.wait_ge(tile_evac[(PM + JOBS - 1) % 2], evacs(i, JOBS - 1) + 1)

        xf = [at(f"xf{i}", 88 + 4 * i, [D]) for i in range(2)]
        fn = [at(f"fn{i}", 96 + 4 * i, [D]) for i in range(2)]
        of = [at(f"of{i}", 104 + 4 * i, [D]) for i in range(2)]
        g_last, junkf = at("g_last", 112, [D]), at("junkf", 116, [D])
        out_v = out[0].rearrange("(t p) d -> t p d", p=P)
        gl_in = sem("gl_in")
        xf_in = [sem("xf_in0"), sem("xf_in1")]
        of_out = [sem("of_out0"), sem("of_out1")]
        FP = Steps(sem("fin_pe"), ["y"])
        FA = Steps(sem("fin_act"), ["ss", "rt"])
        FV = Steps(sem("fin_dve"), ["r", "n", "o"])

        def sp_fin(sp):
            sp.dma_start(g_last[:], bc(A["g_ff_post"][0], D)).then_inc(gl_in, 16)
            for t in range(TB + 1):
                if t < TB:
                    if t >= 2:
                        FV.wait(sp, t - 2, "o")
                    sp.dma_start(xf[t % 2][:], x1_dram[t]).then_inc(xf_in[t % 2], 16)
                if t >= 1:
                    FV.wait(sp, t - 1, "o")
                    sp.dma_start(out_v[t - 1], of[(t - 1) % 2][:]).then_inc(of_out[(t - 1) % 2], 16)
            for i in range(2):
                sp.wait_ge(of_out[i], 16 * TB // 2)

        def pe_fin(pe):
            for t in range(TB):
                if t >= 2:
                    FV.wait(pe, t - 2, "n")
                for k in range(KT):
                    last = nc.tensor.transpose(pair(t % 2)[:, k * P:(k + 1) * P], FT[:, k, t * P:(t + 1) * P], ident[:])
                gstep(FP, last)

        def act_fin(act):
            for t in range(TB):
                b = t % 2
                FP.wait(act, t, "y")
                if t >= 2:
                    FV.wait(act, t - 2, "n")
                if t:
                    FA.wait(act, t - 1, "rt")
                gstep(FA, nc.scalar.activation(junkf[:], pair(b), ACT.Square, accum_out=sq1[:, b:b + 1]))
                FA.wait(act, t, "ss")
                gstep(FA, nc.scalar.activation(sq1[:, 2 + b:3 + b], sq1[:, b:b + 1], ACT.Sqrt, scale=1.0 / D, bias=eps_t))

        def dve_fin(dve):
            dve.wait_ge(gl_in, 16)
            for t in range(TB):
                b = t % 2
                FA.wait(dve, t, "rt")
                gstep(FV, nc.vector.reciprocal(sq1[:, 2 + b:3 + b], sq1[:, 2 + b:3 + b]))
                FV.wait(dve, t, "r")
                gstep(FV, nc.vector.scalar_tensor_tensor(out=fn[b][:], in0=pair(b), scalar=sq1[:, 2 + b:3 + b], in1=g_last[:],
                                                         op0=ALU.mult, op1=ALU.mult))
                FV.wait(dve, t, "n")
                dve.wait_ge(xf_in[b], 16 * (t // 2 + 1))
                if t >= 2:
                    dve.wait_ge(of_out[b], 16 * (t // 2))
                gstep(FV, nc.vector.tensor_tensor(of[b][:], xf[b][:], fn[b][:], ALU.add))

        block = ctx.enter_context(nc.Block())
        phases = [
            (sp_phase0, None, act_phase0, dve_phase0, pe_phase0),
            (sp_gdn, pool_gdn, act_gdn, dve_gdn, pe_gdn),
            (None, None, act_gdn_blocks, dve_gdn_blocks, pe_gdn_blocks),
            (sp_gdn_out, pool_gdn_out, act_gdn_out, dve_gdn_out, pe_gdn_out),
            tuple((lambda f: lambda e: f(e, 0))(f) for f in (sp_merge, pool_merge, act_merge, dve_merge, pe_merge)),
            (sp_nsa, pool_nsa, act_nsa, dve_nsa, pe_nsa),
            (None, None, act_nsa_cmp, dve_nsa_cmp, pe_nsa_cmp),
            (None, pool_nsa_attn, act_nsa_attn, dve_nsa_attn, pe_nsa_attn),
            (None, None, lambda e: act_turn_y(e, 1), lambda e: dve_turn_y(e, 1), lambda e: pe_turn_y(e, 1, oall)),
            tuple((lambda f: lambda e: f(e, 1))(f) for f in (sp_merge, pool_merge, act_merge, dve_merge, pe_merge)),
            (sp_sb, pool_sb, act_sb, dve_sb, pe_sb),
            (None, None, act_sb_attn, dve_sb_attn, pe_sb_attn),
            (None, None, lambda e: act_turn_y(e, 2), lambda e: dve_turn_y(e, 2), lambda e: pe_turn_y(e, 2, osb)),
            tuple((lambda f: lambda e: f(e, 2))(f) for f in (sp_merge, pool_merge, act_merge, dve_merge, pe_merge)),
            (None, None, act_split_m, dve_split_m, None),
            (sp_wout, pool_wout, act_wout, None, pe_wout),
            (sp_res, None, act_res, dve_res, pe_res),
            (sp_mlp, pool_mlp, act_mlp, dve_mlp, pe_mlp),
            (sp_fin, None, act_fin, dve_fin, pe_fin),
        ]
        column = ("sync", "gpsimd", "scalar", "vector", "tensor")

        def run(eng, name):
            for row in phases:
                f = row[column.index(name)]
                if f:
                    f(eng)
                end_phase(eng, name)

        @block.sync
        def _(sp):
            run(sp, "sync")

        @block.gpsimd
        def _(pool):
            run(pool, "gpsimd")

        @block.scalar
        def _(act):
            run(act, "scalar")

        @block.vector
        def _(dve):
            run(dve, "vector")

        @block.tensor
        def _(pe):
            run(pe, "tensor")


_INS = ["x", "g_mix_pre", "g_mix_post", "g_ff_pre", "g_ff_post", "w_in", "gdn_conv_w", "gdn_a_log", "gdn_dt_bias",
        "gdn_norm_g", "nsa_cmp_wk", "nsa_cmp_pk", "nsa_cmp_wv", "nsa_cmp_pv", "w_br_gdn", "w_br_nsa", "w_br_sb",
        "w_out", "w_ff1", "w_ff2"]
_CONSTS = ["c_ident", "c_gdn", "c_nsa", "c_sb"]


def kernel(**inputs):
    import numpy as _np
    import concourse.bacc as _bacc
    from concourse import mybir as _mybir
    from concourse.bass_utils import run_bass_kernel_spmd as _run

    nc = _bacc.Bacc("TRN2", target_bir_lowering=False, num_devices=1)
    arrays, A = {}, {}
    for name in _INS:
        arrays[f"in_{name}"] = _np.ascontiguousarray(inputs[name])
    for name, table in zip(_CONSTS, shape_constants()):
        arrays[f"in_{name}"] = table
    for name in _INS + _CONSTS:
        a = arrays[f"in_{name}"]
        A[name] = nc.dram_tensor(f"in_{name}", a.shape, _mybir.dt.from_np(a.dtype), kind="ExternalInput").ap()
    out = nc.dram_tensor("out_0_dram", (1, T, D), _mybir.dt.float32, kind="ExternalOutput").ap()
    build(nc, A, out)
    r = _run(nc, [arrays], core_ids=[0])
    return r.results[0]["out_0_dram"]
```

```python
from contextlib import ExitStack

import numpy as np

import concourse.bass as bass
from concourse import mybir

F32 = mybir.dt.float32
F32R = mybir.dt.float32r
ALU = mybir.AluOpType
ACT = mybir.ActivationFunctionType
AX_X = mybir.AxisListType.X

P = 128
D = 1024
T = 1024
KT = D // P
TB = T // P
FF = 4 * D
SB0 = 16544
EPS = 1e-6
NEG = -1e30
PIECE = KT * P

GH, GD, GC = 4, 128, 64
NH, NG, ND = 8, 2, 64
NM = NH // NG
CL, CS = 32, 16
NCMP = (T - CL) // CS + 1
SL, TOPK = 64, 8
NSEL = T // SL
WIN = 512
WT = WIN // P + 1
SH, SD = 8, 64

SPLITS = [512, 512, 512, 512, 4, 4, 512, 768, 24, 512, 512, 512, 3072]
OFF = [sum(SPLITS[:i]) for i in range(len(SPLITS))]
(O_GQ, O_GK, O_GV, O_GZ, O_GA, O_GB, O_NQ, O_NKV, O_NGATE, O_SQ, O_SK, O_SV, O_MERGE) = OFF
N_IN = sum(SPLITS)


def shape_constants():
    i = np.arange(P)
    row, col = i[:, None], i[None, :]
    chunk = (row // GC) == (col // GC)
    f = lambda m: m.astype(np.float32)
    neg = lambda m: np.where(m, 0.0, NEG).astype(np.float32)
    gdn = [f(chunk & (row <= col)), neg(chunk & (row <= col)), f(chunk & (row < col))]
    for level in range(6):
        b = 1 << level
        gdn.append(f((row // b % 2 == 0) & (col // b == row // b + 1)))
    gdn += [f(chunk), np.ones((P, P), np.float32), f(row // GC == 0) * np.ones((1, P), np.float32),
            f(row // GC == 1) * np.ones((1, P), np.float32)]
    j = np.arange(NSEL)
    lower = f(j[None, :] < j[:, None]).reshape(1, -1) * np.ones((P, 1), np.float32)
    pos = np.arange(T).reshape(TB, P)
    start = np.arange(64) * CS
    valid = (start + CL - 1)[None, None, :] <= pos[:, :, None]
    valid = valid & (np.arange(64) < NCMP)
    valid = valid.transpose(1, 0, 2)
    cur = (pos // SL)[:, :, None]
    forced = (j == 0) | (j == cur) | (j == cur - 1)
    bias = np.where(j <= cur, 1e3 * forced, NEG).astype(np.float32).transpose(1, 0, 2)
    nsa = [neg(col <= row), neg(col > row), lower, neg(valid).reshape(P, -1), f(valid).reshape(P, -1),
           bias.reshape(P, -1)]
    sb = [neg(col < row)]
    cat = lambda x: np.ascontiguousarray(np.concatenate(x, 1))
    return np.eye(P, dtype=np.float32), cat(gdn), cat(nsa), cat(sb)


class Steps:

    def __init__(self, sem, names, base=0):
        self.sem, self.names, self.base = sem, names, base

    def done(self, i, name):
        return self.base + i * len(self.names) + self.names.index(name) + 1

    def wait(self, eng, i, name):
        eng.wait_ge(self.sem, self.done(i, name))


class Stages:

    def __init__(self, sem, prefix, names):
        self.sems = {n: sem(f"{prefix}_{n}") for n in names}

    def wait(self, eng, i, name):
        eng.wait_ge(self.sems[name], i + 1)

    def done(self, name, ins):
        ins.then_inc(self.sems[name], 1)


def build(nc, A, out):
    ctx = ExitStack()
    with ctx:
        def at(name, kb, shape, dt=F32):
            return nc.alloc_sbuf_tensor_at(name, [P] + list(shape), dt, offset=SB0 + int(kb * 1024))

        def sem(name):
            return ctx.enter_context(nc.semaphore(name))

        hT_hi = at("hT_hi", 0, [KT, T], F32R)
        hT_lo = at("hT_lo", 32, [KT, T], F32R)
        w_raw = [at(f"w_raw{i}", 64 + 4 * i, [KT, P]) for i in range(2)]
        w_hi = [at(f"w_hi{i}", 72 + 4 * i, [KT, P], F32R) for i in range(2)]
        w_lo = [at(f"w_lo{i}", 80 + 4 * i, [KT, P], F32R) for i in range(2)]
        mT = at("mT", 88, [KT, T])
        yT = at("yT", 120, [4, T])
        small = at("small", 194, [1152])
        ident = at("ident", 198.5, [P])
        consts = at("consts", 199, [1664])
        PS = ctx.enter_context(nc.psum_tensor("PS", [P, 8, 512], F32))

        def pair(k):
            return PS[:, 2 * k:2 * k + 2, :].rearrange("p a b -> p (a b)")

        w_loaded = [sem("w_loaded0"), sem("w_loaded1")]
        w_high = sem("w_high")
        w_split = sem("w_split")
        tile_done = sem("tile_done")
        tile_evac = [sem("tile_evac0"), sem("tile_evac1")]
        phase = sem("phase")
        consts_in = sem("consts_in")
        dve_step, act_step, pool_step = sem("dve_step"), sem("act_step"), sem("pool_step")

        counts = {"dve": 0, "act": 0, "phase": {}}

        def dstep(ins):
            counts["dve"] += 1
            ins.then_inc(dve_step, 1)
            nc.vector.wait_ge(dve_step, counts["dve"])

        def astep(ins):
            counts["act"] += 1
            ins.then_inc(act_step, 1)
            nc.scalar.wait_ge(act_step, counts["act"])

        def end_phase(eng, name, wait=True):
            n = counts["phase"].get(name, 0) + 1
            counts["phase"][name] = n
            eng.drain().then_inc(phase, 1)
            if wait:
                eng.wait_ge(phase, 5 * n)

        w_in = A["w_in"][0].rearrange("(k p) n -> p k n", p=P)

        pieces = []
        def cols(o, n=P):
            return lambda dst, eng: eng.dma_start(dst[:, :, 0:n], w_in[:, :, o:o + n])
        for c in range(12):
            pieces.append((cols(O_GQ + c * P), KT))
        def gates_piece(dst, eng):
            eng.dma_start(dst[:, :, 0:2 * GH], w_in[:, :, O_GA:O_GA + 2 * GH]).then_inc(w_loaded[P_SMALL % 2], 16)
            return eng.dma_start(dst[:, :, 8:8 + 3 * NH], w_in[:, :, O_NGATE:O_NGATE + 3 * NH])
        P_SMALL = len(pieces)
        pieces.append((gates_piece, KT))
        P_STAGED = len(pieces)
        staged_cols = ([O_GZ + c * P for c in range(4)] +
                       [o + m * P for m in range(4) for o in (O_SQ, O_SK, O_SV)] +
                       [O_MERGE + c * P for c in range(3 * KT)])
        S_GZ, S_SB, S_GATE = 0, 4, 16
        NST = len(staged_cols)
        for c in staged_cols[:-TB]:
            pieces.append((cols(c), KT))
        P_MERGE = []
        def merge_pieces(name, heads_of_groups=False):
            P_MERGE.append(len(pieces))
            wb = A[name][0]
            for c in range(KT):
                if not heads_of_groups:
                    v = wb.rearrange("(k p) n -> p k n", p=P)
                    pieces.append(((lambda v, c: lambda dst, eng: eng.dma_start(dst[:, 0:4, :], v[:, :, c * P:(c + 1) * P]))(v, c), 4))
                else:
                    def two(c):
                        par = len(pieces) % 2

                        def go(dst, eng):
                            v = wb.rearrange("(g m d) n -> g d m n", g=NG, m=NM)
                            eng.dma_start(dst[0:ND, 0:4, :], v[0, :, :, c * P:(c + 1) * P]).then_inc(w_loaded[par], 16)
                            return eng.dma_start(dst[ND:P, 0:4, :], v[1, :, :, c * P:(c + 1) * P])
                        return go
                    pieces.append((two(c), 4))
        P_NSA = len(pieces)
        nq_v = A["w_in"][0][:, O_NQ:O_NQ + 512].rearrange("(k p) (g m d) -> g m p k d", p=P, g=NG, m=NM)
        for c in range(6):
            pieces.append((cols(O_NKV + c * P), KT))
        def nq_piece(m):
            par = len(pieces) % 2

            def go(dst, eng):
                eng.dma_start(dst[:, :, 0:ND], nq_v[0, m]).then_inc(w_loaded[par], 16)
                return eng.dma_start(dst[:, :, ND:P], nq_v[1, m])
            return go
        for m in range(NM):
            pieces.append((nq_piece(m), KT))
        P_LATE = len(pieces)
        for c in staged_cols[-TB:]:
            pieces.append((cols(c), KT))

        def staged_piece(j):
            return P_STAGED + j if j < NST - TB else P_LATE + j - (NST - TB)
        merge_pieces("w_br_gdn")
        merge_pieces("w_br_nsa", heads_of_groups=True)
        merge_pieces("w_br_sb")
        P_OUT = len(pieces)
        wo_v = A["w_out"][0].rearrange("(k p) n -> p k n", p=P)
        for c in range(KT):
            pieces.append(((lambda c: lambda dst, eng: eng.dma_start(dst[:], wo_v[:, :, c * P:(c + 1) * P]))(c), KT))
        P_MLP = len(pieces)
        two_dma = {P_SMALL} | {P_NSA + 6 + m for m in range(NM)} | {P_MERGE[1] + c for c in range(KT)}
        loaded_at = []
        loaded = [0, 0]
        for p in range(P_MLP):
            loaded[p % 2] += 32 if p in two_dma else 16
            loaded_at.append(loaded[p % 2])
        CH = FF // D
        w1_v = A["w_ff1"][0].rearrange("(k p) (f n) -> f p k n", p=P, n=P)
        w2_v = A["w_ff2"][0].rearrange("(i k p) (c n) -> i c p k n", k=KT, p=P, n=P)

        def load_pieces(sp, lo, hi):
            for p in range(lo, hi):
                if p >= 2:
                    sp.wait_ge(w_split, p - 1)
                pieces[p][0](w_raw[p % 2], sp).then_inc(w_loaded[p % 2], 16)

        def split_pieces(pool, lo, hi):
            for p in range(lo, hi):
                b, k = p % 2, pieces[p][1]
                pool.wait_ge(w_loaded[b], loaded_at[p])
                if p >= 2:
                    pool.wait_ge(tile_done, p - 1)
                nc.gpsimd.tensor_copy(w_hi[b][:, 0:k], w_raw[b][:, 0:k]).then_inc(w_high, 1)
                pool.wait_ge(w_high, p + 1)
                nc.gpsimd.tensor_tensor(w_lo[b][:, 0:k], w_raw[b][:, 0:k], w_hi[b][:, 0:k].bitcast(F32),
                                        ALU.subtract).then_inc(w_split, 1)

        def job(pe, p, rhs_hi, rhs_lo, ktiles=KT, par=None, waits=None):
            b = p % 2 if par is None else par
            dst = 2 * b
            last = None
            for k in range(ktiles):
                if waits:
                    waits(k)
                for w, r, first, end in ((w_hi, rhs_hi, True, False), (w_hi, rhs_lo, False, False),
                                         (w_lo, rhs_hi, False, True)):
                    for h in range(2):
                        last = nc.tensor.matmul(PS[:, dst + h, :], w[b][:, k, :], r[:, k, h * 512:(h + 1) * 512],
                                                start=(k == 0 and first), stop=(k == ktiles - 1 and end))
            last.then_inc(tile_done, 1)

        def run_job(pe, p, rhs_hi=None, rhs_lo=None):
            pe.wait_ge(w_split, p + 1)
            if p >= 2:
                pe.wait_ge(tile_evac[p % 2], p // 2)
            job(pe, p, hT_hi if rhs_hi is None else rhs_hi, hT_lo if rhs_lo is None else rhs_lo, pieces[p][1])

        def evac_done(ins, p):
            ins.then_inc(tile_evac[p % 2], 1)

        xin = [at(f"xin{i}", 136 + 4 * i, [D]) for i in range(2)]
        xs = [at(f"xs{i}", 144 + 4 * i, [D]) for i in range(2)]
        g_pre = at("g_pre", 152, [D])
        junk0 = at("junk0", 156, [D])
        ss0 = small[:, 0:TB]
        rt0 = small[:, TB:2 * TB]
        rr0 = small[:, 2 * TB:3 * TB]
        eps_t = small[:, 1151:1152]
        x_v = A["x"][0].rearrange("(t p) d -> t p d", p=P)
        x_in = [sem("x_in0"), sem("x_in1")]
        x_ss, x_norm, x_tr, x_hi, x_lo, eps_set = (sem(n) for n in (
            "x_ss", "x_norm", "x_tr", "x_hi", "x_lo", "eps_set"))

        def bc(ap, n):
            return ap.rearrange("(a n) -> a n", a=1).to_broadcast([P, n])

        def sp_phase0(sp):
            sp.dma_start(ident[:], A["c_ident"]).then_inc(consts_in, 16)
            sp.dma_start(g_pre[:], bc(A["g_mix_pre"][0], D)).then_inc(consts_in, 16)
            for t in range(TB):
                if t >= 2:
                    sp.wait_ge(x_norm, t - 1)
                sp.dma_start(xin[t % 2][:], x_v[t]).then_inc(x_in[t % 2], 16)

        def act_phase0(act):
            act.wait_ge(eps_set, 1)
            for t in range(TB):
                act.wait_ge(x_in[t % 2], 16 * (t // 2 + 1))
                astep(nc.scalar.activation(junk0[:], xin[t % 2][:], ACT.Square, accum_out=ss0[:, t:t + 1]))
                nc.scalar.activation(rt0[:, t:t + 1], ss0[:, t:t + 1], ACT.Sqrt, scale=1.0 / D,
                                     bias=eps_t).then_inc(x_ss, 1)
                if t >= 1:
                    act_split_x(act, t - 1)
            act_split_x(act, TB - 1)

        def act_split_x(act, t):
            act.wait_ge(x_tr, t + 1)
            nc.scalar.activation(hT_hi[:, :, t * P:(t + 1) * P],
                                 pair(t % 2).rearrange("p (k n) -> p k n", n=P), ACT.Copy).then_inc(x_hi, 1)

        def dve_phase0(dve):
            nc.vector.memset(eps_t, EPS).then_inc(eps_set, 1)
            nc.vector.memset(small[:, 1150:1151], 0.0)
            dve.wait_ge(consts_in, 32)
            for t in range(TB + 1):
                if t < TB:
                    dve.wait_ge(x_ss, t + 1)
                    dstep(nc.vector.reciprocal(rr0[:, t:t + 1], rt0[:, t:t + 1]))
                    if t >= 2:
                        dve.wait_ge(x_tr, t - 1)
                    nc.vector.scalar_tensor_tensor(out=xs[t % 2][:], in0=xin[t % 2][:], scalar=rr0[:, t:t + 1],
                                                   in1=g_pre[:], op0=ALU.mult, op1=ALU.mult).then_inc(x_norm, 1)
                if t >= 1:
                    dve_split_x(dve, t - 1)

        def dve_split_x(dve, t):
            dve.wait_ge(x_hi, t + 1)
            s = slice(t * P, (t + 1) * P)
            nc.vector.tensor_tensor(hT_lo[:, :, s], pair(t % 2).rearrange("p (k n) -> p k n", n=P),
                                    hT_hi[:, :, s].bitcast(F32), ALU.subtract).then_inc(x_lo, 1)

        def pe_phase0(pe):
            pe.wait_ge(consts_in, 32)
            for t in range(TB):
                pe.wait_ge(x_norm, t + 1)
                if t >= 2:
                    pe.wait_ge(x_lo, t - 1)
                for k in range(KT):
                    last = nc.tensor.transpose(PS[:, 2 * (t % 2) + k // 4, (k % 4) * P:(k % 4 + 1) * P],
                                               xs[t % 2][:, k * P:(k + 1) * P], ident[:])
                last.then_inc(x_tr, 1)

        cT = at("cT", 136, [12, T])
        xpad = [at(f"xpad{i}", 88 + 5 * i, [T + 3]) for i in range(2)]
        acc = [at(f"acc{i}", 98 + 4 * i, [T]) for i in range(2)]
        abT = at("abT", 106, [T])
        cw_in = at("cw_in", 110, [P])
        sq = [at(f"sq{i}", 111 + 4 * i, [T]) for i in range(2)]
        slot = lambda name, i, shape, n=1: at(name, 88 + 2 * i if i < 16 else 184 + 2 * (i - 16), shape)
        qn, kn, kb, kbg = (slot(n, i, [GH, P]) for i, n in enumerate(("qn", "kn", "kb", "kbg")))
        kd, vb = slot("kd", 4, [GH, P]), slot("vb", 5, [GH, P])
        qkb = slot("qkb", 6, [GH, 2 * P])
        knT, DT, DsT, attnT, AT, X, Z = (slot(n, 8 + i, [GH, P]) for i, n in enumerate(
            ("knT", "DT", "DsT", "attnT", "AT", "X", "Z")))
        Y, U, uu = slot("Y", 0, [GH, P]), slot("U", 1, [GH, P]), slot("uu", 2, [GH, P])
        trig = DsT
        S, vnew, qS = slot("S", 15, [GH, P]), slot("vnew", 19, [GH, P]), slot("qS", 20, [GH, P])
        staging = at("staging", 184, [T])
        staged = nc.dram_tensor("staged", (NST, P, T), F32).ap()
        o_all = at("o_all", 120, [TB, GH, P])
        zT = at("zT", 136, [GH, T])
        y_hi, y_lo = at("y_hi", 152, [4, T], F32R), at("y_lo", 168, [4, T], F32R)
        y_his = [y_hi, at("y_hi_b", 0, [4, T], F32R), y_hi]
        y_los = [y_lo, at("y_lo_b", 16, [4, T], F32R), y_lo]
        ytmp = [at(f"ytmp{i}", 184 + 4 * i, [T]) for i in range(2)]
        osq = at("osq", 88, [TB, GH, P])

        def scal(o, n=TB * GH):
            return small[:, o:o + n]
        abn = scal(24, 256).rearrange("p (t c) -> p t c", c=32)
        s4 = lambda o: scal(o).rearrange("p (t h) -> p t h", h=GH)
        beta, graw, gcs, dgl, eg, ekd, rq, skb, skbg, skd, egl0, egl1, sp_a, sp_b, sp_c = (
            s4(280 + 32 * i) for i in range(15))
        rr = scal(760, 64).rearrange("p (t c) -> p t c", c=8)
        alog, dtb = scal(824, 4), scal(828, 4)
        normg = scal(832, 1)
        cw = scal(840, 48)
        nsa_gate = scal(888, 192).rearrange("p (t c) -> p t c", c=24)
        oss = s4(280)
        ort = s4(312)

        GI = {n: i * P for i, n in enumerate(("tri", "dneg", "strict", "l0", "l1", "l2", "l3", "l4", "l5",
                                              "chunk", "ones", "c0", "c1"))}
        gc = lambda n: consts[:, GI[n]:GI[n] + P]
        overh = lambda ap: ap.unsqueeze(1).to_broadcast([P, GH, P])
        overd = lambda ap: ap.unsqueeze(2).to_broadcast([P, GH, P])

        (g_small_in, cw_tr, cw_ok, pads_ok, conv_sum, conv_act, ab_tr, ab_tok) = (sem(n) for n in (
            "g_small_in", "cw_tr", "cw_ok", "pads_ok", "conv_sum", "conv_act", "ab_tr", "ab_tok"))
        gs_a, gs_d, gs_p, sq_ok, ss_ok = (sem(n) for n in ("gs_a", "gs_d", "gs_p", "sq_ok", "ss_ok"))

        def sp_gdn(sp):
            sp.dma_start(consts[:], A["c_gdn"]).then_inc(g_small_in, 16)
            sp.dma_start(cw_in[0:48, :], A["gdn_conv_w"][0].rearrange("i (c p) -> (i c) p", p=P)).then_inc(g_small_in, 16)
            sp.dma_start(alog, bc(A["gdn_a_log"][0], GH)).then_inc(g_small_in, 16)
            sp.dma_start(dtb, bc(A["gdn_dt_bias"][0], GH)).then_inc(g_small_in, 16)
            sp.dma_start(normg, A["gdn_norm_g"][0].rearrange("(p a) -> p a", a=1)).then_inc(g_small_in, 16)
            load_pieces(sp, 0, P_SMALL + 1)

        def pool_gdn(pool):
            split_pieces(pool, 0, P_SMALL + 1)

        def pe_gdn(pe):
            pe.wait_ge(g_small_in, 80)
            nc.tensor.transpose(PS[:, 4, 0:48], cw_in[0:48, :], ident[0:48, 0:48]).then_inc(cw_tr, 1)
            for p in range(P_SMALL + 1):
                run_job(pe, p)
            pe.wait_ge(tile_evac[P_SMALL % 2], P_SMALL // 2 + 1)
            pe.wait_ge(cw_ok, 1)
            for t in range(TB):
                last = nc.tensor.transpose(PS[:, 5, t * 32:t * 32 + 32], abT[0:32, t * P:(t + 1) * P],
                                           ident[0:32, 0:32])
            last.then_inc(ab_tr, 1)
            pe.wait_ge(gs_d, 3)
            for k, n in enumerate(("tri", "chunk", "c0", "c1")):
                last = nc.tensor.matmul(PS[:, 7, 32 * k:32 * k + 32], gc(n), scal(280 + 32), start=True, stop=True)
            last.then_inc(gs_p, 1)
            for c in range(8):
                pe.wait_ge(sq_ok, c + 1)
                for t in range(TB):
                    last = nc.tensor.matmul(PS[:, 6, t * 8 + c:t * 8 + c + 1], sq[c % 2][:, t * P:(t + 1) * P],
                                            gc("ones")[:, 0:1], start=True, stop=True)
                last.then_inc(ss_ok, 1)

        def act_gdn(act):
            for c in range(12 + 1):
                if c < 12:
                    act.wait_ge(tile_done, c + 1)
                    if c == 0:
                        act.wait_ge(pads_ok, 2)
                    if c >= 2:
                        act.wait_ge(conv_sum, c - 1)
                    evac_done(nc.scalar.activation(xpad[c % 2][:, 3:], pair(c % 2), ACT.Copy), c)
                if c >= 1:
                    act.wait_ge(conv_sum, c)
                    nc.scalar.activation(cT[:, c - 1], acc[(c - 1) % 2][:], ACT.Silu).then_inc(conv_act, 1)
            act.wait_ge(tile_done, P_SMALL + 1)
            evac_done(nc.scalar.activation(abT[0:32, :], pair(P_SMALL % 2)[0:32, :], ACT.Copy), P_SMALL)
            act.wait_ge(ab_tok, 1)
            astep(nc.scalar.activation(beta, abn[:, :, 4:8], ACT.Sigmoid))
            astep(nc.scalar.activation(nsa_gate, abn[:, :, 8:32], ACT.Sigmoid))
            act.wait_ge(gs_d, 1)
            astep(nc.scalar.activation(sp_b, sp_a, ACT.Abs))
            astep(nc.scalar.activation(sp_b, sp_b, ACT.Exp, scale=-1.0))
            astep(nc.scalar.activation(sp_b, sp_b, ACT.Ln, bias=1.0))
            nc.scalar.activation(alog, alog, ACT.Exp).then_inc(gs_a, 1)
            act.wait_ge(gs_p, 1)
            psg = lambda k: PS[:, 7, 32 * k:32 * k + 32].rearrange("p (t h) -> p t h", h=GH)
            nc.scalar.activation(eg, psg(0), ACT.Exp)
            nc.scalar.activation(egl0, psg(2), ACT.Exp)
            nc.scalar.activation(egl1, psg(3), ACT.Exp).then_inc(gs_a, 1)
            act.wait_ge(gs_d, 5)
            nc.scalar.activation(ekd, dgl, ACT.Exp).then_inc(gs_a, 1)
            for c in range(8):
                act.wait_ge(conv_act, c + 1)
                if c >= 2:
                    act.wait_ge(ss_ok, c - 1)
                nc.scalar.activation(sq[c % 2][:], cT[:, c], ACT.Square).then_inc(sq_ok, 1)
            act.wait_ge(ss_ok, 8)
            nc.scalar.activation(scal(760, 64), PS[:, 6, 0:64], ACT.Sqrt, bias=eps_t).then_inc(gs_a, 1)

        def dve_gdn(dve):
            nc.vector.memset(xpad[0][:, 0:3], 0.0).then_inc(pads_ok, 1)
            nc.vector.memset(xpad[1][:, 0:3], 0.0).then_inc(pads_ok, 1)
            dve.wait_ge(cw_tr, 1)
            nc.vector.tensor_copy(cw, PS[:, 4, 0:48]).then_inc(cw_ok, 1)
            dve.wait_ge(cw_ok, 1)
            for c in range(12):
                x, a = xpad[c % 2], acc[c % 2]
                dve.wait_ge(tile_evac[c % 2], c // 2 + 1)
                if c >= 2:
                    dve.wait_ge(conv_act, c - 1)
                w = lambda i: cw[:, i * 12 + c:i * 12 + c + 1]
                dstep(nc.vector.tensor_scalar(a[:], x[:, 3:T + 3], w(3), None, ALU.mult))
                for i in (2, 1):
                    dstep(nc.vector.scalar_tensor_tensor(out=a[:], in0=x[:, i:T + i], scalar=w(i), in1=a[:],
                                                         op0=ALU.mult, op1=ALU.add))
                nc.vector.scalar_tensor_tensor(out=a[:], in0=x[:, 0:T], scalar=w(0), in1=a[:],
                                               op0=ALU.mult, op1=ALU.add).then_inc(conv_sum, 1)
            dve.wait_ge(ab_tr, 1)
            nc.vector.tensor_copy(scal(24, 256), PS[:, 5, 0:256]).then_inc(ab_tok, 1)
            dve.wait_ge(ab_tok, 1)
            b8 = lambda ap: ap.unsqueeze(1).to_broadcast([P, TB, GH])
            dve.wait_ge(g_small_in, 80)
            nc.vector.tensor_tensor(sp_a, abn[:, :, 0:4], b8(dtb), ALU.add).then_inc(gs_d, 1)
            dve.wait_ge(gs_a, 1)
            dve.wait_ge(gs_d, 1)
            nc.vector.scalar_tensor_tensor(out=sp_c, in0=sp_a, scalar=0.0, in1=sp_b, op0=ALU.max,
                                           op1=ALU.add).then_inc(gs_d, 1)
            dve.wait_ge(gs_d, 2)
            nc.vector.scalar_tensor_tensor(out=graw, in0=sp_c, scalar=-1.0, in1=b8(alog), op0=ALU.mult,
                                           op1=ALU.mult).then_inc(gs_d, 1)
            dve.wait_ge(gs_p, 1)
            dve.wait_ge(gs_a, 2)
            psg = lambda k: PS[:, 7, 32 * k:32 * k + 32].rearrange("p (t h) -> p t h", h=GH)
            nc.vector.tensor_copy(gcs, psg(0)).then_inc(gs_d, 1)
            dve.wait_ge(gs_d, 4)
            nc.vector.tensor_tensor(dgl, psg(1), gcs, ALU.subtract).then_inc(gs_d, 1)
            dve.wait_ge(gs_a, 4)
            dstep(nc.vector.reciprocal(scal(760, 64), scal(760, 64)))
            dstep(nc.vector.tensor_scalar(rq, rr[:, :, 0:4], float(GD) ** -0.5, None, ALU.mult))
            dstep(nc.vector.tensor_tensor(skb, rr[:, :, 4:8], beta, ALU.mult))
            dstep(nc.vector.tensor_tensor(skbg, skb, eg, ALU.mult))
            dstep(nc.vector.tensor_tensor(skd, rr[:, :, 4:8], ekd, ALU.mult))

        LV = range(1, 6)
        PE_STEPS = ["tok", "tr", "gram", "xz"] + [n for l in LV for n in (f"y{l}", f"z{l}", f"t{l}")][:-1] + [
            "uw", "ws0", "st0", "ws1", "st1", "oi"]
        GP = Steps(sem("gdn_pe"), PE_STEPS)
        GA = Steps(sem("gdn_act"), ["trs", "exp", "x0"] + [n for l in LV for n in (f"y{l}", f"x{l}")][:-1] +
                   ["w", "qs0", "qs1"])
        GV = Steps(sem("gdn_dve"), ["scaled", "trig", "dm", "dg", "ds", "attn", "at", "u0", "z0", "u1"] +
                   [n for l in LV for n in (f"u{l + 1}", f"z{l}") if n != "u6"] +
                   ["u", "v0", "sd0", "s0", "v1", "sd1", "s1", "qe", "o"])
        JB = NST // TB - 1
        NSG = JB * TB
        NS = len(PE_STEPS)
        kt_done = [JB * KT * i // NS for i in range(NS + 1)]
        ends_at = {min(i for i in range(NS) if kt_done[i + 1] >= KT * (j + 1)): j for j in range(JB)}
        stored = sem("stored")

        def gstep(steps, ins):
            ins.then_inc(steps.sem, 1)

        def bank4(k):
            return PS[:, k, :].rearrange("p (h n) -> p h n", h=GH)

        def chunks(ap):
            return ap.rearrange("p h (c n) -> p h c n", n=GC)[:, :, 0::3]

        def store_staged(sp, first, last, buf, among=lambda j: None):
            for j in range(first, last + 4):
                if j >= first + 4:
                    p = staged_piece(j - 4)
                    sp.wait_ge(tile_evac[p % 2], p // 2 + 1)
                    sp.dma_start(staged[j - 4], buf[:]).then_inc(stored, 16)
                among(j - first)
                if j < last:
                    q = staged_piece(j)
                    load_pieces(sp, q, q + 1)
            sp.wait_ge(stored, 16 * last)

        def sp_gdn_blocks(sp):
            store_staged(sp, 0, NSG, staging)

        def pool_gdn_blocks(pool):
            split_pieces(pool, P_STAGED, P_STAGED + NSG)

        def behind(pe, p, k, banks):
            b = p % 2
            if k == 0:
                pe.wait_ge(w_split, p + 1)
                pe.wait_ge(tile_evac[(p - 1) % 2], (p - 1) // 2 + 1)
            for w, r, first, end in ((w_hi, hT_hi, True, False), (w_hi, hT_lo, False, False),
                                     (w_lo, hT_hi, False, True)):
                for h in range(2):
                    last = nc.tensor.matmul(PS[:, banks + h, :], w[b][:, k, :], r[:, k, h * 512:(h + 1) * 512],
                                            start=(k == 0 and first), stop=(k == KT - 1 and end))
            if k == KT - 1:
                last.then_inc(tile_done, 1)

        def pe_behind(pe, t, name):
            i = PE_STEPS.index(name)
            for kk in range(kt_done[i], kt_done[i + 1]):
                j, k = divmod(kk, KT)
                behind(pe, P_STAGED + t * JB + j, k, 6)

        def act_behind(act, t, done, upto):
            for i in range(done, upto):
                if i in ends_at:
                    j = t * JB + ends_at[i]
                    p = P_STAGED + j
                    act.wait_ge(tile_done, p + 1)
                    if j:
                        act.wait_ge(stored, 16 * j)
                    q = S_SB <= j < S_GATE and (j - S_SB) % 3 == 0
                    evac_done(nc.scalar.activation(staging[:], pair(3), ACT.Copy,
                                                   scale=float(SD) ** -0.5 if q else 1.0), p)

        def pe_gdn_blocks(pe):
            for t in range(TB):
                s = slice(t * P, (t + 1) * P)

                def step(name, ins):
                    gstep(GP, ins)
                    pe_behind(pe, t, name)
                if t:
                    GV.wait(pe, t - 1, "o")
                for j in range(3):
                    for h in range(GH):
                        last = nc.tensor.transpose(bank4(j)[:, h], cT[:, 4 * j + h, s], ident[:])
                step("tok", last)
                GV.wait(pe, t, "scaled")
                for j, src in enumerate((qn, kn, kb)):
                    for h in range(GH):
                        last = nc.tensor.transpose(bank4(3 + j)[:, h], src[:, h], ident[:])
                step("tr", last)
                GV.wait(pe, t, "trig")
                nc.tensor.matmul(PS[:, 0, :], gc("ones"), trig[:].rearrange("p h n -> p (h n)"), start=True, stop=True)
                GA.wait(pe, t, "trs")
                for h in range(GH):
                    last = nc.tensor.matmul(PS[:, 1 + h // 2, (h % 2) * 256:(h % 2) * 256 + 256], knT[:, h],
                                            qkb[:, h], start=True, stop=True)
                step("gram", last)
                GV.wait(pe, t, "z0")
                for h in range(GH):
                    last = nc.tensor.transpose(bank4(1)[:, h], Z[:, h], ident[:])
                step("xz", last)
                for l in LV:
                    GV.wait(pe, t, f"u{l}")
                    GA.wait(pe, t, f"x{l - 1}")
                    for h in range(GH):
                        last = nc.tensor.matmul(bank4(2)[:, h], U[:, h], X[:, h], start=True, stop=True)
                    step(f"y{l}", last)
                    GA.wait(pe, t, f"y{l}")
                    for h in range(GH):
                        last = nc.tensor.matmul(bank4(4)[:, h], Y[:, h], Z[:, h], start=True, stop=True)
                    step(f"z{l}", last)
                    GV.wait(pe, t, f"z{l}")
                    if l < 5:
                        for h in range(GH):
                            last = nc.tensor.transpose(bank4(3)[:, h], Z[:, h], ident[:])
                        step(f"t{l}", last)
                for h in range(GH):
                    nc.tensor.matmul(bank4(5)[:, h], Z[:, h], vb[:, h], start=True, stop=True)
                for h in range(GH):
                    last = nc.tensor.matmul(bank4(0)[:, h], kbg[:, h], Z[:, h], start=True, stop=True)
                step("uw", last)
                for c in range(2):
                    r = slice(GC * c, GC * c + GC)
                    GA.wait(pe, t, "w" if c == 0 else "qs0")
                    GV.wait(pe, t, "u" if c == 0 else "s0")
                    for h in range(GH):
                        last = nc.tensor.matmul(bank4(1)[:, h], qkb[:, h, c * P:(c + 1) * P], S[:, h], start=True, stop=True)
                    step(f"ws{c}", last)
                    GV.wait(pe, t, f"v{c}")
                    for h in range(GH):
                        last = nc.tensor.matmul(bank4(2)[:, h], kd[r, h], vnew[r, h], start=True, stop=True)
                    step(f"st{c}", last)
                for h in range(GH):
                    last = nc.tensor.matmul(bank4(3)[:, h], attnT[:, h], vnew[:, h], start=True, stop=True)
                step("oi", last)

        def act_gdn_blocks(act):
            for t in range(TB):
                seen = [0]

                def wait(name):
                    i = PE_STEPS.index(name)
                    act_behind(act, t, seen[0], i)
                    seen[0] = i
                    GP.wait(act, t, name)
                wait("tr")
                nc.scalar.activation(qkb[:, :, GC:3 * GC], bank4(3), ACT.Copy)
                nc.scalar.activation(chunks(qkb[:]), bank4(5).rearrange("p h (c n) -> p h c n", n=GC), ACT.Copy)
                gstep(GA, nc.scalar.activation(knT[:], bank4(4), ACT.Copy))
                GV.wait(act, t, "dg")
                gstep(GA, nc.scalar.activation(DT[:], DT[:], ACT.Exp))
                wait("xz")
                gstep(GA, nc.scalar.activation(X[:], bank4(1), ACT.Copy))
                for l in LV:
                    wait(f"y{l}")
                    gstep(GA, nc.scalar.activation(Y[:], bank4(2), ACT.Copy))
                    if l < 5:
                        wait(f"t{l}")
                        gstep(GA, nc.scalar.activation(X[:], bank4(3), ACT.Copy))
                wait("uw")
                gstep(GA, nc.scalar.activation(chunks(qkb[:]), bank4(0).rearrange("p h (c n) -> p h c n", n=GC),
                                               ACT.Copy))
                for c in range(2):
                    wait(f"ws{c}")
                    GV.wait(act, t, f"v{c}")
                    gstep(GA, nc.scalar.activation(qS[GC * c:GC * c + GC], bank4(1)[GC * (1 - c):GC * (1 - c) + GC],
                                                   ACT.Copy))
                act_behind(act, t, seen[0], NS)

        def dve_gdn_blocks(dve):
            tt = nc.vector.tensor_tensor
            dstep(nc.vector.memset(S[:], 0.0))
            for t in range(TB):
                if t:
                    GV.wait(dve, t - 1, "o")
                GP.wait(dve, t, "tok")
                rk = rr[:, t, 4:8]
                tt(qn[:], bank4(0), overd(rq[:, t]), ALU.mult)
                tt(kn[:], bank4(1), overd(rk), ALU.mult)
                tt(kb[:], bank4(1), overd(skb[:, t]), ALU.mult)
                tt(kbg[:], bank4(1), overd(skbg[:, t]), ALU.mult)
                tt(kd[:], bank4(1), overd(skd[:, t]), ALU.mult)
                gstep(GV, tt(vb[:], bank4(2), overd(beta[:, t]), ALU.mult))
                gstep(GV, tt(trig[:], overh(gc("tri")), overd(graw[:, t]), ALU.mult))
                GP.wait(dve, t, "gram")
                gstep(GV, tt(DT[:], bank4(0), overh(gc("dneg")), ALU.add))
                GV.wait(dve, t, "dm")
                gstep(GV, tt(DT[:], DT[:], overd(gcs[:, t]), ALU.subtract))
                GA.wait(dve, t, "exp")
                gstep(GV, tt(DsT[:], DT[:], overh(gc("strict")), ALU.mult))
                gram = PS[:, 1:3, :].rearrange("p a (b n) -> p (a b) n", b=2)
                gstep(GV, tt(attnT[:], gram[:, :, GC:3 * GC], DT[:], ALU.mult))
                GV.wait(dve, t, "ds")
                byc = lambda ap: ap.rearrange("p h (c n) -> p h c n", n=GC)
                gstep(GV, tt(byc(AT[:]), chunks(gram), byc(DsT[:]), ALU.mult))
                GV.wait(dve, t, "at")
                gstep(GV, tt(U[:], AT[:], overh(gc("l0")), ALU.mult))
                GV.wait(dve, t, "u0")
                gstep(GV, tt(Z[:], overh(ident[:]), U[:], ALU.subtract))
                GV.wait(dve, t, "z0")
                gstep(GV, tt(U[:], AT[:], overh(gc("l1")), ALU.mult))
                for l in LV:
                    if l < 5:
                        GP.wait(dve, t, f"y{l}")
                        gstep(GV, tt(U[:], AT[:], overh(gc(f"l{l + 1}")), ALU.mult))
                    GP.wait(dve, t, f"z{l}")
                    gstep(GV, tt(Z[:], Z[:], bank4(4), ALU.subtract))
                    GV.wait(dve, t, f"z{l}")
                GP.wait(dve, t, "uw")
                gstep(GV, nc.vector.tensor_copy(uu[:], bank4(5)))
                GV.wait(dve, t, "u")
                for c in range(2):
                    r = slice(GC * c, GC * c + GC)
                    GP.wait(dve, t, f"ws{c}")
                    gstep(GV, tt(vnew[r], uu[r], bank4(1)[r], ALU.subtract))
                    gstep(GV, tt(S[:], S[:], overd((egl0, egl1)[c][:, t]), ALU.mult))
                    GP.wait(dve, t, f"st{c}")
                    GV.wait(dve, t, f"sd{c}")
                    gstep(GV, tt(S[:], S[:], bank4(2), ALU.add))
                    GV.wait(dve, t, f"s{c}")
                GA.wait(dve, t, "qs1")
                gstep(GV, tt(qS[:], qS[:], overd(eg[:, t]), ALU.mult))
                GP.wait(dve, t, "oi")
                GV.wait(dve, t, "qe")
                gstep(GV, tt(o_all[:, t], qS[:], bank4(3), ALU.add))

        o_ss, o_r, o_nrm, o_tr, y_mul, y_hi_ok, y_lo_ok = (sem(n) for n in (
            "o_ss", "o_r", "o_nrm", "o_tr", "y_mul", "y_hi_ok", "y_lo_ok"))

        z_in, z_act = sem("z_in"), sem("z_act")
        y0_dram = nc.dram_tensor("y0_scratch", (GH, P, T), F32).ap()
        y0_out = [sem("y0_out0"), sem("y0_out1")]
        y0_in = sem("y0_in")
        y0T = at("y0T", 0, [GH, T])

        def sp_gdn_out(sp):
            for h in range(GH):
                sp.dma_start(zT[:, h], staged[S_GZ + h]).then_inc(z_in, 16)
            load_pieces(sp, P_NSA, P_NSA + 2)
            for h in range(GH):
                sp.wait_ge(y_mul, h + 1)
                sp.dma_start(y0_dram[h], ytmp[h % 2][:]).then_inc(y0_out[h % 2], 16)
            for i in range(2):
                sp.wait_ge(y0_out[i], 16 * GH // 2)

        def pool_gdn_out(pool):
            split_pieces(pool, P_NSA, P_NSA + 2)

        def pe_gdn_out(pe):
            pe.wait_ge(o_nrm, 1)
            for h in range(GH):
                if h >= 2:
                    pe.wait_ge(y_mul, h - 1)
                for t in range(TB):
                    last = nc.tensor.transpose(PS[:, 4 + 2 * (h % 2) + t // 4, (t % 4) * P:(t % 4 + 1) * P],
                                               o_all[:, t, h], ident[:])
                last.then_inc(o_tr, 1)

        def split_y(act, b, k, src):
            nc.scalar.activation(y_his[b][:, k], src, ACT.Copy).then_inc(y_hi_ok, 1)

        def act_gdn_out(act):
            nc.scalar.activation(osq[:], o_all[:], ACT.Square).then_inc(o_ss, 1)
            act.wait_ge(o_r, 1)
            nc.scalar.activation(ort, oss, ACT.Sqrt, scale=1.0 / GD, bias=eps_t).then_inc(o_ss, 1)
            for h in range(GH):
                act.wait_ge(z_in, 16 * GH)
                nc.scalar.activation(zT[:, h], zT[:, h], ACT.Silu).then_inc(z_act, 1)

        def dve_gdn_out(dve):
            dve.wait_ge(o_ss, 1)
            nc.vector.tensor_reduce(oss, osq[:], AX_X, ALU.add).then_inc(o_r, 1)
            dve.wait_ge(o_ss, 2)
            dstep(nc.vector.reciprocal(ort, ort))
            nc.vector.tensor_tensor(o_all[:], o_all[:], ort.unsqueeze(3).to_broadcast([P, TB, GH, P]),
                                    ALU.mult).then_inc(o_nrm, 1)
            for h in range(GH):
                dve.wait_ge(o_tr, h + 1)
                dve.wait_ge(z_act, h + 1)
                if h >= 2:
                    dve.wait_ge(y0_out[h % 2], 16)
                nc.vector.scalar_tensor_tensor(out=ytmp[h % 2][:], in0=pair(2 + h % 2), scalar=normg, in1=zT[:, h],
                                               op0=ALU.mult, op1=ALU.mult).then_inc(y_mul, 1)

        def sp_y0(sp):
            for h in range(GH):
                sp.dma_start(y0T[:, h], y0_dram[h]).then_inc(y0_in, 16)

        def act_y0(act):
            act.wait_ge(y0_in, 16 * GH)
            for h in range(GH):
                split_y(act, 0, h, y0T[:, h])

        def dve_low_y(dve, b, k, src):
            dve.wait_ge(y_hi_ok, 4 * b + k + 1)
            nc.vector.tensor_tensor(y_los[b][:, k], src, y_his[b][:, k].bitcast(F32), ALU.subtract).then_inc(y_lo_ok, 1)

        def dve_y0(dve):
            for h in range(GH):
                dve_low_y(dve, 0, h, y0T[:, h])

        G = [at(f"G{i}", o, [T]) for i, o in enumerate((136, 140, 148))]
        mtmp = at("mtmp", 144, [T])
        gate_in = [sem(f"gate_in{i}") for i in range(3)]
        gate_ok, merged = sem("gate_ok"), sem("merged")

        def sp_merge(sp, b):
            for c in range(KT):
                n = b * KT + c
                load_pieces(sp, P_MERGE[b] + c, P_MERGE[b] + c + 1)
                if n >= 3:
                    sp.wait_ge(merged, n - 2)
                sp.dma_start(G[n % 3][:], staged[S_GATE + n]).then_inc(gate_in[n % 3], 16)

        def pool_merge(pool, b):
            split_pieces(pool, P_MERGE[b], P_MERGE[b] + KT)

        def pe_merge(pe, b):
            for c in range(KT):
                run_job(pe, P_MERGE[b] + c, y_his[b], y_los[b])
                if b == 0 and c < NM:
                    pe_turn_y(pe, c)

        def act_merge(act, b):
            for c in range(KT):
                n = b * KT + c
                act.wait_ge(gate_in[n % 3], 16 * (n // 3 + 1))
                nc.scalar.activation(G[n % 3][:], G[n % 3][:], ACT.Sigmoid).then_inc(gate_ok, 1)
                if b == 0 and 1 <= c <= NM:
                    act.wait_ge(ny_tr, c)
                    split_y(act, 1, c - 1, pair(2 + (c - 1) % 2))
                if b == 1 and c < 4:
                    split_y(act, 2, c, osT[:, c])
                if b == 2 and c:
                    act_split_m(act, c - 1)
            if b == 2:
                act_split_m(act, KT - 1)

        def dve_merge(dve, b):
            for c in range(KT):
                p, n = P_MERGE[b] + c, b * KT + c
                dve.wait_ge(tile_done, p + 1)
                dve.wait_ge(gate_ok, n + 1)
                dst = mT[:, c] if b == 0 else mtmp[:]
                evac_done(nc.vector.tensor_tensor(dst, pair(p % 2), G[n % 3][:], ALU.mult), p)
                dve.wait_ge(tile_evac[p % 2], p // 2 + 1)
                if b == 0:
                    nc.vector.tensor_copy(mtmp[:, 0:1], mT[:, c, 0:1]).then_inc(merged, 1)
                else:
                    nc.vector.tensor_tensor(mT[:, c], mT[:, c], mtmp[:], ALU.add).then_inc(merged, 1)
                dve.wait_ge(merged, n + 1)
                if b == 0 and 2 <= c < NM + 2:
                    dve_low_y(dve, 1, c - 2, pair(2 + c % 2))
                if b == 1 and c < 4:
                    dve_low_y(dve, 2, c, osT[:, c])
                if b == 2 and c:
                    dve_split_m(dve, c - 1)
            if b == 2:
                dve_split_m(dve, KT - 1)
        sq_hl = [at(f"sq_hl{i}", 4 * i, [T], F32R) for i in range(2)]
        sk_hi = [at(f"sk_hi{i}", 8 + 4 * i, [T], F32R) for i in range(2)]
        sk_lo = [at(f"sk_lo{i}", 16 + 4 * i, [T], F32R) for i in range(2)]
        sv_tok = at("sv_tok", 88, [4, TB, P])
        osT = at("osT", 40, [4, T])
        twice = [at(f"twice{i}", 56 + 4 * i, [T]) for i in range(2)]
        svT = [at(f"svT{i}", 110 + 4 * i, [T]) for i in range(2)]
        sbz = [at(f"sbz{i}", o, [T]) for i, o in enumerate((72, 76, 80, 199.5))]
        sbl = [at(f"sbl{i}", o, [T]) for i, o in enumerate((84, 203.5))]
        cum = [at(f"cum{i}", o, [T + 8]) for i, o in enumerate((104, 32))]
        spT = [at(f"spT{i}", 24 + 4 * i, [TB, P]) for i in range(2)]
        sneg_in = at("sneg_in", 190.5, [P])
        ident_r, sneg = at("ident_r", 191, [P], F32R), at("sneg", 191.5, [P], F32R)
        ntot = scal(1092, 4)
        sb_in, cum0, sv_tr, sv_ok, mask_r = (sem(n) for n in ("sb_in", "cum0", "sv_tr", "sv_ok", "mask_r"))
        sv_in = [sem("sv_in0"), sem("sv_in1")]
        SB = Stages(sem, "sb", ["z", "copy", "abs", "exp", "log", "softplus", "prefix", "total", "added", "weights",
                                "turned", "copied", "out", "kept"])
        SU = 4 * TB * 2

        def sb_unit(u):
            head, t = divmod(u, TB)
            return head // 2, head % 2, t, t + 1

        def sp_sb_values(sp, m):
            if m >= 2:
                sp.wait_ge(sv_tr, m - 1)
            sp.dma_start(svT[m % 2][:], staged[S_SB + 3 * m + 2]).then_inc(sv_in[m % 2], 16)

        def pe_sb_values(pe, m):
            pe.wait_ge(sv_in[m % 2], 16 * (m // 2 + 1))
            if m:
                pe.wait_ge(sv_ok, m)
            for t in range(TB):
                last = nc.tensor.transpose(pair(1)[:, t * P:(t + 1) * P], svT[m % 2][:, t * P:(t + 1) * P],
                                           ident[:])
            last.then_inc(sv_tr, 1)

        def dve_sb_values(dve, m):
            dve.wait_ge(sv_tr, m + 1)
            nc.vector.tensor_copy(sv_tok[:, m].rearrange("p t n -> p (t n)"), pair(1)).then_inc(sv_ok, 1)

        QT = at("QT", 136, [NM, T])
        kslc, kwin = at("kslc", 152, [T]), at("kwin", 156, [T])
        vslc, vwin = at("vslc", 160, [TB, P]), at("vwin", 164, [TB, P])
        cmpT = [at("kcmpT", 168, [T]), at("vcmpT", 172, [T])]
        vT = [at(f"vT{i}", 176 + 4 * i, [T]) for i in range(2)]
        window = at("window", 184, [CL, 64])
        wcmp = at("wcmp", 120, [CL, P])
        pos_in = at("pos_in", 192, [2, P])
        posT = at("posT", 193, [2, CL])
        kcT, vcT = at("kcT", 205.5, [64]), at("vcT", 205.75, [2, 64])
        vc = at("vc", 206.25, [P])
        P4 = at("P4", 206.75, [NG, 68])
        msel_all = at("msel_all", 192, [TB, NG, NSEL])
        score = at("score", 207.40625, [NG, NSEL])
        maskw = at("maskw", 188, [WT, P])
        maskg = at("maskg", 168, [2, T])
        q_hl = [at(f"q_hl{m}", 136 + 4 * m, [T], F32R) for m in range(NM)]
        k_hi = [at("kslc_hi", 152, [T], F32R), at("kwin_hi", 110, [T], F32R)]
        k_lo = [at("kslc_lo", 156, [T], F32R), at("kwin_lo", 114, [T], F32R)]
        qk_dram = nc.dram_tensor("qk_scratch", (NM + 2, P, T), F32).ap()
        qk_out = sem("qk_out")
        sbuf = [at(f"sbuf{i}", o, [T]) for i, o in enumerate((176, 180, 64))]
        pT = [at(f"pT{i}", o, [TB, P]) for i, o in enumerate((184, 68))]
        oall = at("oall", 120, [TB, NM, NG, ND])
        sc = at("sc", 176, [NH, 64])
        pcT = at("pcT", 180, [NH // 2, P])
        cgt, ceq = at("cgt", 184, [NG, NSEL, NSEL]), at("ceq", 186, [NG, NSEL, NSEL])
        c8 = lambda o: scal(o, 8)
        cmx, csm = c8(0), c8(8)
        mark = scal(1096, 2)
        nmx, rsum, wrow = scal(1080, 4), scal(1084, 4), scal(1088, 4)
        NI = {}
        o = 0
        for n, k in (("causal", P), ("old", P), ("lower", NSEL * NSEL), ("cneg", TB * 64), ("cval", TB * 64),
                     ("bias", TB * NSEL)):
            NI[n] = (o, o + k)
            o += k
        ncst = lambda n: consts[:, NI[n][0]:NI[n][1]]

        (n_in, pos_tr, pos_ok, v_tr, v_tok, win_ok, kc_ok, kc_evac, vc_tr, vc_ok, wc_zero, mw_ok) = (
            sem(n) for n in ("n_in", "pos_tr", "pos_ok", "v_tr", "v_tok", "win_ok", "kc_ok", "kc_evac", "vc_tr",
                             "vc_ok", "wc_zero", "mw_ok"))
        wc_in = sem("wc_in")

        def load_wcmp(sp, name):
            src = A[name][0].rearrange("l d e -> d l e")
            for g in range(NG):
                r = slice(ND * g, ND * g + ND)
                sp.dma_start(wcmp[r, :, r], src).then_inc(wc_in, 16)

        def sp_nsa(sp):
            sp.dma_start(consts[:], A["c_nsa"]).then_inc(n_in, 16)
            for i, n in enumerate(("nsa_cmp_pk", "nsa_cmp_pv")):
                for g in range(NG):
                    sp.dma_start(pos_in[0:CL, i, ND * g:ND * g + ND], A[n][0]).then_inc(n_in, 16)
            sp.wait_ge(wc_zero, 1)
            load_wcmp(sp, "nsa_cmp_wk")
            load_pieces(sp, P_NSA + 2, P_NSA + 10)
            for k, (src, i) in enumerate([(kslc[:], 2), (kwin[:], 4)] + [(QT[:, m], 6 + m) for m in range(NM)]):
                p = P_NSA + i
                sp.wait_ge(tile_evac[p % 2], p // 2 + 1)
                sp.dma_start(qk_dram[NM + k if k < 2 else k - 2], src).then_inc(qk_out, 16)
            sp.wait_ge(kc_ok, 1)
            load_wcmp(sp, "nsa_cmp_wv")
            sp.wait_ge(qk_out, 16 * (NM + 2))

        def pool_nsa(pool):
            nc.gpsimd.memset(wcmp[:], 0.0).then_inc(wc_zero, 1)
            split_pieces(pool, P_NSA + 2, P_NSA + 10)
            for k in range(2):
                pool.wait_ge(tile_evac[(P_NSA + k) % 2], (P_NSA + k) // 2 + 1)
                pool.wait_ge(pos_ok, 2)
                if k == 1:
                    pool.wait_ge(kc_ok, 1)
                for half in range(2):
                    ins = nc.gpsimd.tensor_tensor(
                        window[:, 16 * half:16 * half + 16, 0:NCMP],
                        cmpT[k][:, 16 * half:16 * half + 16 * NCMP].rearrange("p (n s) -> p s n", s=CS),
                        posT[:, k, 16 * half:16 * half + 16].unsqueeze(2).to_broadcast([P, 16, NCMP]), ALU.add)
                ins.then_inc(win_ok, 1)

        def pe_nsa(pe):
            pe.wait_ge(n_in, 80)
            for i in range(2):
                nc.tensor.transpose(PS[:, 4, CL * i:CL * i + CL], pos_in[0:CL, i], ident[0:CL, 0:CL]).then_inc(pos_tr, 1)
            for p in range(P_NSA, P_NSA + 10):
                run_job(pe, p)
                if p - P_NSA in (4, 6):
                    i = (p - P_NSA - 4) // 2
                    q = P_NSA + 3 + 2 * i
                    pe.wait_ge(tile_evac[q % 2], q // 2 + 1)
                    if i:
                        pe.wait_ge(v_tok, 1)
                    for t in range(TB):
                        last = nc.tensor.transpose(PS[:, 6 + t // 4, (t % 4) * P:(t % 4 + 1) * P],
                                                   vT[i][:, t * P:(t + 1) * P], ident[:])
                    last.then_inc(v_tr, 1)
            for k in range(2):
                pe.wait_ge(win_ok, k + 1)
                pe.wait_ge(wc_in, 32 * (k + 1))
                for l in range(CL):
                    last = nc.tensor.matmul(PS[:, 4 + k, 0:NCMP], wcmp[:, l], window[:, l, 0:NCMP],
                                            start=(l == 0), stop=(l == CL - 1))
                last.then_inc(kc_ok, 1)
            pe.wait_ge(kc_evac, 2)
            pe.wait_ge(v_tok, 2)
            nc.tensor.transpose(PS[:, 6, 0:P], vcT[:].rearrange("p a n -> p (a n)"), ident[:]).then_inc(vc_tr, 1)

        def act_nsa(act):
            for k in range(10):
                p = P_NSA + k
                act.wait_ge(tile_done, p + 1)
                dst = (cmpT[0], cmpT[1], kslc, vT[0], kwin, vT[1])[k][:] if k < 6 else QT[:, k - 6]
                evac_done(nc.scalar.activation(dst, pair(p % 2), ACT.Copy, scale=1.0 if k < 6 else float(ND) ** -0.5), p)
            act.wait_ge(mw_ok, 3)
            act.wait_ge(kc_ok, 1)
            nc.scalar.activation(kcT[:, 0:NCMP], PS[:, 4, 0:NCMP], ACT.Copy).then_inc(kc_evac, 1)
            act.wait_ge(kc_ok, 2)
            nc.scalar.activation(vcT[:, :, 0:NCMP], PS[:, 5, 0:NCMP].unsqueeze(1).to_broadcast([P, 2, NCMP]),
                                 ACT.Copy).then_inc(kc_evac, 1)
            act.wait_ge(vc_tr, 1)
            nc.scalar.activation(vc[:], PS[:, 6, 0:P], ACT.Copy).then_inc(vc_ok, 1)

        def dve_nsa(dve):
            for i in range(2):
                dve.wait_ge(pos_tr, 2)
                nc.vector.tensor_copy(posT[:, i], PS[:, 4, CL * i:CL * i + CL]).then_inc(pos_ok, 1)
            for zero in (P4[:], kcT[:], vcT[:]):
                nc.vector.memset(zero, 0.0).then_inc(mw_ok, 1)
            for i, dst in enumerate((vslc, vwin)):
                dve.wait_ge(v_tr, i + 1)
                nc.vector.tensor_copy(dst[:].rearrange("p t n -> p (t n)"), pair(3)).then_inc(v_tok, 1)

        CP = Stages(sem, "cmp_pe", ["s", "t", "o"])
        CA = Stages(sem, "cmp_act", ["e", "pt"])
        CV = Stages(sem, "cmp_dve", ["sub", "pv", "oacc"])
        CG = Stages(sem, "mask", ["m", "mc"])
        UN = Stages(sem, "unit", ["scores", "masked", "max", "exp", "turned", "copied", "out", "recip", "weight", "sum"])
        NU = 2 * NM
        UALL = NG * TB * NU

        def unit(u):
            blk, r = divmod(u, NU)
            g, t = divmod(blk, TB)
            m, kind = divmod(r, 2)
            first = 0 if kind == 0 else max(0, t - WT + 1)
            n = t + 1 - first
            mask = maskg[:, blk % 2, 0:n * P] if kind == 0 else maskw[:, WT - n:WT].rearrange("p a b -> p (a b)")
            return t, g, m, kind, first, n, (vslc, vwin)[kind], mask

        def pe_cmp(pe, t):
            if t:
                CV.wait(pe, t - 1, "oacc")
            for g in range(NG):
                r = slice(ND * g, ND * g + ND)
                for m in range(NM):
                    last = nc.tensor.matmul(PS[:, 4 + g, 64 * m:64 * m + 64], QT[r, m, t * P:(t + 1) * P],
                                            kcT[r, :], start=True, stop=True)
            CP.done("s", last)
            for k in range(3):
                behind(pe, P_LATE + t, k, 0)
            CV.wait(pe, t, "pv")
            for k in range(NH // 2):
                last = nc.tensor.transpose(PS[:, 6, k * P:(k + 1) * P],
                                           sc[:, 2 * k:2 * k + 2].rearrange("p a n -> p (a n)"), ident[:])
            CP.done("t", last)
            for k in range(3, 6):
                behind(pe, P_LATE + t, k, 0)
            CA.wait(pe, t, "pt")
            for hh in range(NH):
                g, r = hh // NM, slice(64 * (hh % 2), 64 * (hh % 2) + 64)
                last = nc.tensor.matmul(PS[:, 4 + hh % 2, ND * (hh // 2):ND * (hh // 2) + ND], pcT[r, hh // 2],
                                        vc[r, ND * g:ND * g + ND], start=True, stop=True)
            CP.done("o", last)
            for k in range(6, KT):
                behind(pe, P_LATE + t, k, 0)

        def pe_nsa_cmp(pe):
            for t in range(TB):
                if t % 2 == 0:
                    pe_sb_values(pe, t // 2)
                pe_cmp(pe, t)

        def act_nsa_cmp(act):
            for t in range(TB):
                CV.wait(act, t, "sub")
                CA.done("e", nc.scalar.activation(sc[:], sc[:], ACT.Exp))
                CP.wait(act, t, "t")
                CA.done("pt", nc.scalar.activation(pcT[:].rearrange("p h n -> p (h n)"), PS[:, 6, :], ACT.Copy))
                p = P_LATE + t
                act.wait_ge(tile_done, p + 1)
                act.wait_ge(stored, 16 * (NSG + t))
                evac_done(nc.scalar.activation(late[:], pair(0), ACT.Copy), p)

        late = at("late", 188, [T])

        def sp_cmp(sp):
            sp_sb_values(sp, 0)
            sp_sb_values(sp, 1)
            store_staged(sp, NSG, NST, late, lambda j: sp_sb_values(sp, j // 2 + 1) if j in (2, 4) else None)

        def pool_cmp(pool):
            split_pieces(pool, P_LATE, P_LATE + TB)

        def dve_nsa_cmp(dve):
            for t in range(TB):
                if t % 2 == 0:
                    dve_sb_values(dve, t // 2)
                dve_cmp(dve, t)

        def pe_scores(pe, u):
            t, g, m, kind, first, n, vals, mask = unit(u)
            if u % (TB * NU) == 0:
                pe.wait_ge(lows, (NM + 2) * (g + 1))
            if u >= 1:
                UN.wait(pe, u - 1, "masked")
            for a in range(0, n * P, 512):
                w = min(512, n * P - a)
                for keys in (k_hi[kind], k_lo[kind]):
                    last = nc.tensor.matmul(pair(0)[:, a:a + w], q_hl[m][:, t * P:(t + 1) * P],
                                            keys[:, first * P + a:first * P + a + w], start=(keys is k_hi[kind]),
                                            stop=(keys is k_lo[kind]))
            UN.done("scores", last)

        def pe_turn(pe, u):
            UN.wait(pe, u, "exp")
            if u % 2 == 0 and 0 <= u // 2 - 3 < SU:
                SB.wait(pe, u // 2 - 3, "copied")
            elif u >= 1:
                UN.wait(pe, u - 1, "copied")
            for j in range(unit(u)[5]):
                last = nc.tensor.transpose(pair(2)[:, j * P:(j + 1) * P], sbuf[u % 3][:, j * P:(j + 1) * P], ident[:])
            UN.done("turned", last)

        def pe_out(pe, u):
            t, g, m, kind, first, n, vals, mask = unit(u)
            UN.wait(pe, u, "copied")
            if u >= 1:
                UN.wait(pe, u - 1, "sum")
            for j in range(n):
                last = nc.tensor.matmul(PS[:, 6, 0:ND], pT[u % 2][:, j], vals[:, first + j, ND * g:ND * g + ND],
                                        start=(j == 0), stop=(j == n - 1))
            UN.done("out", last)

        def pe_z(pe, s):
            m, a, t, n = sb_unit(s)
            b = (2 * m + a) % 2
            if s % TB == 0:
                pe.wait_ge(stick_ops, 4 * (2 * m + a + 1))
            if s >= 1:
                SB.wait(pe, s - 1, "copy")
            for c in range(0, n * P, 512):
                w = min(512, n * P - c)
                q = sq_hl[b][:, t * P:(t + 1) * P]
                nc.tensor.matmul(pair(1)[:, c:c + w], q, sk_hi[b][:, c:c + w], start=True, stop=False)
                nc.tensor.matmul(pair(1)[:, c:c + w], q, sk_lo[b][:, c:c + w], start=False, stop=(c + w < n * P))
            SB.done("z", nc.tensor.matmul(pair(1)[:, t * P:n * P], ident_r[:], sneg[:], start=False, stop=True))

        def pe_sb_turn(pe, s):
            SB.wait(pe, s, "weights")
            if 2 * s + 5 < UALL:
                UN.wait(pe, 2 * s + 5, "copied")
            else:
                UN.wait(pe, UALL - 1, "copied")
                SB.wait(pe, s - 1, "copied")
            for j in range(sb_unit(s)[3]):
                last = nc.tensor.transpose(pair(2)[:, j * P:(j + 1) * P], sbz[s % 4][:, j * P:(j + 1) * P], ident[:])
            SB.done("turned", last)

        def pe_sb_out(pe, s):
            m, a, t, n = sb_unit(s)
            SB.wait(pe, s, "copied")
            if s >= 1:
                SB.wait(pe, s - 1, "kept")
            for j in range(n):
                last = nc.tensor.matmul(PS[SD * a:SD * a + SD, 7, 0:P], sv_tok[:, m, j, SD * a:SD * a + SD],
                                        spT[s % 2][:, j], start=(j == 0), stop=(j == n - 1))
            SB.done("out", last)

        TURNS = 2 * (SU + 5)

        groups = lambda g: [(qk_dram[i], g) for i in range(NM + 2)]
        heads = lambda j: [(staged[S_SB + 3 * (j // 2) + i], j % 2) for i in range(2)]
        loads = groups(0)
        place_group, place_head = [0], []
        for j in range(2 * NM):
            if j == 5:
                place_group.append(len(loads))
                loads += groups(1)
            place_head.append(len(loads))
            loads += heads(j)
        twice_in = [sem("twice_in0"), sem("twice_in1")]
        twice_used = [sem("twice_used0"), sem("twice_used1")]
        highs, lows, stick_ops = sem("highs"), sem("lows"), sem("stick_ops")

        def sp_attn(sp):
            sp.dma_start(sneg_in[:], A["c_sb"]).then_inc(sb_in, 16)
            for i, (src, half) in enumerate(loads):
                if i >= 2:
                    sp.wait_ge(twice_used[i % 2], i // 2)
                for r in (slice(0, 64), slice(64, P)):
                    sp.dma_start(twice[i % 2][r], src[64 * half:64 * half + 64]).then_inc(twice_in[i % 2], 16)

        def wait_twice(eng, i):
            eng.wait_ge(twice_in[i % 2], 32 * (i // 2 + 1))
            return twice[i % 2]

        def act_group(act, g):
            if g:
                UN.wait(act, TB * NU - 1, "scores")
            for k in range(NM + 2):
                raw = wait_twice(act, place_group[g] + k)
                dst = q_hl[k] if k < NM else k_hi[k - NM]
                nc.scalar.activation(dst[:], raw[:], ACT.Copy).then_inc(highs, 1)

        def dve_group(dve, g):
            if g:
                UN.wait(dve, TB * NU - 1, "scores")
            for k in range(NM + 2):
                i = place_group[g] + k
                raw = wait_twice(dve, i)
                dve.wait_ge(highs, (NM + 2) * g + k + 1)
                if k < NM:
                    ins = nc.vector.tensor_tensor(q_hl[k][64:P], raw[64:P], q_hl[k][64:P].bitcast(F32), ALU.subtract)
                else:
                    ins = nc.vector.tensor_tensor(k_lo[k - NM][:], raw[:], k_hi[k - NM][:].bitcast(F32), ALU.subtract)
                ins.then_inc(twice_used[i % 2], 1)
                dve.wait_ge(twice_used[i % 2], i // 2 + 1)
                nc.vector.memset(mark[:, 0:1], 0.0).then_inc(lows, 1)

        def pool_head(pool, j, k):
            i, b = place_head[j] + k, j % 2
            if j >= 2:
                SB.wait(pool, TB * (j - 1) - 1, "z")
            raw = wait_twice(pool, i)
            high = (sq_hl, sk_hi)[k][b]
            nc.gpsimd.tensor_copy(high[:], raw[:]).then_inc(stick_ops, 1)
            pool.wait_ge(stick_ops, 4 * j + 2 * k + 1)
            r = slice(64, P) if k == 0 else slice(0, P)
            low = (sq_hl, sk_lo)[k][b]
            nc.gpsimd.tensor_tensor(low[r], raw[r], high[r].bitcast(F32), ALU.subtract).then_inc(stick_ops, 1)
            pool.wait_ge(stick_ops, 4 * j + 2 * k + 2)
            nc.gpsimd.memset(mark[:, 1:2], 0.0).then_inc(twice_used[i % 2], 1)

        def during(u, count):
            return 0 <= u < count

        def pe_attn(pe):
            pe.wait_ge(mask_r, 2)
            for h in range(TURNS):
                s, odd = divmod(h, 2)
                if during(h - 2, UALL):
                    pe_turn(pe, h - 2)
                if during(h, UALL):
                    pe_scores(pe, h)
                if not odd and during(s, SU):
                    pe_z(pe, s)
                if odd and during(s - 3, SU):
                    pe_sb_turn(pe, s - 3)
                if during(h - 3, UALL):
                    pe_out(pe, h - 3)
                if odd and during(s - 4, SU):
                    pe_sb_out(pe, s - 4)

        def act_attn(act):
            nc.scalar.preload_act_table_set("natural_log_exp_and_others")
            for h in range(TURNS):
                s, odd = divmod(h, 2)
                if h in (0, TB * NU):
                    act_group(act, h // (TB * NU))
                if during(h - 1, UALL):
                    u = h - 1
                    x = sbuf[u % 3][:, 0:unit(u)[5] * P]
                    c = u % 4
                    UN.wait(act, u, "max")
                    if u >= 4:
                        UN.wait(act, u - 4, "recip")
                    UN.done("exp", nc.scalar.activation(x, x, ACT.Exp, bias=nmx[:, c:c + 1], accum_out=rsum[:, c:c + 1]))
                if during(s, SU):
                    w = sb_unit(s)[3] * P
                    z, l = sbz[s % 4][:, 0:w], sbl[s % 2][:, 0:w]
                if not odd and during(s, SU):
                    SB.wait(act, s, "z")
                    if s >= 4:
                        SB.wait(act, s - 4, "turned")
                    SB.done("copy", nc.scalar.activation(z, pair(1)[:, 0:w], ACT.Copy))
                if during(h - 2, UALL):
                    u = h - 2
                    n = unit(u)[5]
                    UN.wait(act, u, "turned")
                    if u >= 2:
                        UN.wait(act, u - 2, "out")
                    UN.done("copied", nc.scalar.activation(pT[u % 2][:, 0:n].rearrange("p k n -> p (k n)"),
                                                           pair(2)[:, 0:n * P], ACT.Copy))
                if not odd and during(s, SU):
                    SB.wait(act, s, "copy")
                    if s >= 2:
                        SB.wait(act, s - 2, "prefix")
                    SB.done("abs", nc.scalar.activation(l, z, ACT.Abs))
                    SB.wait(act, s, "abs")
                    SB.done("exp", nc.scalar.activation(l, l, ACT.Exp, scale=-1.0))
                if odd and during(s, SU):
                    SB.wait(act, s, "exp")
                    SB.done("log", nc.scalar.activation(l, l, ACT.Ln, bias=1.0))
                if odd and during(s - 2, SU):
                    v = s - 2
                    x = sbz[v % 4][:, 0:sb_unit(v)[3] * P]
                    SB.wait(act, v, "added")
                    SB.wait(act, v, "total")
                    SB.done("weights", nc.scalar.activation(x, x, ACT.Exp, bias=ntot[:, v % 4:v % 4 + 1]))

        def pool_mask(pool, blk):
            g, t = divmod(blk, TB)
            if blk >= 2:
                UN.wait(pool, (blk - 1) * NU - 1, "masked")
            w = (t + 1) * P
            CG.done("m", nc.gpsimd.tensor_copy(maskg[:, blk % 2, 0:w].rearrange("p (j l) -> p j l", l=SL),
                                               msel_all[:, t, g, 0:2 * (t + 1)].unsqueeze(2)
                                               .to_broadcast([P, 2 * (t + 1), SL])))
            CG.wait(pool, blk, "m")
            last = maskg[:, blk % 2, t * P:w]
            CG.done("mc", nc.gpsimd.tensor_tensor(last, last, ncst("causal"), ALU.add))

        def dve_cmp(dve, t):
            tt, red = nc.vector.tensor_tensor, nc.vector.tensor_reduce
            scn = sc[:]
            sc4 = sc[:].rearrange("p (g m) n -> p g m n", g=NG)
            over8 = lambda n: ncst(n)[:, 64 * t:64 * t + 64].unsqueeze(1).unsqueeze(1).to_broadcast([P, NG, NM, 64])
            along = lambda ap: ap.unsqueeze(2).to_broadcast([P, NH, 64])

            def step(name, ins):
                CV.done(name, ins)
                CV.wait(dve, t, name)
            CP.wait(dve, t, "s")
            dstep(tt(sc4, PS[:, 4:6, 0:256].rearrange("p g (m n) -> p g m n", m=NM), over8("cneg"), ALU.add))
            dstep(red(cmx, scn, AX_X, ALU.max))
            step("sub", tt(scn, scn, along(cmx), ALU.subtract))
            CA.wait(dve, t, "e")
            dstep(red(csm, scn, AX_X, ALU.add))
            dstep(nc.vector.reciprocal(csm, csm))
            dstep(tt(scn, scn, along(csm), ALU.mult))
            step("pv", tt(sc4, sc4, over8("cval"), ALU.mult))
            CP.wait(dve, t, "o")
            gates = nsa_gate[:, t].rearrange("p (g k a c) -> p a g k c", g=NG, a=2, c=3)[:, :, :, :, 0]
            for par in range(2):
                ins = tt(oall[:, t].rearrange("p (k a) g d -> p a g k d", a=2)[:, par],
                         PS[:, 4 + par, 0:256].rearrange("p (g k d) -> p g k d", g=NG, k=2),
                         gates[:, par].unsqueeze(3).to_broadcast([P, NG, 2, ND]), ALU.mult)
            step("oacc", ins)
            msel = msel_all[:, t]
            if 2 * (t + 1) <= TOPK:
                dstep(nc.vector.memset(msel, 0.0))
                return
            imp = score[:]
            dstep(red(P4[:, :, 1:1 + NCMP], sc[:].rearrange("p (g m) n -> p g n m", g=NG)[:, :, 0:NCMP, :], AX_X,
                           ALU.add))
            dstep(red(imp, P4[:, :, 0:64].rearrange("p g (j f) -> p g j f", f=4), AX_X, ALU.add))
            dstep(tt(imp, imp, P4[:, :, 4:68].rearrange("p g (j f) -> p g j f", f=4)[:, :, :, 0], ALU.add))
            dstep(tt(imp, imp, ncst("bias")[:, NSEL * t:NSEL * (t + 1)].unsqueeze(1).to_broadcast([P, NG, NSEL]),
                          ALU.add))
            full = [P, NG, NSEL, NSEL]
            si, sj = imp.unsqueeze(2).to_broadcast(full), imp.unsqueeze(3).to_broadcast(full)
            dstep(tt(cgt[:], si, sj, ALU.is_gt))
            dstep(tt(ceq[:], si, sj, ALU.is_equal))
            dstep(tt(ceq[:], ceq[:], ncst("lower").rearrange("p (j i) -> p j i", i=NSEL).unsqueeze(1)
                           .to_broadcast(full), ALU.mult))
            dstep(tt(cgt[:], cgt[:], ceq[:], ALU.add))
            dstep(red(msel, cgt[:], AX_X, ALU.add))
            dstep(nc.vector.tensor_scalar(msel, msel, float(TOPK), NEG, ALU.is_ge, ALU.mult))

        def pool_attn(pool):
            pool_mask(pool, 0)
            pool_head(pool, 0, 0)
            pool_head(pool, 0, 1)
            pool_mask(pool, 1)
            for s in range(SU):
                n = sb_unit(s)[3]
                z = sbz[s % 4][:, 0:n * P]
                SB.wait(pool, s, "prefix")
                SB.done("added", nc.gpsimd.tensor_tensor(z, z, cum[s % 2][:, 0:n * P], ALU.add))
                if (s + 1) % (NU // 2) == 0 and 2 <= (s + 1) // (NU // 2) + 1 < NG * TB:
                    pool_mask(pool, (s + 1) // (NU // 2) + 1)
                for k, ahead in ((0, TB + 1), (1, TB - 1)):
                    j, r = divmod(s + ahead, TB)
                    if r == 0 and 2 <= j < 2 * NM:
                        pool_head(pool, j, k)
                    if j == 1 and s == 2 * k:
                        pool_head(pool, 1, k)

        def dve_sum(dve, u):
            t, g, m, kind, first, n, vals, mask = unit(u)
            c = u % 4
            UN.wait(dve, u, "exp")
            UN.done("recip", nc.vector.reciprocal(wrow[:, c:c + 1], rsum[:, c:c + 1]))
            UN.wait(dve, u, "recip")
            gate = nsa_gate[:, t, 3 * (g * NM + m) + 1 + kind:3 * (g * NM + m) + 2 + kind]
            UN.done("weight", nc.vector.tensor_tensor(wrow[:, c:c + 1], wrow[:, c:c + 1], gate, ALU.mult))
            UN.wait(dve, u, "out")
            UN.wait(dve, u, "weight")
            if u:
                UN.wait(dve, u - 1, "sum")
            o = oall[:, t, m, g]
            UN.done("sum", nc.vector.scalar_tensor_tensor(out=o, in0=PS[:, 6, 0:ND], scalar=wrow[:, c:c + 1], in1=o,
                                                          op0=ALU.mult, op1=ALU.add))

        def dve_attn(dve):
            dstep(nc.vector.memset(maskw[:], 0.0))
            dstep(nc.vector.tensor_copy(maskw[:, 0], ncst("old")))
            dstep(nc.vector.tensor_copy(maskw[:, WT - 1], ncst("causal")))
            dve.wait_ge(sb_in, 16)
            nc.vector.tensor_copy(ident_r[:], ident[:]).then_inc(mask_r, 1)
            nc.vector.tensor_copy(sneg[:], sneg_in[:]).then_inc(mask_r, 1)
            dstep(nc.vector.memset(cum[0][:, 0:1], 0.0))
            dstep(nc.vector.memset(cum[1][:, 0:1], 0.0))
            for h in range(TURNS + 1):
                s, odd = divmod(h, 2)
                if h in (0, TB * NU):
                    dve_group(dve, h // (TB * NU))
                if during(h - 4, UALL):
                    dve_sum(dve, h - 4)
                if not odd and during(s - 5, SU):
                    v = s - 5
                    m, a, t, n = sb_unit(v)
                    SB.wait(dve, v, "out")
                    r = slice(SD * a, SD * a + SD)
                    SB.done("kept", nc.vector.tensor_copy(osT[r, m, t * P:(t + 1) * P], PS[r, 7, 0:P]))
                if during(h, UALL):
                    u = h
                    t, g, m, kind, first, n, vals, mask = unit(u)
                    c, x = u % 4, sbuf[u % 3][:, 0:n * P]
                    UN.wait(dve, u, "scores")
                    if u % NU == 0:
                        CG.wait(dve, u // NU, "mc")
                    if u >= 3:
                        UN.wait(dve, u - 3, "turned")
                    UN.done("masked", nc.vector.tensor_tensor(x, pair(0)[:, 0:n * P], mask, ALU.add))
                    UN.wait(dve, u, "masked")
                    UN.done("max", nc.vector.tensor_reduce(nmx[:, c:c + 1], x, AX_X, ALU.max, negate=True))
                if not odd and during(s - 1, SU):
                    v = s - 1
                    w = sb_unit(v)[3] * P
                    l, z, cs = sbl[v % 2][:, 0:w], sbz[v % 4][:, 0:w], cum[v % 2]
                    SB.wait(dve, v, "log")
                    SB.done("softplus", nc.vector.scalar_tensor_tensor(out=l, in0=z, scalar=0.0, in1=l, op0=ALU.max,
                                                                       op1=ALU.add))
                    SB.wait(dve, v, "softplus")
                    if v >= 2:
                        SB.wait(dve, v - 2, "added")
                        SB.wait(dve, v - 2, "total")
                    SB.done("prefix", nc.vector.tensor_tensor_scan(cs[:, 1:w + 1], l, l, 0.0, ALU.add, ALU.max))
                    SB.wait(dve, v, "prefix")
                    if v >= 4:
                        SB.wait(dve, v - 4, "weights")
                    SB.done("total", nc.vector.tensor_scalar(ntot[:, v % 4:v % 4 + 1], cs[:, w:w + 1], -1.0, None,
                                                             ALU.mult))
                if odd and during(s - 3, SU):
                    v = s - 3
                    n = sb_unit(v)[3]
                    SB.wait(dve, v, "turned")
                    if v >= 2:
                        SB.wait(dve, v - 2, "out")
                    SB.done("copied", nc.vector.tensor_copy(spT[v % 2][:, 0:n].rearrange("p k n -> p (k n)"),
                                                            pair(2)[:, 0:n * P]))

        ny_tr = sem("ny_tr")

        def pe_turn_y(pe, m):
            if m >= 2:
                pe.wait_ge(y_lo_ok, 4 + m - 1)
            for t in range(TB):
                last = nc.tensor.transpose(pair(2 + m % 2)[:, t * P:(t + 1) * P],
                                           oall[:, t, m].rearrange("p g d -> p (g d)"), ident[:])
            last.then_inc(ny_tr, 1)
        YT = at("YT", 120, [KT, T])
        xb = [at(f"xb{i}", 152 + 4 * i, [D]) for i in range(2)]
        nrm = [at(f"nrm{i}", 160 + 4 * i, [D]) for i in range(2)]
        x1 = [at(f"x1_{i}", 168 + 4 * i, [D]) for i in range(2)]
        g_post, g_ff = at("g_post", 176, [D]), at("g_ff", 180, [D])
        junk = [at(f"junk{i}", 184 + 4 * i, [D]) for i in range(2)]
        x1_dram = nc.dram_tensor("x1_scratch", (T, D), F32).ap().rearrange("(t p) d -> t p d", p=P)
        mt_hi, mt_lo, gains_in = sem("mt_hi"), sem("mt_lo"), sem("gains_in")
        xb_in = [sem("xb_in0"), sem("xb_in1")]
        x1_out = [sem("x1_out0"), sem("x1_out1")]

        def act_split_m(act, k):
            act.wait_ge(merged, 2 * KT + k + 1)
            nc.scalar.activation(hT_hi[:, k], mT[:, k], ACT.Copy).then_inc(mt_hi, 1)

        def dve_split_m(dve, k):
            dve.wait_ge(mt_hi, k + 1)
            nc.vector.tensor_tensor(hT_lo[:, k], mT[:, k], hT_hi[:, k].bitcast(F32), ALU.subtract).then_inc(mt_lo, 1)

        def sp_wout(sp):
            load_pieces(sp, P_OUT, P_OUT + KT)

        def pool_wout(pool):
            split_pieces(pool, P_OUT, P_OUT + KT)

        def pe_wout(pe):
            for c in range(KT):
                run_job(pe, P_OUT + c)

        def act_wout(act):
            for c in range(KT):
                p = P_OUT + c
                act.wait_ge(tile_done, p + 1)
                evac_done(nc.scalar.activation(YT[:, c], pair(p % 2), ACT.Copy), p)

        NP = Stages(sem, "res_pe", ["y", "h"])
        NA = Stages(sem, "res_act", ["ss", "rt", "ss1", "rt1", "hi"])
        NV = Stages(sem, "res_dve", ["r", "n", "x1", "r1", "h", "lo"])
        sq1 = scal(0, 8)

        def sp_res(sp):
            sp.dma_start(g_post[:], bc(A["g_mix_post"][0], D)).then_inc(gains_in, 16)
            sp.dma_start(g_ff[:], bc(A["g_ff_pre"][0], D)).then_inc(gains_in, 16)
            for t in range(TB + 1):
                if t < TB:
                    if t >= 2:
                        NV.wait(sp, t - 2, "x1")
                    sp.dma_start(xb[t % 2][:], x_v[t]).then_inc(xb_in[t % 2], 16)
                if t >= 1:
                    NV.wait(sp, t - 1, "x1")
                    sp.dma_start(x1_dram[t - 1], x1[(t - 1) % 2][:]).then_inc(x1_out[(t - 1) % 2], 16)
            for i in range(2):
                sp.wait_ge(x1_out[i], 16 * TB // 2)

        def pe_res(pe):
            for k in range(TB + 2):
                if k < TB:
                    if k >= 2:
                        NV.wait(pe, k - 2, "n")
                    for c in range(KT):
                        last = nc.tensor.transpose(pair(k % 2)[:, c * P:(c + 1) * P], YT[:, c, k * P:(k + 1) * P],
                                                   ident[:])
                    NP.done("y", last)
                if k >= 2:
                    t = k - 2
                    NV.wait(pe, t, "h")
                    if t >= 2:
                        NV.wait(pe, t - 2, "lo")
                    for c in range(KT):
                        last = nc.tensor.transpose(pair(2 + t % 2)[:, c * P:(c + 1) * P],
                                                   nrm[t % 2][:, c * P:(c + 1) * P], ident[:])
                    NP.done("h", last)

        def act_res(act):
            sums = lambda t, i: sq1[:, 4 * (t % 2) + i:4 * (t % 2) + i + 1]
            for k in range(TB + 2):
                if k < TB:
                    NP.wait(act, k, "y")
                    if k >= 2:
                        NV.wait(act, k - 2, "h")
                    if k:
                        NA.wait(act, k - 1, "ss")
                    NA.done("ss", nc.scalar.activation(junk[0][:], pair(k % 2), ACT.Square, accum_out=sums(k, 0)))
                    NA.wait(act, k, "ss")
                    NA.done("rt", nc.scalar.activation(sums(k, 1), sums(k, 0), ACT.Sqrt, scale=1.0 / D, bias=eps_t))
                if k >= 2:
                    t = k - 2
                    NP.wait(act, t, "h")
                    NA.done("hi", nc.scalar.activation(hT_hi[:, :, t * P:(t + 1) * P],
                                                       pair(2 + t % 2).rearrange("p (k n) -> p k n", n=P), ACT.Copy))
                if 1 <= k <= TB:
                    t = k - 1
                    NV.wait(act, t, "x1")
                    if t:
                        NA.wait(act, t - 1, "ss1")
                    NA.done("ss1", nc.scalar.activation(junk[1][:], x1[t % 2][:], ACT.Square, accum_out=sums(t, 2)))
                    NA.wait(act, t, "ss1")
                    NA.done("rt1", nc.scalar.activation(sums(t, 3), sums(t, 2), ACT.Sqrt, scale=1.0 / D, bias=eps_t))

        def dve_res(dve):
            sums = lambda t, i: sq1[:, 4 * (t % 2) + i:4 * (t % 2) + i + 1]
            dve.wait_ge(gains_in, 32)
            for k in range(TB + 3):
                if k < TB:
                    b = k % 2
                    NA.wait(dve, k, "rt")
                    NV.done("r", nc.vector.reciprocal(sums(k, 1), sums(k, 1)))
                    NV.wait(dve, k, "r")
                    if k >= 2:
                        NP.wait(dve, k - 2, "h")
                    NV.done("n", nc.vector.scalar_tensor_tensor(out=nrm[b][:], in0=pair(b), scalar=sums(k, 1),
                                                                in1=g_post[:], op0=ALU.mult, op1=ALU.mult))
                    NV.wait(dve, k, "n")
                    dve.wait_ge(xb_in[b], 16 * (k // 2 + 1))
                    if k >= 2:
                        dve.wait_ge(x1_out[b], 16 * (k // 2))
                    NV.done("x1", nc.vector.tensor_tensor(x1[b][:], xb[b][:], nrm[b][:], ALU.add))
                if k >= 3:
                    t = k - 3
                    NA.wait(dve, t, "hi")
                    s = slice(t * P, (t + 1) * P)
                    NV.done("lo", nc.vector.tensor_tensor(hT_lo[:, :, s], pair(2 + t % 2).rearrange("p (k n) -> p k n", n=P),
                                                          hT_hi[:, :, s].bitcast(F32), ALU.subtract))
                if 1 <= k <= TB:
                    t = k - 1
                    NA.wait(dve, t, "rt1")
                    NV.done("r1", nc.vector.reciprocal(sums(t, 3), sums(t, 3)))
                    NV.wait(dve, t, "r1")
                    NV.wait(dve, t, "x1")
                    NV.done("h", nc.vector.scalar_tensor_tensor(out=nrm[t % 2][:], in0=x1[t % 2][:], scalar=sums(t, 3),
                                                                in1=g_ff[:], op0=ALU.mult, op1=ALU.mult))

        aT_hi, aT_lo = at("aT_hi", 88, [KT, T], F32R), at("aT_lo", 120, [KT, T], F32R)
        FT = at("FT", 152, [KT, T])
        relu = [at(f"relu{i}", 184 + 4 * i, [T]) for i in range(2)]
        r_ok, s_ok, a_hi_ok, a_lo_ok, ft_zero = (sem(n) for n in ("relu_ok", "square_ok", "a_hi_ok", "a_lo_ok", "ft_zero"))
        JOBS = 2 * KT
        PM = P_MLP
        L0 = [loaded[0], loaded[1]]

        def pc(i, j):
            return i * JOBS + (PM + j)

        zero1 = small[:, 1150:1151]

        def sp_mlp(sp):
            with sp.Fori(0, CH) as i:
                for j in range(JOBS):
                    b = (PM + j) % 2
                    sp.wait_ge(w_split, pc(i, j) - 1)
                    src = w1_v[i * KT + j] if j < KT else w2_v[i, j - KT]
                    sp.dma_start(w_raw[b][:], src).then_inc(w_loaded[b], 16)

        def pool_mlp(pool):
            with pool.Fori(0, CH) as i:
                for j in range(JOBS):
                    b = (PM + j) % 2
                    pool.wait_ge(w_loaded[b], i * (8 * JOBS) + (L0[b] + 16 * (j // 2 + 1)))
                    pool.wait_ge(tile_done, pc(i, j) - 1)
                    nc.gpsimd.tensor_tensor(w_hi[b][:], w_raw[b][:], zero1.unsqueeze(2).to_broadcast([P, KT, P]),
                                            ALU.add).then_inc(w_high, 1)
                    pool.wait_ge(w_high, pc(i, j) + 1)
                    nc.gpsimd.tensor_tensor(w_lo[b][:], w_raw[b][:], w_hi[b][:].bitcast(F32),
                                            ALU.subtract).then_inc(w_split, 1)

        def evacs(i, j):
            return i * (JOBS // 2) + (PM + j) // 2

        def pe_mlp(pe):
            with pe.Fori(0, CH) as i:
                for j in range(JOBS):
                    b = (PM + j) % 2
                    pe.wait_ge(w_split, pc(i, j) + 1)
                    pe.wait_ge(tile_evac[b], evacs(i, j))
                    taken = (lambda k: pe.wait_ge(a_lo_ok, i * KT + (k + 3))) if j == KT else None
                    job(pe, None, *((hT_hi, hT_lo) if j < KT else (aT_hi, aT_lo)), par=b, waits=taken)

        def act_mlp(act):
            with act.Fori(0, CH) as i:
                for j in range(KT):
                    b = (PM + j) % 2
                    act.wait_ge(tile_done, pc(i, j) + 1)
                    act.wait_ge(a_lo_ok, i * KT + j + 1)
                    nc.scalar.activation(relu[j % 2][:], pair(b), ACT.Relu).then_inc(tile_evac[b], 1)
                    act.wait_ge(s_ok, i * KT + j + 1)
                    nc.scalar.activation(aT_hi[:, j], relu[j % 2][:], ACT.Copy).then_inc(a_hi_ok, 1)

        def dve_mlp(dve):
            nc.vector.memset(FT[:], 0.0).then_inc(ft_zero, 1)
            for b in range(2):
                nc.vector.memset(relu[b][:, 0:1], 0.0).then_inc(a_lo_ok, 1)
            dve.wait_ge(ft_zero, 1)
            with dve.Fori(0, CH) as i:
                for j in range(KT):
                    b = (PM + j) % 2
                    r = relu[j % 2]
                    dve.wait_ge(tile_evac[b], evacs(i, j) + 1)
                    nc.vector.tensor_tensor(r[:], r[:], r[:], ALU.mult).then_inc(s_ok, 1)
                    dve.wait_ge(s_ok, i * KT + j + 1)
                    dve.wait_ge(a_hi_ok, i * KT + j + 1)
                    nc.vector.tensor_tensor(aT_lo[:, j], r[:], aT_hi[:, j].bitcast(F32), ALU.subtract).then_inc(a_lo_ok, 1)
                for j in range(KT, JOBS):
                    b = (PM + j) % 2
                    dve.wait_ge(tile_done, pc(i, j) + 1)
                    nc.vector.tensor_tensor(FT[:, j - KT], FT[:, j - KT], pair(b), ALU.add).then_inc(tile_evac[b], 1)
                dve.wait_ge(tile_evac[(PM + JOBS - 1) % 2], evacs(i, JOBS - 1) + 1)

        xf = [at(f"xf{i}", 88 + 4 * i, [D]) for i in range(2)]
        fn = [at(f"fn{i}", 96 + 4 * i, [D]) for i in range(2)]
        of = [at(f"of{i}", 104 + 4 * i, [D]) for i in range(2)]
        g_last, junkf = at("g_last", 112, [D]), at("junkf", 116, [D])
        out_v = out[0].rearrange("(t p) d -> t p d", p=P)
        gl_in = sem("gl_in")
        xf_in = [sem("xf_in0"), sem("xf_in1")]
        of_out = [sem("of_out0"), sem("of_out1")]
        FP = Steps(sem("fin_pe"), ["y"])
        FA = Steps(sem("fin_act"), ["ss", "rt"])
        FV = Steps(sem("fin_dve"), ["r", "n", "o"])

        def sp_fin(sp):
            sp.dma_start(g_last[:], bc(A["g_ff_post"][0], D)).then_inc(gl_in, 16)
            for t in range(TB + 1):
                if t < TB:
                    if t >= 2:
                        FV.wait(sp, t - 2, "o")
                    sp.dma_start(xf[t % 2][:], x1_dram[t]).then_inc(xf_in[t % 2], 16)
                if t >= 1:
                    FV.wait(sp, t - 1, "o")
                    sp.dma_start(out_v[t - 1], of[(t - 1) % 2][:]).then_inc(of_out[(t - 1) % 2], 16)
            for i in range(2):
                sp.wait_ge(of_out[i], 16 * TB // 2)

        def pe_fin(pe):
            for t in range(TB):
                if t >= 2:
                    FV.wait(pe, t - 2, "n")
                for k in range(KT):
                    last = nc.tensor.transpose(pair(t % 2)[:, k * P:(k + 1) * P], FT[:, k, t * P:(t + 1) * P], ident[:])
                gstep(FP, last)

        def act_fin(act):
            for t in range(TB):
                b = t % 2
                FP.wait(act, t, "y")
                if t >= 2:
                    FV.wait(act, t - 2, "n")
                if t:
                    FA.wait(act, t - 1, "rt")
                gstep(FA, nc.scalar.activation(junkf[:], pair(b), ACT.Square, accum_out=sq1[:, b:b + 1]))
                FA.wait(act, t, "ss")
                gstep(FA, nc.scalar.activation(sq1[:, 2 + b:3 + b], sq1[:, b:b + 1], ACT.Sqrt, scale=1.0 / D, bias=eps_t))

        def dve_fin(dve):
            dve.wait_ge(gl_in, 16)
            for t in range(TB):
                b = t % 2
                FA.wait(dve, t, "rt")
                gstep(FV, nc.vector.reciprocal(sq1[:, 2 + b:3 + b], sq1[:, 2 + b:3 + b]))
                FV.wait(dve, t, "r")
                gstep(FV, nc.vector.scalar_tensor_tensor(out=fn[b][:], in0=pair(b), scalar=sq1[:, 2 + b:3 + b], in1=g_last[:],
                                                         op0=ALU.mult, op1=ALU.mult))
                FV.wait(dve, t, "n")
                dve.wait_ge(xf_in[b], 16 * (t // 2 + 1))
                if t >= 2:
                    dve.wait_ge(of_out[b], 16 * (t // 2))
                gstep(FV, nc.vector.tensor_tensor(of[b][:], xf[b][:], fn[b][:], ALU.add))

        block = ctx.enter_context(nc.Block())
        def merge_of(b):
            return tuple((lambda f: lambda e: f(e, b))(f) for f in (sp_merge, pool_merge, act_merge, dve_merge, pe_merge))

        merges = [merge_of(b) for b in range(3)]

        phases = [
            (sp_phase0, None, act_phase0, dve_phase0, pe_phase0),
            (sp_gdn, pool_gdn, act_gdn, dve_gdn, pe_gdn),
            (sp_gdn_blocks, pool_gdn_blocks, act_gdn_blocks, dve_gdn_blocks, pe_gdn_blocks),
            (sp_gdn_out, pool_gdn_out, act_gdn_out, dve_gdn_out, pe_gdn_out),
            (sp_nsa, pool_nsa, act_nsa, dve_nsa, pe_nsa),
            (sp_cmp, pool_cmp, act_nsa_cmp, dve_nsa_cmp, pe_nsa_cmp),
            (sp_attn, pool_attn, act_attn, dve_attn, pe_attn),
            (sp_y0, None, act_y0, dve_y0, None),
            merges[0],
            merges[1],
            merges[2],
            (sp_wout, pool_wout, act_wout, None, pe_wout),
            (sp_res, None, act_res, dve_res, pe_res),
            (sp_mlp, pool_mlp, act_mlp, dve_mlp, pe_mlp),
            (sp_fin, None, act_fin, dve_fin, pe_fin),
        ]
        AHEAD = [i for i, row in enumerate(phases) if row[4] in (pe_gdn, pe_wout, pe_mlp) or row in merges]
        column = ("sync", "gpsimd", "scalar", "vector", "tensor")

        def run(eng, name):
            for i, row in enumerate(phases):
                f = row[column.index(name)]
                if f:
                    f(eng)
                end_phase(eng, name, wait=not (name in ("sync", "gpsimd") and i + 1 in AHEAD))

        @block.sync
        def _(sp):
            run(sp, "sync")

        @block.gpsimd
        def _(pool):
            run(pool, "gpsimd")

        @block.scalar
        def _(act):
            run(act, "scalar")

        @block.vector
        def _(dve):
            run(dve, "vector")

        @block.tensor
        def _(pe):
            run(pe, "tensor")


_INS = ["x", "g_mix_pre", "g_mix_post", "g_ff_pre", "g_ff_post", "w_in", "gdn_conv_w", "gdn_a_log", "gdn_dt_bias",
        "gdn_norm_g", "nsa_cmp_wk", "nsa_cmp_pk", "nsa_cmp_wv", "nsa_cmp_pv", "w_br_gdn", "w_br_nsa", "w_br_sb",
        "w_out", "w_ff1", "w_ff2"]
_CONSTS = ["c_ident", "c_gdn", "c_nsa", "c_sb"]


def kernel(**inputs):
    import numpy as _np
    import concourse.bacc as _bacc
    from concourse import mybir as _mybir
    from concourse.bass_utils import run_bass_kernel_spmd as _run

    nc = _bacc.Bacc("TRN2", target_bir_lowering=False, num_devices=1)
    arrays, A = {}, {}
    for name in _INS:
        arrays[f"in_{name}"] = _np.ascontiguousarray(inputs[name])
    for name, table in zip(_CONSTS, shape_constants()):
        arrays[f"in_{name}"] = table
    for name in _INS + _CONSTS:
        a = arrays[f"in_{name}"]
        A[name] = nc.dram_tensor(f"in_{name}", a.shape, _mybir.dt.from_np(a.dtype), kind="ExternalInput").ap()
    out = nc.dram_tensor("out_0_dram", (1, T, D), _mybir.dt.float32, kind="ExternalOutput").ap()
    build(nc, A, out)
    r = _run(nc, [arrays], core_ids=[0])
    return r.results[0]["out_0_dram"]
```
